# Optimizing a Trainium2 kernel written in Bass

```python
import jax, jax.numpy as jnp
from jax import lax
import numpy as np

D_MODEL = 1024
BATCH = 1
SEQ = 256
DEPTH = 2
DEC_BATCH = 8
DEC_SEQ = 4
PAST_LEN = 1024
PAGE_SIZE = 128

N_HEADS_A = 8
HEAD_DIM_A = 64
MOBA_BLOCK = 256
MOBA_TOPK = 3
Q_CHUNK = 16
N_HEADS_R = 4
KEY_DIM_R = 128
VAL_DIM_R = 128
RET_CHUNK = 128
D_FF = 2816
EPS = 1e-6
NEG_INF = -1e30

W_A = N_HEADS_A * HEAD_DIM_A
W_RK = N_HEADS_R * KEY_DIM_R
W_RV = N_HEADS_R * VAL_DIM_R
SPLITS = (W_A, W_A, W_A, W_RK, W_RK, W_RV, W_RV, D_MODEL, D_MODEL)
D_IN = W_A * 3 + W_RK * 2 + W_RV * 2 + D_MODEL * 2

kernel_name = 'moba_retention_macaron_decode_step'

def rmsnorm(x, g):
    xf = x.astype(jnp.float32)
    y = xf * lax.rsqrt(jnp.mean(xf * xf, axis=-1, keepdims=True) + EPS)
    return (y * g.astype(jnp.float32)).astype(x.dtype)

def swiglu(x, w1, w3, w2):
    return (jax.nn.silu(x @ w1) * (x @ w3)) @ w2

def alibi_slopes():
    return 2.0 ** (-8.0 * (jnp.arange(N_HEADS_A, dtype=jnp.float32) + 1.0) / N_HEADS_A)

def retention_log_decay():
    return jnp.log(1.0 - 2.0 ** (-5.0 - jnp.arange(N_HEADS_R, dtype=jnp.float32)))

def to_blocks(k, v):
    B, L, H, Dh = k.shape
    pad = (-L) % MOBA_BLOCK
    k = jnp.pad(k, ((0, 0), (0, pad), (0, 0), (0, 0)))
    v = jnp.pad(v, ((0, 0), (0, pad), (0, 0), (0, 0)))
    nb = (L + pad) // MOBA_BLOCK
    kb = k.reshape(B, nb, MOBA_BLOCK, H, Dh).transpose(0, 3, 1, 2, 4)
    vb = v.reshape(B, nb, MOBA_BLOCK, H, Dh).transpose(0, 3, 1, 2, 4)
    kmean = jnp.mean(kb.astype(jnp.float32), axis=3)
    return kb, vb, kmean

def moba_core(q, q_pos, kb, vb, kmean):
    B, Sq, H, Dh = q.shape
    nb = kb.shape[2]
    n_top = min(MOBA_TOPK, nb)
    qf = q.astype(jnp.float32)
    own = q_pos // MOBA_BLOCK
    gate = jnp.einsum('bqhd,bhnd->bhqn', qf, kmean)
    fully_past = jnp.arange(nb)[None, :] < own[:, None]
    gate = jnp.where(fully_past[None, None], gate, NEG_INF)
    _, top_idx = lax.top_k(gate, n_top)
    top_ok = jnp.arange(n_top)[None, :] < own[:, None]
    own_idx = jnp.broadcast_to(own[None, None, :, None], (B, H, Sq, 1)).astype(top_idx.dtype)
    idx = jnp.concatenate([top_idx, own_idx], axis=-1)
    blk_ok = jnp.concatenate([top_ok, jnp.ones((Sq, 1), dtype=bool)], axis=-1)
    bi = jnp.arange(B)[:, None, None, None]
    hi = jnp.arange(H)[None, :, None, None]
    kg = kb[bi, hi, idx]
    vg = vb[bi, hi, idx]
    kpos = idx[..., None] * MOBA_BLOCK + jnp.arange(MOBA_BLOCK, dtype=idx.dtype)
    dist = q_pos.astype(idx.dtype)[None, None, :, None, None] - kpos
    s = jnp.einsum('bqhd,bhqnkd->bhqnk', qf, kg.astype(jnp.float32)) * (Dh ** -0.5)
    s = s - alibi_slopes()[None, :, None, None, None] * dist.astype(jnp.float32)
    s = jnp.where(blk_ok[None, None, :, :, None] & (dist >= 0), s, NEG_INF)
    ns = idx.shape[-1]
    p = jax.nn.softmax(s.reshape(B, H, Sq, ns * MOBA_BLOCK), axis=-1).reshape(s.shape)
    return jnp.einsum('bhqnk,bhqnkd->bqhd', p.astype(vg.dtype), vg)

def moba_prompt(q, k, v):
    B, S, H, Dh = q.shape
    kb, vb, kmean = to_blocks(k, v)
    nq = S // Q_CHUNK
    qc = q.reshape(B, nq, Q_CHUNK, H, Dh).transpose(1, 0, 2, 3, 4)
    pos = jnp.arange(S, dtype=jnp.int32).reshape(nq, Q_CHUNK)
    o = lax.map(lambda a: moba_core(a[0], a[1], kb, vb, kmean), (qc, pos))
    return o.transpose(1, 0, 2, 3, 4).reshape(B, S, H, Dh)

def moba_sample(q, k_new, v_new, cache_k_l, cache_v_l, page_table):
    Bd, n_pages = page_table.shape
    past = n_pages * cache_k_l.shape[1]
    H, Dh = cache_k_l.shape[2], cache_k_l.shape[3]
    k_past = cache_k_l[page_table].reshape(Bd, past, H, Dh)
    v_past = cache_v_l[page_table].reshape(Bd, past, H, Dh)
    k_all = jnp.concatenate([k_past, k_new.astype(k_past.dtype)], axis=1)
    v_all = jnp.concatenate([v_past, v_new.astype(v_past.dtype)], axis=1)
    kb, vb, kmean = to_blocks(k_all, v_all)
    pos = past + jnp.arange(q.shape[1], dtype=jnp.int32)
    return moba_core(q, pos, kb, vb, kmean)

def retention_chunk(state, q, k, v):
    q = q.astype(jnp.float32)
    k = k.astype(jnp.float32)
    v = v.astype(jnp.float32)
    C = q.shape[1]
    lg = retention_log_decay()
    i = jnp.arange(C, dtype=jnp.float32)
    diff = i[:, None] - i[None, :]
    dmat = jnp.where(diff[None] >= 0, jnp.exp(lg[:, None, None] * jnp.maximum(diff, 0.0)[None]), 0.0)
    inner = jnp.einsum('bihd,bjhd->bhij', q, k) * dmat[None]
    o = jnp.einsum('bhij,bjhe->bihe', inner, v)
    o = o + jnp.einsum('bihd,bhde->bihe', q, state) * jnp.exp(lg[None, :] * (i[:, None] + 1.0))[None, :, :, None]
    k_dec = k * jnp.exp(lg[None, :] * (C - 1.0 - i[:, None]))[None, :, :, None]
    new_state = jnp.exp(lg * C)[None, :, None, None] * state + jnp.einsum('bjhd,bjhe->bhde', k_dec, v)
    return new_state, o

def retention_prompt(q, k, v):
    B, S, H, Dk = q.shape
    Dv = v.shape[-1]
    nc = S // RET_CHUNK
    def chunks(a):
        return a.reshape(B, nc, RET_CHUNK, H, a.shape[-1]).transpose(1, 0, 2, 3, 4)
    s0 = jnp.zeros((B, H, Dk, Dv), jnp.float32)
    s_fin, o = lax.scan(lambda s, a: retention_chunk(s, a[0], a[1], a[2]), s0, (chunks(q), chunks(k), chunks(v)))
    return o.transpose(1, 0, 2, 3, 4).reshape(B, S, H, Dv), s_fin

def retention_sample(state, q, k, v):
    s_new, o = retention_chunk(state.astype(jnp.float32), q, k, v)
    return o, s_new

def head_groupnorm(o, g, b):
    mu = jnp.mean(o, axis=-1, keepdims=True)
    var = jnp.mean(jnp.square(o - mu), axis=-1, keepdims=True)
    y = ((o - mu) * lax.rsqrt(var + EPS)).reshape(o.shape[0], o.shape[1], -1)
    return y * g.astype(jnp.float32) + b.astype(jnp.float32)

def decoder_layer(x, attend, retain, g_ffn1, w1_ffn1, w3_ffn1, w2_ffn1, g_mix, w_in, g_q, g_k,
                  gn_gain, gn_bias, w_pa, w_pr, w_o, g_ffn2, w1_ffn2, w3_ffn2, w2_ffn2):
    B, S, _ = x.shape
    x = x + 0.5 * swiglu(rmsnorm(x, g_ffn1), w1_ffn1, w3_ffn1, w2_ffn1)
    h = rmsnorm(x, g_mix)
    z = h @ w_in
    qa, ka, va, qr, kr, vr, gr, gate_a, gate_r = jnp.split(z, np.cumsum(SPLITS)[:-1], axis=-1)
    qa = rmsnorm(qa.reshape(B, S, N_HEADS_A, HEAD_DIM_A), g_q)
    ka = rmsnorm(ka.reshape(B, S, N_HEADS_A, HEAD_DIM_A), g_k)
    va = va.reshape(B, S, N_HEADS_A, HEAD_DIM_A)
    oa = attend(qa, ka, va).reshape(B, S, W_A)
    qr = qr.reshape(B, S, N_HEADS_R, KEY_DIM_R)
    kr = kr.reshape(B, S, N_HEADS_R, KEY_DIM_R) * (KEY_DIM_R ** -0.5)
    vr = vr.reshape(B, S, N_HEADS_R, VAL_DIM_R)
    o_r, s_new = retain(qr, kr, vr)
    o_r = head_groupnorm(o_r, gn_gain, gn_bias).astype(x.dtype) * jax.nn.silu(gr)
    merged = jax.nn.sigmoid(gate_a) * (oa @ w_pa) + jax.nn.sigmoid(gate_r) * (o_r @ w_pr)
    x = x + merged @ w_o
    x = x + 0.5 * swiglu(rmsnorm(x, g_ffn2), w1_ffn2, w3_ffn2, w2_ffn2)
    return x, ka, va, s_new

def setup_inputs(seed: int = 0) -> dict:
    key = jax.random.key(seed)
    ks = jax.random.split(key, 32)
    f32 = jnp.float32
    n_pages = PAST_LEN // PAGE_SIZE
    n_used = DEC_BATCH * n_pages
    n_pool = n_used + max(1, n_used // 4)

    def nrm(k, shape, scale):
        return jax.random.normal(k, shape, f32) * scale

    def gain(k, shape):
        return 1.0 + 0.05 * jax.random.normal(k, shape, f32)

    perm = jax.random.permutation(ks[5], n_pool).astype(jnp.int32)
    return {
        'x_prompt': nrm(ks[0], (BATCH, SEQ, D_MODEL), 1.0),
        'x_sample': nrm(ks[1], (DEC_BATCH, DEC_SEQ, D_MODEL), 1.0),
        'cache_k': nrm(ks[2], (DEPTH, n_pool, PAGE_SIZE, N_HEADS_A, HEAD_DIM_A), 1.0),
        'cache_v': nrm(ks[3], (DEPTH, n_pool, PAGE_SIZE, N_HEADS_A, HEAD_DIM_A), 1.0),
        'state_ret': nrm(ks[4], (DEPTH, DEC_BATCH, N_HEADS_R, KEY_DIM_R, VAL_DIM_R), 1.0),
        'page_table': perm[:n_used].reshape(DEC_BATCH, n_pages),
        'g_ffn1': gain(ks[6], (DEPTH, D_MODEL)),
        'w1_ffn1': nrm(ks[7], (DEPTH, D_MODEL, D_FF), D_MODEL ** -0.5),
        'w3_ffn1': nrm(ks[8], (DEPTH, D_MODEL, D_FF), D_MODEL ** -0.5),
        'w2_ffn1': nrm(ks[9], (DEPTH, D_FF, D_MODEL), D_FF ** -0.5),
        'g_mix': gain(ks[10], (DEPTH, D_MODEL)),
        'w_in': nrm(ks[11], (DEPTH, D_MODEL, D_IN), D_MODEL ** -0.5),
        'g_q': gain(ks[12], (DEPTH, HEAD_DIM_A)),
        'g_k': gain(ks[13], (DEPTH, HEAD_DIM_A)),
        'gn_gain': gain(ks[14], (DEPTH, W_RV)),
        'gn_bias': nrm(ks[15], (DEPTH, W_RV), 0.02),
        'w_pa': nrm(ks[16], (DEPTH, W_A, D_MODEL), W_A ** -0.5),
        'w_pr': nrm(ks[17], (DEPTH, W_RV, D_MODEL), W_RV ** -0.5),
        'w_o': nrm(ks[18], (DEPTH, D_MODEL, D_MODEL), D_MODEL ** -0.5),
        'g_ffn2': gain(ks[19], (DEPTH, D_MODEL)),
        'w1_ffn2': nrm(ks[20], (DEPTH, D_MODEL, D_FF), D_MODEL ** -0.5),
        'w3_ffn2': nrm(ks[21], (DEPTH, D_MODEL, D_FF), D_MODEL ** -0.5),
        'w2_ffn2': nrm(ks[22], (DEPTH, D_FF, D_MODEL), D_FF ** -0.5),
    }

def reference(x_prompt, x_sample, cache_k, cache_v, state_ret, page_table,
              g_ffn1, w1_ffn1, w3_ffn1, w2_ffn1, g_mix, w_in, g_q, g_k, gn_gain, gn_bias,
              w_pa, w_pr, w_o, g_ffn2, w1_ffn2, w3_ffn2, w2_ffn2):
    xp = x_prompt
    xs = x_sample
    kp_l, vp_l, sp_l, ks_l, vs_l, ss_l = [], [], [], [], [], []
    for l in range(DEPTH):
        lw = (g_ffn1[l], w1_ffn1[l], w3_ffn1[l], w2_ffn1[l], g_mix[l], w_in[l], g_q[l], g_k[l],
              gn_gain[l], gn_bias[l], w_pa[l], w_pr[l], w_o[l], g_ffn2[l], w1_ffn2[l], w3_ffn2[l], w2_ffn2[l])
        xp, kp, vp, sp = decoder_layer(xp, moba_prompt, retention_prompt, *lw)
        attend_s = lambda q, k, v, ck=cache_k[l], cv=cache_v[l]: moba_sample(q, k, v, ck, cv, page_table)
        retain_s = lambda q, k, v, st=state_ret[l]: retention_sample(st, q, k, v)
        xs, kd, vd, sd = decoder_layer(xs, attend_s, retain_s, *lw)
        kp_l.append(kp); vp_l.append(vp); sp_l.append(sp)
        ks_l.append(kd); vs_l.append(vd); ss_l.append(sd)
    k_prompt = jnp.stack(kp_l)
    v_prompt = jnp.stack(vp_l)
    state_prompt = jnp.stack(sp_l)
    k_sample = jnp.stack(ks_l)
    v_sample = jnp.stack(vs_l)
    state_sample = jnp.stack(ss_l)
    return (xp, xs, k_prompt, v_prompt, state_prompt, k_sample, v_sample, state_sample)


_drawn_inputs = setup_inputs


def setup_inputs(seed=0):
    import zlib

    import numpy as np

    out = dict(_drawn_inputs(seed))
    spreads = {}
    factors = {'gn_bias': 6.427, 'g_q': 2.889}
    for name, (base, spread) in spreads.items():
        noise = np.random.default_rng([zlib.crc32(name.encode()), seed]).standard_normal(out[name].shape)
        drawn = base * np.exp(spread * noise) if base else spread * noise
        out[name] = __import__('jax').numpy.asarray(drawn.astype(out[name].dtype))
    for name, factor in factors.items():
        out[name] = (out[name] * factor).astype(out[name].dtype)
    return out
```

```python
from contextlib import ExitStack
import math

import numpy as np
import concourse.bass as bass
from concourse import mybir

F32 = mybir.dt.float32
F32R = mybir.dt.float32r
I32 = mybir.dt.int32
ALU = mybir.AluOpType
ACT = mybir.ActivationFunctionType
AX = mybir.AxisListType.X
ds = bass.ds

P = 128
D_MODEL, D_FF, DEPTH = 1024, 2816, 2
SEQ, DEC_BATCH, DEC_SEQ = 256, 8, 4
TS = DEC_BATCH * DEC_SEQ
T = SEQ + TS
PAST, PAGE, N_POOL = 1024, 128, 80
N_PAGES = PAST // PAGE
H_A, D_A = 8, 64
H_R, D_R = 4, 128
EPS = 1e-6
NEG = -1e30
SCALE_A = D_A ** -0.5

KC = D_MODEL // P
FC = D_FF // P
CW = 2 * P
SLAB = KC * CW
UP_PAIRS = D_FF // CW
DP = D_MODEL // CW
F_PARTS = ((0, 8), (8, 15), (15, 22))

UP1 = 0
DOWN1 = UP1 + 2 * UP_PAIRS
ZIN = DOWN1 + 3 * DP
GATE = ZIN + 14
WO = GATE + 4 * DP
UP2 = WO + DP
DOWN2 = UP2 + 2 * UP_PAIRS
SLABS = DOWN2 + 3 * DP
assert SLABS % 2 == 0

ZQ, ZK, ZV, ZQR, ZKR, ZVR, ZGR, ZN = 0, 4, 8, 12, 16, 20, 24, 28

C_SHAPES = (("ident", 128), ("ones", 128), ("heads", 128), ("causal", 384), ("pastb", PAST), ("newb", 2 * TS),
            ("decay", H_R * 384), ("kdecay", 3 * H_R), ("qdecay", H_R * TS), ("batch", DEC_BATCH),
            ("rank", 4), ("sdecay", H_R * TS))
C_AT, _at = {}, 0
for _name, _n in C_SHAPES:
    C_AT[_name] = (_at, _n)
    _at += _n
C_N = _at
GL = 3 * KC + 2 * H_R + 2
G_FFN1, G_MIX, G_FFN2, G_GN, G_GB, G_Q, G_K = 0, 8, 16, 24, 28, 32, 33


def slope(h):
    return 2.0 ** (-8.0 * (h + 1.0) / H_A)


def log_decay(h):
    return math.log(1.0 - 2.0 ** (-5.0 - h))


def constants():
    c = {n: np.zeros((P, w), np.float64) for n, w in C_SHAPES}
    r = np.arange(P)
    c["ident"][:] = np.eye(P)
    c["ones"][:] = 1.0
    c["heads"][:] = (r[:, None] // D_A) == (r[None, :] // D_A)
    d = r[None, :] - r[:, None]
    c["causal"][:, 0:P] = np.where(d <= 0, d, -1e32)
    d = np.arange(SEQ)[None, :] - (r[:, None] + P)
    c["causal"][:, P:] = np.where(d <= 0, d, -1e32)
    q, h, jb = r % 4, (r // 4) % H_A, r // 32
    s8 = np.array([8.0 * slope(x) for x in h])
    c["pastb"][:] = s8[:, None] * (np.arange(PAST)[None, :] - PAST - q[:, None])
    for g in range(2):
        for t in range(TS):
            ok = (t // 4 == 4 * g + jb) & (t % 4 <= q)
            c["newb"][:, g * TS + t] = np.where(ok, s8 * (t % 4 - q), NEG)
    ks = D_R ** -0.5
    for hh in range(H_R):
        lg = log_decay(hh)
        d = np.arange(SEQ)[None, :] - r[:, None]
        m = np.where(d >= 0, np.exp(lg * np.maximum(d, 0)), 0.0) * ks
        c["decay"][:, hh * 384:hh * 384 + 256] = m
        c["decay"][:, hh * 384 + 256:hh * 384 + 384] = m[:, 0:P]
        for t in range(2):
            c["kdecay"][:, t * H_R + hh] = np.exp(lg * (SEQ - 1.0 - (t * P + r))) * ks
        c["kdecay"][:, 2 * H_R + hh] = np.exp(lg * (DEC_SEQ - 1.0 - r % 4)) * ks
        i = np.arange(TS)
        c["qdecay"][:, hh * TS:(hh + 1) * TS] = np.exp(lg * (i % 4 + 1.0))[None, :]
        ok = (r[:, None] // 4 == i[None, :] // 4) & (i[None, :] % 4 >= r[:, None] % 4)
        c["sdecay"][:, hh * TS:(hh + 1) * TS] = np.where(ok, np.exp(lg * np.maximum(i[None, :] % 4 - r[:, None] % 4, 0)), 0) * ks
    c["batch"][:] = (r[:, None] // 4) == np.arange(DEC_BATCH)[None, :]
    c["rank"][:] = np.arange(1, 5)[None, :]
    return np.concatenate([c[n] for n, _ in C_SHAPES], axis=1).astype(np.float32)


class Signal:

    def __init__(self, sem, per_layer, credit=0, step=1):
        self.sem, self.per_layer, self.credit, self.step = sem, per_layer, credit, step

    def after(self, layer, n):
        return (layer * self.per_layer + (n + self.credit)) * self.step


def trunk(nc, x_prompt, x_sample, cache_k, cache_v, state_ret, page_table, g_ffn1, w1_ffn1, w3_ffn1, w2_ffn1,
          g_mix, w_in, g_q, g_k, gn_gain, gn_bias, w_pa, w_pr, w_o, g_ffn2, w1_ffn2, w3_ffn2, w2_ffn2, consts,
          y_prompt, y_sample, k_prompt, v_prompt, state_prompt, k_sample, v_sample, state_sample):
    ctx = ExitStack()
    with ctx:
        def sb(name, shape, dt=F32):
            return ctx.enter_context(nc.sbuf_tensor(name, shape, dt))

        def signal(name, per_layer=1, credit=0, step=1):
            return Signal(ctx.enter_context(nc.semaphore(name)), per_layer, credit, step)

        xT = sb("xT", [P, KC, T])
        h_hi = sb("h_hi", [P, KC, T], F32R)
        h_lo = sb("h_lo", [P, KC, T], F32R)
        raw = sb("raw", [P, 2, SLAB])
        w_hi = sb("w_hi", [P, 2, SLAB], F32R)
        w_lo = sb("w_lo", [P, 2, SLAB], F32R)
        const = sb("const", [P, C_N])
        gains = sb("gains", [P, DEPTH * GL])
        gain = sb("gain", [P, GL])
        gain_rows = sb("gain_rows", [DEPTH * GL, P])
        pages = sb("pages", [1, DEC_BATCH * N_PAGES], I32)
        silu = sb("silu", [P, 2, 2, T])
        hid_f = sb("hid_f", [P, 2, 2, T])
        rstd = sb("rstd", [P, T])
        kv = sb("kv", [P, 2, 4, H_A * D_A])
        q_blocks = sb("q_blocks", [P, DEC_BATCH, 4, 32])
        mx = sb("mx", [P, 16])
        small = sb("small", [P, 2, 64])
        attn_s = sb("attn_s", [P, 2 * (PAST + TS)])
        work = sb("work", [P, 2, 2048])
        o_all = sb("o_all", [P, 2, 4, T])
        arena = sb("arena", [P, 2, FC, T], F32R)
        hid_hi, hid_lo = arena[:, 0], arena[:, 1]
        base = nc.sbuf_base - 2 * FC * T * 4
        chunk = 4 * T

        def over(name, shape, dt, at):
            return nc.alloc_sbuf_tensor_at(name, shape, dt, offset=base + at)

        z = over("z", [P, ZN, T], F32, 0)
        v_tok = over("v_tok", [P, 3, 512], F32, ZN * chunk)
        kd_tok = over("kd_tok", [P, 3, 512], F32, ZN * chunk + 6144)
        vr_tok = over("vr_tok", [P, 3, 512], F32, ZN * chunk + 12288)
        oa_hi = over("oa_hi", [P, 4, T], F32R, 0)
        oa_lo = over("oa_lo", [P, 4, T], F32R, 4 * chunk)
        or_hi = over("or_hi", [P, 4, T], F32R, 8 * chunk)
        or_lo = over("or_lo", [P, 4, T], F32R, 12 * chunk)
        mg_hi = over("mg_hi", [P, KC, T], F32R, ZN * chunk)
        mg_lo = over("mg_lo", [P, KC, T], F32R, ZN * chunk + 9216)
        stage = over("stage", [P, 3, D_MODEL], F32, 0)

        k_tok = o_all[:, :, :, :].rearrange("p a c t -> p (a c t)")[:, 0:1536].rearrange("p (t n) -> p t n", t=3)
        oT, orT = o_all[:, 0], o_all[:, 1]
        wk = work[:, :, :].rearrange("p a n -> p (a n)")
        squares = wk[:, 0:KC * T].rearrange("p (c t) -> p c t", c=KC)
        state = work[:, 0, :].rearrange("p (a b e) -> p a b e", a=2, b=8)
        v_masked = wk[0:TS, 2048:3072].rearrange("p (b e) -> p b e", b=8)
        inner = wk[:, 3072:3456]
        inner_s = wk[0:TS, 3456:3488]
        q_dec = wk[:, 3488:3520]
        state_p = wk[:, 3520:4032].rearrange("p (h e) -> p h e", h=H_R)
        squares_r = attn_s[:, 0:4 * T].rearrange("p (c t) -> p c t", c=4)
        prob_p = attn_s[:, 0:1536].rearrange("p (h k) -> p h k", h=4)
        probT_p = wk[:, 2048:3584].rearrange("p (h k) -> p h k", h=4)
        S = attn_s[:, :].rearrange("p (g k) -> p g k", g=2)
        kT = work[:, :, :].rearrange("p s (j n) -> p s j n", j=4)
        probT = work[:, 0, :].rearrange("p (g n r) -> p g n r", g=2, n=N_PAGES)
        probT_new = work[0:TS, 1, 0:256].rearrange("p (g r) -> p g r", g=2)

        def cst(name, lo=0, hi=None):
            at, n = C_AT[name]
            return const[:, at + lo:at + (n if hi is None else hi)]

        ident, ones, heads = cst("ident"), cst("ones"), cst("heads")
        ps = ctx.enter_context(nc.psum_tensor("ps", [P, 8, 512], F32))

        raw_loaded = [signal(f"raw_loaded{s}", SLABS // 2, 0, 16) for s in range(2)]
        hi_done = signal("hi_done", SLABS)
        split_done = signal("split_done", SLABS, 2)
        slab_used = signal("slab_used", SLABS, 2)
        silu_done = signal("silu_done", 2 * UP_PAIRS)
        up_read = signal("up_read", 2 * UP_PAIRS, 2)
        hid_hi_done = signal("hid_hi_done", 2 * UP_PAIRS)
        hid_done = signal("hid_done", 2 * UP_PAIRS)
        x_done = signal("x_done", 3 * DP, 4)
        rms_sq = signal("rms_sq", 3)
        rms_sum = signal("rms_sum", 3)
        rms_ln = signal("rms_ln", 3)
        rms_rstd = signal("rms_rstd", 3)
        rms_h = signal("rms_h", 12)
        h_hi_done = signal("h_hi_done", 12)
        h_done = signal("h_done", 12)
        gain_done = signal("gain_done")
        z_done = signal("z_done", 14)
        qk_sq, qk_sum, qk_ln, qk_rstd, qk_done = (signal(n, 2) for n in ("qk_sq", "qk_sum", "qk_ln", "qk_rstd", "qk_done"))
        q_blocks_done = signal("q_blocks_done")
        tr_done = signal("tr_done", 4)
        tok_act = signal("tok_act", 3)
        tok_dve = signal("tok_dve", 1)
        kv_stored = signal("kv_stored", 4, 0, 16)
        state_loaded = [signal(f"state_loaded{s}", 2, 0, 16) for s in range(2)]
        state_stored = [signal(f"state_stored{s}", 2, 0, 16) for s in range(2)]
        state_p_stored = signal("state_p_stored", 1, 0, 16)
        inner_done = signal("inner_done", H_R)
        ret_in = signal("ret_in", H_R)
        ret_out = signal("ret_out", H_R)
        ret_act = signal("ret_act", H_R)
        ret_dve = signal("ret_dve", H_R)
        gn_mean, gn_cen, gn_sq, gn_var, gn_ln, gn_rstd = (signal(n) for n in ("gn_mean", "gn_cen", "gn_sq", "gn_var", "gn_ln", "gn_rstd"))
        gr_silu, or_done, or_hi_done, or_lo_done = (signal(n) for n in ("gr_silu", "or_done", "or_hi_done", "or_lo_done"))
        pp_scores, pp_max, pp_exp, pp_norm, pp_tr, pp_tr_act, pp_tr_dve, pp_out, pp_read = (
            signal(n, 2) for n in ("pp_scores", "pp_max", "pp_exp", "pp_norm", "pp_tr", "pp_tr_act", "pp_tr_dve", "pp_out", "pp_read"))
        new_scores, new_read = signal("new_scores"), signal("new_read")
        kv_loaded = [signal(f"kv_loaded{s}", 16, 0, 64) for s in range(2)]
        kv_used = signal("kv_used", 64, 4)
        kt_act = signal("kt_act", 16, 1)
        kt_dve = signal("kt_dve", 16, 1)
        sc_done = signal("sc_done", 16, 2)
        sc_read = signal("sc_read", 16, 2)
        sm_bias, sm_exp, sm_norm, sm_tr, sm_tr_act, sm_tr_dve = (
            signal(n, 2) for n in ("sm_bias", "sm_exp", "sm_norm", "sm_tr", "sm_tr_act", "sm_tr_dve"))
        oa_done, oa_hi_done, oa_lo_done = (signal(n) for n in ("oa_done", "oa_hi_done", "oa_lo_done"))
        gate_done = signal("gate_done", 2 * DP, 2)
        merge_t = signal("merge_t", DP)
        merged = signal("merged", DP, 1)
        mg_hi_done = signal("mg_hi_done", DP)
        mg_done = signal("mg_done", DP)
        LINKS = 28
        dve_link = signal("dve_link", LINKS)
        pool_passed = signal("pool_passed")
        loaded = signal("loaded", 1, 0, 16)
        pages_loaded = signal("pages_loaded", 1, 0, 16)
        first_tr, gains_done, zeroed = signal("first_tr"), signal("gains_done"), signal("zeroed")
        last_tr, last_act, last_dve, y_stored = signal("last_tr"), signal("last_act"), signal("last_dve"), signal("y_stored", 1, 0, 16)

        def by_chunks(w):
            return w.rearrange("l (k p) f -> l p k f", p=P)

        up = ((by_chunks(w1_ffn1), by_chunks(w3_ffn1)), (by_chunks(w1_ffn2), by_chunks(w3_ffn2)))
        down = (by_chunks(w2_ffn1), by_chunks(w2_ffn2))
        w_in_v, w_pa_v, w_pr_v, w_o_v = (by_chunks(w) for w in (w_in, w_pa, w_pr, w_o))
        k_pages = cache_k.rearrange("l n p h d -> (l n) p (h d)")
        v_pages = cache_v.rearrange("l n p h d -> (l n) p (h d)")

        block = ctx.enter_context(nc.Block())

        @block.sync
        def _(sp):
            def load(layer, pair, slot, src, chunks, col):
                sp.wait_ge(split_done.sem, split_done.after(layer, 0) - 1 + (pair * 2 + slot))
                k0, k1 = chunks
                n = k1 - k0
                dst = raw[:, slot, 0:n * CW].rearrange("p (k f) -> p k f", k=n)
                sp.dma_start(dst, src[ds(layer, 1), :, k0:k1, ds(col, CW)].rearrange("l p k f -> p (l k) f"))\
                    .then_inc(raw_loaded[slot].sem, 16)

            with sp.Fori(0, DEPTH) as layer:
                def up_slabs(f, first):
                    with sp.Fori(0, UP_PAIRS) as i:
                        for s in range(2):
                            load(layer, i + first // 2, s, up[f][s], (0, KC), i * CW)

                def down_slabs(f, first):
                    with sp.Fori(0, DP // 2) as i:
                        for n in range(6):
                            load(layer, i * 3 + (first // 2 + n // 2), n % 2, down[f], F_PARTS[n % 3], i * (2 * CW) + n // 3 * CW)

                up_slabs(0, UP1)
                down_slabs(0, DOWN1)
                with sp.Fori(0, 7) as i:
                    for s in range(2):
                        load(layer, i + ZIN // 2, s, w_in_v, (0, KC), i * (2 * CW) + s * CW)
                with sp.Fori(0, DP) as i:
                    load(layer, i * 2 + GATE // 2, 0, w_in_v, (0, KC), i * CW + ZN * P)
                    load(layer, i * 2 + GATE // 2, 1, w_in_v, (0, KC), i * CW + (ZN * P + D_MODEL))
                    load(layer, i * 2 + (GATE // 2 + 1), 0, w_pa_v, (0, 4), i * CW)
                    load(layer, i * 2 + (GATE // 2 + 1), 1, w_pr_v, (0, 4), i * CW)
                with sp.Fori(0, DP // 2) as i:
                    for s in range(2):
                        load(layer, i + WO // 2, s, w_o_v, (0, KC), i * (2 * CW) + s * CW)
                up_slabs(1, UP2)
                down_slabs(1, DOWN2)

        @block.gpsimd
        def _(pool):
            pool.dma_start(pages[:, :], page_table.rearrange("(o b) n -> o (b n)", o=1)).then_inc(pages_loaded.sem, 16)
            pool.wait_ge(pages_loaded.sem, 16)
            with pool.Fori(0, DEPTH) as layer:
                def load_unit(cache, g, n, slot, unit):
                    pool.wait_ge(kv_used.sem, kv_used.after(layer, 2 * unit - 2))
                    for j in range(4):
                        page = pool.value_load(pages[0:1, ds(n + (4 * g + j) * N_PAGES, 1)], min_val=0, max_val=N_POOL - 1)
                        pool.dma_start(kv[:, slot, j:j + 1, :], cache[ds(layer * N_POOL + page, 1), :, :].rearrange("a p n -> p a n"))\
                            .then_inc(kv_loaded[slot].sem, 16)

                def wait(signal, n):
                    pool.wait_ge(signal.sem, signal.after(layer, n))
                    pool.sem_inc(pool_passed.sem, 1)

                def load_state(h):
                    src = state_ret[ds(layer, 1), :, h, :, :].rearrange("l b d e -> d (l b) e")
                    pool.dma_start(state[:, h % 2], src).then_inc(state_loaded[h % 2].sem, 16)

                def load_units(cache, g, first):
                    with pool.Fori(0, N_PAGES // 2) as i:
                        for s in range(2):
                            load_unit(cache, g, i * 2 + s, s, i * 2 + (first + s))

                wait(qk_done, 2)
                load_state(0)
                load_state(1)
                wait(tok_act, 1)
                pool.dma_start(v_prompt[ds(layer, 1), 0].rearrange("l (t p) h d -> p (l t) (h d)", p=P),
                               v_tok[:, 0:2, :]).then_inc(kv_stored.sem, 16)
                pool.dma_start(v_sample[ds(layer, 1)].rearrange("l b s h d -> (l b s) (h d)"),
                               v_tok[0:TS, 2, :]).then_inc(kv_stored.sem, 16)
                wait(tok_act, 3)
                pool.dma_start(k_prompt[ds(layer, 1), 0].rearrange("l (t p) h d -> p (l t) (h d)", p=P),
                               k_tok[:, 0:2, :]).then_inc(kv_stored.sem, 16)
                pool.dma_start(k_sample[ds(layer, 1)].rearrange("l b s h d -> (l b s) (h d)"),
                               k_tok[0:TS, 2, :]).then_inc(kv_stored.sem, 16)
                for h in range(H_R):
                    wait(ret_dve, h + 1)
                    pool.dma_start(state_sample[ds(layer, 1), :, h, :, :].rearrange("l b d e -> d (l b) e"),
                                   state[:, h % 2]).then_inc(state_stored[h % 2].sem, 16)
                    if h < 2:
                        wait(state_stored[h], 1)
                        load_state(h + 2)
                wait(ret_act, H_R)
                pool.dma_start(state_prompt[ds(layer, 1), 0].rearrange("l h d e -> d (l h) e"),
                               state_p).then_inc(state_p_stored.sem, 16)
                load_units(k_pages, 0, 0)
                load_units(k_pages, 1, 8)
                load_units(v_pages, 0, 16)
                load_units(v_pages, 1, 24)
            for s in range(2):
                pool.wait_ge(state_stored[s].sem, state_stored[s].after(DEPTH - 1, 2))
            pool.wait_ge(state_p_stored.sem, 16 * DEPTH)
            pool.wait_ge(kv_stored.sem, kv_stored.after(DEPTH - 1, 4))
            pool.wait_ge(last_act.sem, 3)
            pool.wait_ge(last_dve.sem, 3)
            pool.dma_start(y_prompt[0].rearrange("(t p) d -> p t d", p=P), stage[:, 0:2, :]).then_inc(y_stored.sem, 16)
            pool.dma_start(y_sample.rearrange("b s d -> (b s) d"), stage[0:TS, 2, :]).then_inc(y_stored.sem, 16)
            pool.wait_ge(y_stored.sem, 32)

        @block.scalar
        def _(act):
            n_loads = 0
            for dst, src in ((const[:, :], consts),
                             (stage[:, 0:2, :], x_prompt[0].rearrange("(t p) d -> p t d", p=P)),
                             (stage[0:TS, 2, :], x_sample.rearrange("b s d -> (b s) d"))):
                act.dma_start(dst, src).then_inc(loaded.sem, 16)
                n_loads += 1
            for row, arr, n in ((G_FFN1, g_ffn1, KC), (G_MIX, g_mix, KC), (G_FFN2, g_ffn2, KC), (G_GN, gn_gain, H_R), (G_GB, gn_bias, H_R)):
                for l in range(DEPTH):
                    act.dma_start(gain_rows[l * GL + row:l * GL + row + n, :], arr[l].rearrange("(c p) -> c p", p=P)).then_inc(loaded.sem, 16)
                    n_loads += 1
            for row, arr in ((G_Q, g_q), (G_K, g_k)):
                for l in range(DEPTH):
                    for half in range(2):
                        act.dma_start(gain_rows[l * GL + row:l * GL + row + 1, half * D_A:(half + 1) * D_A],
                                      arr[l:l + 1, :]).then_inc(loaded.sem, 16)
                        n_loads += 1
            assert n_loads == N_LOADS

            with act.Fori(0, DEPTH) as layer:
                def hi(pair, slot, chunks=KC):
                    act.wait_ge(raw_loaded[slot].sem, raw_loaded[slot].after(layer, pair + 1))
                    act.wait_ge(slab_used.sem, slab_used.after(layer, 2 * pair + slot - 1))
                    act.activation(w_hi[:, slot, 0:chunks * CW], raw[:, slot, 0:chunks * CW], ACT.Copy).then_inc(hi_done.sem, 1)

                def hi_slab(n, chunks=KC):
                    hi(n // 2, n % 2, chunks)

                def rms(r):
                    act.wait_ge(x_done.sem, x_done.after(layer, DP * r))
                    act.activation(squares, xT[:, :, :], ACT.Square).then_inc(rms_sq.sem, 1)
                    act.wait_ge(rms_sum.sem, rms_sum.after(layer, r + 1))
                    act.activation(rstd[:, :], ps[:, 0, 0:T], ACT.Ln, bias=eps_col, scale=1.0 / D_MODEL).then_inc(rms_ln.sem, 1)
                    act.wait_ge(rms_ln.sem, rms_ln.after(layer, r + 1))
                    act.activation(rstd[:, :], rstd[:, :], ACT.Exp, scale=-0.5).then_inc(rms_rstd.sem, 1)
                    for c in range(0, KC, 2):
                        act.wait_ge(rms_h.sem, rms_h.after(layer, 4 * r + c // 2 + 1))
                        act.activation(h_hi[:, c:c + 2, :], squares[:, c:c + 2, :], ACT.Copy).then_inc(h_hi_done.sem, 1)

                def up_silu(f, i, s, slabs, buf):
                    act.wait_ge(up_read.sem, up_read.after(layer, f * UP_PAIRS - 1) + i)
                    act.wait_ge(slab_used.sem, slab_used.after(layer, slabs + 1) + i * 2)
                    act.activation(silu[:, buf], ps[:, 4 * buf:4 * buf + 2, 0:T], ACT.Silu).then_inc(silu_done.sem, 1)
                    act.wait_ge(up_read.sem, up_read.after(layer, f * UP_PAIRS + 1) + i)
                    act.activation(hid_hi[:, ds(i * 2, 2), :], hid_f[:, buf], ACT.Copy).then_inc(hid_hi_done.sem, 1)

                def ffn(f, r, first_up, first_down):
                    hi_slab(first_up)
                    hi_slab(first_up + 1)
                    rms(r)
                    with act.Fori(0, UP_PAIRS // 2) as t:
                        for b in range(2):
                            i = t * 2 + b
                            hi(i + (first_up // 2 + 1), 0)
                            hi(i + (first_up // 2 + 1), 1)
                            up_silu(f, i, b, first_up, b)
                    hi_slab(first_down, 8)
                    hi_slab(first_down + 1, 7)
                    up_silu(f, UP_PAIRS - 1, 0, first_up, 0)
                    for n in range(2, 3 * DP):
                        a, b = F_PARTS[n % 3]
                        hi_slab(first_down + n, b - a)

                eps_col = EPS
                ffn(0, 0, UP1, DOWN1)

                def z_copy(pair, slot):
                    act.wait_ge(slab_used.sem, slab_used.after(layer, ZIN + 1 + slot) + pair * 2)
                    act.activation(z[:, ds(pair * 4 + 2 * slot, 2), :], ps[:, 2 * slot:2 * slot + 2, 0:T], ACT.Copy).then_inc(z_done.sem, 1)

                hi_slab(ZIN)
                hi_slab(ZIN + 1)
                rms(1)
                with act.Fori(0, 6) as i:
                    for s in range(2):
                        z_copy(i, s)
                        hi(i + (ZIN // 2 + 1), s)
                z_copy(6, 0)
                z_copy(6, 1)

                for n, (zc, bank) in enumerate(((ZQ, 4), (ZK, 0))):
                    act.wait_ge(z_done.sem, z_done.after(layer, 14))
                    act.activation(squares[:, 4 * n:4 * n + 4], z[:, zc:zc + 4, :], ACT.Square).then_inc(qk_sq.sem, 1)
                for n, (zc, bank) in enumerate(((ZQ, 4), (ZK, 0))):
                    act.wait_ge(qk_sum.sem, qk_sum.after(layer, n + 1))
                    act.activation(squares[:, 4 * n:4 * n + 4], ps[:, bank:bank + 4, 0:T], ACT.Ln, bias=eps_col, scale=1.0 / D_A).then_inc(qk_ln.sem, 1)
                for n in range(2):
                    act.wait_ge(qk_ln.sem, qk_ln.after(layer, n + 1))
                    act.activation(squares[:, 4 * n:4 * n + 4], squares[:, 4 * n:4 * n + 4], ACT.Exp, scale=-0.5).then_inc(qk_rstd.sem, 1)

                for n, (tr, bank, tok) in enumerate(((0, 4, v_tok), (1, 0, vr_tok), (3, 0, k_tok))):
                    act.wait_ge(tr_done.sem, tr_done.after(layer, tr + 1))
                    act.activation(tok[:, 0:2, :], ps[:, bank:bank + 2, :], ACT.Copy)
                    act.activation(tok[0:TS, 2, :], ps[0:TS, bank + 2, :], ACT.Copy).then_inc(tok_act.sem, 1)

                act.wait_ge(kv_stored.sem, kv_stored.after(layer, 4))
                for h in range(H_R):
                    act.wait_ge(ret_out.sem, ret_out.after(layer, h + 1))
                    act.activation(orT[:, h, :], ps[:, 1, 0:T], ACT.Copy)
                    act.activation(state_p[:, h, :], ps[:, 2, 0:P], ACT.Copy).then_inc(ret_act.sem, 1)
                act.wait_ge(gn_cen.sem, gn_cen.after(layer, 1))
                act.activation(squares_r, orT, ACT.Square).then_inc(gn_sq.sem, 1)
                act.wait_ge(gn_var.sem, gn_var.after(layer, 1))
                act.activation(squares_r, ps[:, 4:8, 0:T], ACT.Ln, bias=eps_col, scale=1.0 / D_R).then_inc(gn_ln.sem, 1)
                act.wait_ge(gn_ln.sem, gn_ln.after(layer, 1))
                act.activation(squares_r, squares_r, ACT.Exp, scale=-0.5).then_inc(gn_rstd.sem, 1)
                act.activation(z[:, ZGR:ZGR + 4, :], z[:, ZGR:ZGR + 4, :], ACT.Silu).then_inc(gr_silu.sem, 1)
                act.wait_ge(or_done.sem, or_done.after(layer, 1))
                act.activation(or_hi[:, :, :], orT, ACT.Copy).then_inc(or_hi_done.sem, 1)

                for hb in range(2):
                    act.wait_ge(pp_max.sem, pp_max.after(layer, hb + 1))
                    for i in range(8):
                        hi_, tile = i % 4, i // 4
                        cols = slice(0, P) if tile == 0 else slice(P, 3 * P)
                        last = act.activation(prob_p[:, hi_, cols], prob_p[:, hi_, cols], ACT.Exp, bias=mx[:, i:i + 1],
                                              scale=SCALE_A, accum_out=small[:, 0, i:i + 1])
                    last.then_inc(pp_exp.sem, 1)
                    act.wait_ge(pp_tr.sem, pp_tr.after(layer, hb + 1))
                    act.wait_ge(state_p_stored.sem, state_p_stored.after(layer, 1))
                    act.activation(probT_p[:, 0:2, :], ps[:, 4:6, 0:384], ACT.Copy).then_inc(pp_tr_act.sem, 1)
                    act.wait_ge(pp_out.sem, pp_out.after(layer, hb + 1))
                    act.activation(oT[:, 2 * hb:2 * hb + 2, 0:SEQ], ps[:, 0:2, 0:SEQ], ACT.Copy).then_inc(pp_read.sem, 1)

                for s in range(2):
                    act.wait_ge(state_stored[s].sem, state_stored[s].after(layer, 2))
                for g in range(2):
                    with act.Fori(0, N_PAGES // 2) as i:
                        for s in range(2):
                            act.wait_ge(kv_used.sem, kv_used.after(layer, 16 * g + 2 * s + 1) + i * 4)
                            act.wait_ge(sc_done.sem, sc_done.after(layer, 8 * g + s - 1) + i * 2)
                            act.activation(kT[:, s, 0:2, :], ps[:, 0:2, :], ACT.Copy).then_inc(kt_act.sem, 1)
                for g in range(2):
                    act.wait_ge(sm_bias.sem, sm_bias.after(layer, g + 1))
                    for n in range(5):
                        cols = slice(256 * n, min(256 * n + 256, PAST + TS))
                        last = act.activation(S[:, g, cols], S[:, g, cols], ACT.Exp, bias=small[:, g, 8 + n:9 + n],
                                              scale=SCALE_A, accum_out=small[:, g, 16 + n:17 + n])
                    last.then_inc(sm_exp.sem, 1)
                for g in range(2):
                    act.wait_ge(sm_tr.sem, sm_tr.after(layer, g + 1))
                    act.activation(probT[:, g].rearrange("p n r -> p (n r)").rearrange("p (a m) -> p a m", a=2),
                                   ps[:, 2 * g:2 * g + 2, :], ACT.Copy).then_inc(sm_tr_act.sem, 1)
                act.wait_ge(kv_used.sem, kv_used.after(layer, 64))
                for half in range(2):
                    rows = slice(64 * half, 64 * half + 64)
                    src = ps[rows, 7, 0:256].rearrange("p (b c a q) -> p c b a q", b=8, c=4, a=2)[:, :, :, half, :]
                    last = act.activation(oT[rows, :, SEQ:T].rearrange("p c (b q) -> p c b q", b=8), src, ACT.Copy)
                last.then_inc(oa_done.sem, 1)
                act.wait_ge(oa_done.sem, oa_done.after(layer, 1))
                act.activation(oa_hi[:, :, :], oT, ACT.Copy).then_inc(oa_hi_done.sem, 1)

                def gate(i, n):
                    act.wait_ge(slab_used.sem, slab_used.after(layer, GATE + 1 + n) + i * 4)
                    act.wait_ge(merged.sem, merged.after(layer, 0) + i)
                    act.activation(silu[:, n], ps[:, 2 * n:2 * n + 2, 0:T], ACT.Sigmoid).then_inc(gate_done.sem, 1)

                def merge_hi(i):
                    act.wait_ge(merged.sem, merged.after(layer, 1) + i)
                    act.activation(mg_hi[:, ds(i * 2, 2), :], hid_f[:, 0], ACT.Copy).then_inc(mg_hi_done.sem, 1)

                def gate_step(i, first):
                    g2 = i * 2 + GATE // 2
                    hi(g2, 0)
                    hi(g2, 1)
                    hi(g2 + 1, 0, 4)
                    gate(i, 0)
                    if not first:
                        merge_hi(i - 1)
                    hi(g2 + 1, 1, 4)
                    gate(i, 1)

                gate_step(0, True)
                with act.Fori(1, DP) as i:
                    gate_step(i, False)
                hi_slab(WO)
                hi_slab(WO + 1)
                merge_hi(DP - 1)
                hi_slab(WO + 2)
                hi_slab(WO + 3)
                ffn(1, 2, UP2, DOWN2)

            act.wait_ge(last_tr.sem, 1)
            for t in range(3):
                rows = P if t < 2 else TS
                act.activation(stage[0:rows, t, 0:512], ps[0:rows, 2 * t, :], ACT.Copy).then_inc(last_act.sem, 1)

        @block.tensor
        def _(pe):
            def triple(out, w, wl, x, xl, start, stop):
                pe.matmul(out, w, x, start=start, stop=False)
                pe.matmul(out, wl, x, start=False, stop=False)
                return pe.matmul(out, w, xl, start=False, stop=stop)

            pe.wait_ge(loaded.sem, 16 * N_LOADS)
            for c in range(KC):
                for t in range(3):
                    rows = P if t < 2 else TS
                    pe.transpose(ps[:, c, t * P:t * P + rows], stage[0:rows, t, c * P:(c + 1) * P], ident[0:rows, 0:rows])
            pe.transpose(ps[:, 0, 300:300 + DEPTH * GL], gain_rows[:, :], ident[0:DEPTH * GL, 0:DEPTH * GL]).then_inc(first_tr.sem, 1)

            with pe.Fori(0, DEPTH) as layer:
                def slab(pair, slot, bank, hi, lo, k0, n, start=True, stop=True):
                    pe.wait_ge(split_done.sem, split_done.after(layer, 2 * pair + slot + 1))
                    for t in range(2):
                        for k in range(n):
                            cols = slice(k * CW + t * P, k * CW + t * P + P)
                            last = triple(ps[:, bank + t, 0:T], w_hi[:, slot, cols], w_lo[:, slot, cols],
                                          hi[:, k0 + k, :], lo[:, k0 + k, :], start and k == 0, stop and k == n - 1)
                    last.then_inc(slab_used.sem, 1)

                def rms(r):
                    pe.wait_ge(rms_sq.sem, rms_sq.after(layer, r + 1))
                    for c in range(KC):
                        last = pe.matmul(ps[:, 0, 0:T], ones, squares[:, c, :], start=c == 0, stop=c == KC - 1)
                    last.then_inc(rms_sum.sem, 1)
                    pe.wait_ge(h_done.sem, h_done.after(layer, 4 * r + 4))

                def ffn(f, r, first_up, first_down):
                    rms(r)

                    def up_pair(i, buf):
                        pe.wait_ge(up_read.sem, up_read.after(layer, f * UP_PAIRS - 1) + i)
                        for s in range(2):
                            slab(i + first_up // 2, s, 4 * buf + 2 * s, h_hi, h_lo, 0, KC)

                    up_pair(0, 0)
                    with pe.Fori(0, UP_PAIRS // 2) as t:
                        up_pair(t * 2 + 1, 1)
                        up_pair(t * 2 + 2, 0)
                    with pe.Fori(0, DP // 2) as t:
                        for n in range(6):
                            k0, k1 = F_PARTS[n % 3]
                            bank = 4 + 2 * (n // 3)
                            if n % 3 == 0:
                                pe.wait_ge(x_done.sem, x_done.after(layer, (0, 2 * DP)[f] + n // 3 - 1) + t * 2)
                                if n == 0:
                                    pe.wait_ge(up_read.sem, up_read.after(layer, f * UP_PAIRS + UP_PAIRS - 1))
                            pe.wait_ge(hid_done.sem, hid_done.after(layer, f * UP_PAIRS + (k1 + 1) // 2))
                            slab(t * 3 + (first_down // 2 + n // 2), n % 2, bank, hid_hi, hid_lo, k0, k1 - k0, n % 3 == 0, n % 3 == 2)

                ffn(0, 0, UP1, DOWN1)

                rms(1)

                def z_pair(i, first):
                    for s in range(2):
                        if not first:
                            pe.wait_ge(z_done.sem, z_done.after(layer, s - 1) + i * 2)
                        slab(i + ZIN // 2, s, 2 * s, h_hi, h_lo, 0, KC)

                z_pair(0, True)
                with pe.Fori(1, 7) as i:
                    z_pair(i, False)

                pe.wait_ge(z_done.sem, z_done.after(layer, 14))
                for n, bank in enumerate((4, 0)):
                    pe.wait_ge(qk_sq.sem, qk_sq.after(layer, n + 1))
                    for c in range(4):
                        last = pe.matmul(ps[:, bank + c, 0:T], heads, squares[:, 4 * n + c, :], start=True, stop=True)
                    last.then_inc(qk_sum.sem, 1)

                for n, (zc, bank) in enumerate(((ZV, 4), (ZVR, 0), (ZKR, 4), (ZK, 0))):
                    if n < 2:
                        pe.wait_ge(qk_ln.sem, qk_ln.after(layer, n + 1))
                    else:
                        pe.wait_ge(tok_act.sem, tok_act.after(layer, n - 1))
                    if n == 3:
                        pe.wait_ge(qk_done.sem, qk_done.after(layer, 2))
                    for c in range(4):
                        for t in range(3):
                            rows = P if t < 2 else TS
                            last = pe.transpose(ps[0:rows, bank + t, c * P:(c + 1) * P], z[:, zc + c, t * P:t * P + rows], ident)
                    last.then_inc(tr_done.sem, 1)
                pe.wait_ge(tok_act.sem, tok_act.after(layer, 3))
                pe.wait_ge(tok_dve.sem, tok_dve.after(layer, 1))

                def ret_inner(h):
                    if h:
                        pe.wait_ge(ret_in.sem, ret_in.after(layer, h))
                    kr, qr = z[:, ZKR + h, :], z[:, ZQR + h, :]
                    pe.matmul(ps[:, 0, 0:256], kr[:, 0:P], qr[:, 0:SEQ], start=True, stop=True)
                    pe.matmul(ps[:, 0, 256:384], kr[:, P:SEQ], qr[:, P:SEQ], start=True, stop=True)
                    pe.matmul(ps[0:TS, 0, 384:384 + TS], kr[:, SEQ:T], qr[:, SEQ:T], start=True, stop=True).then_inc(inner_done.sem, 1)

                ret_inner(0)
                for h in range(H_R):
                    if h + 1 < H_R:
                        ret_inner(h + 1)
                    pe.wait_ge(ret_in.sem, ret_in.after(layer, h + 1))
                    pe.wait_ge(state_loaded[h % 2].sem, state_loaded[h % 2].after(layer, h // 2 + 1))
                    if h:
                        pe.wait_ge(ret_act.sem, ret_act.after(layer, h))
                        pe.wait_ge(ret_dve.sem, ret_dve.after(layer, h))
                    cols = slice(h * D_R, (h + 1) * D_R)
                    pe.matmul(ps[:, 1, 0:P], vr_tok[:, 0, cols], inner[:, 0:P], start=True, stop=True)
                    pe.matmul(ps[:, 1, P:SEQ], vr_tok[:, 0, cols], inner[:, P:SEQ], start=True, stop=False)
                    pe.matmul(ps[:, 1, P:SEQ], vr_tok[:, 1, cols], inner[:, SEQ:384], start=False, stop=True)
                    pe.matmul(ps[:, 1, SEQ:T], vr_tok[0:TS, 2, cols], inner_s, start=True, stop=True, skip_group_check=True)
                    for b in range(DEC_BATCH):
                        pe.matmul(ps[:, 1, SEQ + 4 * b:SEQ + 4 * b + 4], state[:, h % 2, b, :], q_dec[:, 4 * b:4 * b + 4],
                                  start=False, stop=True, skip_group_check=True)
                    for t in range(2):
                        pe.matmul(ps[:, 2, 0:P], kd_tok[:, t, cols], vr_tok[:, t, cols], start=t == 0, stop=t == 1)
                    for n in range(2):
                        last = pe.matmul(ps[:, 3 + n, :], kd_tok[0:TS, 2, cols], v_masked[:, 4 * n:4 * n + 4, :], start=True, stop=True)
                    last.then_inc(ret_out.sem, 1)
                pe.wait_ge(ret_act.sem, ret_act.after(layer, H_R))
                pe.wait_ge(ret_dve.sem, ret_dve.after(layer, H_R))
                for h in range(H_R):
                    last = pe.matmul(ps[:, 4 + h, 0:T], ones, orT[:, h, :], start=True, stop=True)
                last.then_inc(gn_mean.sem, 1)
                pe.wait_ge(gn_sq.sem, gn_sq.after(layer, 1))
                for h in range(H_R):
                    last = pe.matmul(ps[:, 4 + h, 0:T], ones, squares_r[:, h, :], start=True, stop=True)
                last.then_inc(gn_var.sem, 1)

                for hb in range(2):
                    if hb:
                        pe.wait_ge(pp_read.sem, pp_read.after(layer, hb))
                    for i in range(4):
                        h = 4 * hb + i
                        rows = slice(64 * (h % 2), 64 * (h % 2) + 64)
                        q, k = z[rows, ZQ + h // 2, :], z[rows, ZK + h // 2, :]
                        pe.matmul(ps[:, i, 0:P], q[:, 0:P], k[:, 0:P], start=True, stop=True)
                        last = pe.matmul(ps[:, i, P:384], q[:, P:SEQ], k[:, 0:SEQ], start=True, stop=True)
                    last.then_inc(pp_scores.sem, 1)
                    pe.wait_ge(pp_norm.sem, pp_norm.after(layer, hb + 1))
                    if hb == 0:
                        pe.wait_ge(gn_ln.sem, gn_ln.after(layer, 1))
                    for i in range(4):
                        for t in range(3):
                            last = pe.transpose(ps[:, 4 + i, t * P:(t + 1) * P], prob_p[:, i, t * P:(t + 1) * P], ident)
                    last.then_inc(pp_tr.sem, 1)
                    pe.wait_ge(pp_tr_act.sem, pp_tr_act.after(layer, hb + 1))
                    pe.wait_ge(pp_tr_dve.sem, pp_tr_dve.after(layer, hb + 1))
                    for i in range(4):
                        h = 4 * hb + i
                        out = ps[64 * (i % 2):64 * (i % 2) + 64, i // 2, 0:SEQ]
                        cols = slice(h * D_A, (h + 1) * D_A)
                        pe.matmul(out[:, 0:P], v_tok[:, 0, cols], probT_p[:, i, 0:P], start=True, stop=True)
                        pe.matmul(out[:, P:SEQ], v_tok[:, 0, cols], probT_p[:, i, P:SEQ], start=True, stop=False)
                        last = pe.matmul(out[:, P:SEQ], v_tok[:, 1, cols], probT_p[:, i, SEQ:384], start=False, stop=True)
                    last.then_inc(pp_out.sem, 1)

                pe.wait_ge(q_blocks_done.sem, q_blocks_done.after(layer, 1))
                pe.wait_ge(pp_read.sem, pp_read.after(layer, 2))
                for g in range(2):
                    for c in range(4):
                        for j in range(4):
                            last = pe.matmul(ps[32 * j:32 * j + 32, 6, g * TS:(g + 1) * TS], q_blocks[:, 4 * g + j, c, :],
                                             z[:, ZK + c, SEQ:T], start=c == 0, stop=c == 3)
                last.then_inc(new_scores.sem, 1)
                for g in range(2):
                    with pe.Fori(0, N_PAGES // 2) as i:
                        for s in range(2):
                            pe.wait_ge(kv_loaded[s].sem, (layer * 16 + i + (4 * g + 1)) * 64)
                            for half in range(2):
                                free = (kt_act, kt_dve)[half]
                                pe.wait_ge(free.sem, free.after(layer, 8 * g + s) + i * 2)
                                for j in range(2 * half, 2 * half + 2):
                                    for c in range(4):
                                        last = pe.transpose(ps[:, j, c * P:(c + 1) * P], kv[:, s, j, c * P:(c + 1) * P], ident)
                                last.then_inc(kv_used.sem, 1)
                        for s in range(2):
                            pe.wait_ge(kt_act.sem, kt_act.after(layer, 8 * g + s + 1) + i * 2)
                            pe.wait_ge(kt_dve.sem, kt_dve.after(layer, 8 * g + s + 1) + i * 2)
                            pe.wait_ge(sc_read.sem, sc_read.after(layer, 8 * g + s - 1) + i * 2)
                            for c in range(4):
                                for j in range(4):
                                    last = pe.matmul(ps[32 * j:32 * j + 32, 4 + s, 0:P], q_blocks[:, 4 * g + j, c, :],
                                                     kT[:, s, j, c * P:(c + 1) * P], start=c == 0, stop=c == 3)
                            last.then_inc(sc_done.sem, 1)
                for g in range(2):
                    pe.wait_ge(sm_norm.sem, sm_norm.after(layer, g + 1))
                    for n in range(N_PAGES):
                        pe.transpose(ps[:, 2 * g + n // 4, (n % 4) * P:(n % 4 + 1) * P], S[:, g, n * P:(n + 1) * P], ident)
                    pe.transpose(ps[0:TS, 6 - 2 * g, 0:P], S[:, g, PAST:PAST + TS], ident).then_inc(sm_tr.sem, 1)
                pe.wait_ge(sm_tr_act.sem, sm_tr_act.after(layer, 2))
                pe.wait_ge(sm_tr_dve.sem, sm_tr_dve.after(layer, 2))

                def pv(g, j, c, v, p, start=False):
                    at = ((4 * g + j) * 4 + c) * 8
                    return pe.matmul(ps[:, 7, at:at + 8], v, p, start=start, stop=True, skip_group_check=True)

                for g in range(2):
                    for j in range(4):
                        for c in range(4):
                            r = 32 * j + 8 * c
                            pv(g, j, c, v_tok[0:TS, 2, c * P:(c + 1) * P], probT_new[:, g, r:r + 8], start=g + j + c == 0)
                for g in range(2):
                    with pe.Fori(0, N_PAGES // 2) as i:
                        for s in range(2):
                            pe.wait_ge(kv_loaded[s].sem, (layer * 16 + i + (8 + 4 * g + 1)) * 64)
                            for j in range(4):
                                for c in range(4):
                                    r = 32 * j + 8 * c
                                    last = pv(g, j, c, kv[:, s, j, c * P:(c + 1) * P],
                                              probT[:, g, ds(i * 2 + s, 1), r:r + 8].rearrange("p a r -> p (a r)"))
                                if j % 2:
                                    last.then_inc(kv_used.sem, 1)

                with pe.Fori(0, DP) as i:
                    for n in range(2):
                        pe.wait_ge(gate_done.sem, gate_done.after(layer, n - 1) + i * 2)
                        slab(i * 2 + GATE // 2, n, 2 * n, h_hi, h_lo, 0, KC)
                    pe.wait_ge(oa_lo_done.sem, oa_lo_done.after(layer, 1))
                    slab(i * 2 + (GATE // 2 + 1), 0, 4, oa_hi, oa_lo, 0, 4)
                    pe.wait_ge(or_lo_done.sem, or_lo_done.after(layer, 1))
                    slab(i * 2 + (GATE // 2 + 1), 1, 6, or_hi, or_lo, 0, 4)
                with pe.Fori(0, DP // 2) as i:
                    for s in range(2):
                        pe.wait_ge(mg_done.sem, mg_done.after(layer, DP))
                        pe.wait_ge(x_done.sem, x_done.after(layer, DP + s - 1) + i * 2)
                        slab(i + WO // 2, s, 2 * s, mg_hi, mg_lo, 0, KC)
                ffn(1, 2, UP2, DOWN2)

            pe.wait_ge(x_done.sem, x_done.after(DEPTH - 1, 3 * DP))
            for t in range(3):
                rows = P if t < 2 else TS
                for c in range(KC):
                    last = pe.transpose(ps[0:rows, 2 * t + c // 4, (c % 4) * P:(c % 4 + 1) * P], xT[:, c, t * P:t * P + rows], ident)
            last.then_inc(last_tr.sem, 1)

        @block.vector
        def _(dve):
            dve.sem_inc(split_done.sem, 2)
            dve.sem_inc(slab_used.sem, 2)
            dve.sem_inc(up_read.sem, 2)
            dve.sem_inc(kv_used.sem, 4)
            dve.sem_inc(kt_act.sem, 1)
            dve.sem_inc(kt_dve.sem, 1)
            dve.sem_inc(sc_done.sem, 2)
            dve.sem_inc(sc_read.sem, 2)
            dve.sem_inc(gate_done.sem, 2)
            dve.sem_inc(merged.sem, 1)
            dve.memset(q_blocks[:, :, :, :], 0.0).then_inc(zeroed.sem, 1)
            dve.memset(small[:, :, :], 0.0).then_inc(zeroed.sem, 1)
            dve.wait_ge(zeroed.sem, 2)
            dve.wait_ge(first_tr.sem, 1)
            dve.tensor_copy(gains[:, :], ps[:, 0, 300:300 + DEPTH * GL]).then_inc(gains_done.sem, 1)
            for c in range(0, KC, 2):
                dve.tensor_copy(xT[:, c:c + 2, :], ps[:, c:c + 2, 0:T]).then_inc(x_done.sem, 1)
            dve.wait_ge(gains_done.sem, 1)

            with dve.Fori(0, DEPTH) as layer:
                links = [0]

                def link(ins):
                    links[0] += 1
                    ins.then_inc(dve_link.sem, 1)
                    dve.wait_ge(dve_link.sem, dve_link.after(layer, links[0]))

                def lo(pair, slot, chunks=KC):
                    dve.wait_ge(hi_done.sem, hi_done.after(layer, 2 * pair + slot + 1))
                    n = chunks * CW
                    dve.tensor_tensor(w_lo[:, slot, 0:n], raw[:, slot, 0:n], w_hi[:, slot, 0:n].bitcast(F32), ALU.subtract)\
                       .then_inc(split_done.sem, 1)

                def lo_slab(n, chunks=KC):
                    lo(n // 2, n % 2, chunks)

                def x_add(i, slab_n, bank, factor):
                    dve.wait_ge(slab_used.sem, slab_used.after(layer, slab_n + 1))
                    dve.scalar_tensor_tensor(xT[:, 2 * i:2 * i + 2, :], ps[:, bank:bank + 2, 0:T], factor,
                                             xT[:, 2 * i:2 * i + 2, :], ALU.mult, ALU.add).then_inc(x_done.sem, 1)

                def rms(r, g0):
                    dve.wait_ge(rms_rstd.sem, rms_rstd.after(layer, r + 1))
                    for c in range(KC):
                        last = dve.scalar_tensor_tensor(squares[:, c, :], xT[:, c, :], gain[:, g0 + c:g0 + c + 1], rstd[:, :],
                                                        ALU.mult, ALU.mult)
                        if c % 2:
                            last.then_inc(rms_h.sem, 1)
                    for c in range(0, KC, 2):
                        dve.wait_ge(h_hi_done.sem, h_hi_done.after(layer, 4 * r + c // 2 + 1))
                        dve.tensor_tensor(h_lo[:, c:c + 2, :], squares[:, c:c + 2, :], h_hi[:, c:c + 2, :].bitcast(F32), ALU.subtract)\
                           .then_inc(h_done.sem, 1)

                def up_product(f, i, slabs, buf):
                    dve.wait_ge(silu_done.sem, silu_done.after(layer, f * UP_PAIRS + 1) + i)
                    dve.wait_ge(slab_used.sem, slab_used.after(layer, slabs + 2) + i * 2)
                    dve.tensor_tensor(hid_f[:, buf], silu[:, buf], ps[:, 4 * buf + 2:4 * buf + 4, 0:T], ALU.mult).then_inc(up_read.sem, 1)
                    dve.wait_ge(hid_hi_done.sem, hid_hi_done.after(layer, f * UP_PAIRS + 1) + i)
                    at = ds(i * 2, 2)
                    dve.tensor_tensor(hid_lo[:, at, :], hid_f[:, buf], hid_hi[:, at, :].bitcast(F32), ALU.subtract).then_inc(hid_done.sem, 1)

                def ffn(f, r, g0, first_up, first_down):
                    lo_slab(first_up)
                    lo_slab(first_up + 1)
                    rms(r, g0)
                    with dve.Fori(0, UP_PAIRS // 2) as t:
                        for b in range(2):
                            i = t * 2 + b
                            lo(i + (first_up // 2 + 1), 0)
                            lo(i + (first_up // 2 + 1), 1)
                            up_product(f, i, first_up, b)
                    lo_slab(first_down, 8)
                    lo_slab(first_down + 1, 7)
                    up_product(f, UP_PAIRS - 1, first_up, 0)
                    lo_slab(first_down + 2, 7)
                    for i in range(1, DP):
                        lo_slab(first_down + 3 * i, 8)
                        lo_slab(first_down + 3 * i + 1, 7)
                        x_add(i - 1, first_down + 3 * i - 1, 4 + 2 * ((i - 1) % 2), 0.5)
                        lo_slab(first_down + 3 * i + 2, 7)
                    x_add(DP - 1, first_down + 3 * DP - 1, 4 + 2 * ((DP - 1) % 2), 0.5)

                dve.tensor_copy(gain[:, :], gains[:, ds(layer * GL, GL)]).then_inc(gain_done.sem, 1)
                dve.wait_ge(gain_done.sem, layer + 1)
                ffn(0, 0, G_FFN1, UP1, DOWN1)

                lo_slab(ZIN)
                lo_slab(ZIN + 1)
                rms(1, G_MIX)
                with dve.Fori(1, 7) as i:
                    for s in range(2):
                        lo(i + ZIN // 2, s)

                for n, (zc, g) in enumerate(((ZQ, G_Q), (ZK, G_K))):
                    dve.wait_ge(qk_rstd.sem, qk_rstd.after(layer, n + 1))
                    dve.scalar_tensor_tensor(z[:, zc:zc + 4, :], z[:, zc:zc + 4, :], gain[:, g:g + 1], squares[:, 4 * n:4 * n + 4, :],
                                             ALU.mult, ALU.mult).then_inc(qk_done.sem, 1)
                dve.wait_ge(qk_done.sem, qk_done.after(layer, 2))
                for c in range(4):
                    for half in range(2):
                        rows, col = slice(64 * half, 64 * half + 64), 8 * c + 4 * half
                        last = dve.tensor_copy(q_blocks[rows, :, c, col:col + 4],
                                               z[rows, ZQ + c, SEQ:T].rearrange("p (b q) -> p b q", b=8))
                last.then_inc(q_blocks_done.sem, 1)

                dve.wait_ge(tr_done.sem, tr_done.after(layer, 3))
                kdecay = cst("kdecay").rearrange("p (t h) -> p t h", t=3)
                for t in range(3):
                    rows = P if t < 2 else TS
                    last = dve.tensor_tensor(kd_tok[0:rows, t, :].rearrange("p (h d) -> p h d", h=H_R),
                                             ps[0:rows, 4 + t, :].rearrange("p (h d) -> p h d", h=H_R),
                                             kdecay[0:rows, t, :].unsqueeze(2).to_broadcast([rows, H_R, D_R]), ALU.mult)
                last.then_inc(tok_dve.sem, 1)

                dve.wait_ge(tok_act.sem, tok_act.after(layer, 2))
                for h in range(H_R):
                    dve.wait_ge(inner_done.sem, inner_done.after(layer, h + 1))
                    if h:
                        dve.wait_ge(ret_out.sem, ret_out.after(layer, h))
                    dve.tensor_tensor(inner, ps[:, 0, 0:384], cst("decay", h * 384, (h + 1) * 384), ALU.mult)
                    dve.tensor_tensor(inner_s, ps[0:TS, 0, 384:384 + TS], cst("sdecay", h * TS, (h + 1) * TS)[0:TS, :], ALU.mult)
                    dve.tensor_tensor(q_dec, z[:, ZQR + h, SEQ:T], cst("qdecay", h * TS, (h + 1) * TS), ALU.mult)
                    dve.tensor_tensor(v_masked, vr_tok[0:TS, 2:3, h * D_R:(h + 1) * D_R].to_broadcast([TS, DEC_BATCH, D_R]),
                                      cst("batch")[0:TS, :].unsqueeze(2).to_broadcast([TS, DEC_BATCH, D_R]), ALU.mult).then_inc(ret_in.sem, 1)
                    dve.wait_ge(ret_out.sem, ret_out.after(layer, h + 1))
                    st = state[:, h % 2].rearrange("p b e -> p (b e)").rearrange("p (n m) -> p n m", n=2)
                    dve.scalar_tensor_tensor(st, st, math.exp(log_decay(h) * DEC_SEQ), ps[:, 3:5, :], ALU.mult, ALU.add)\
                       .then_inc(ret_dve.sem, 1)
                dve.wait_ge(gn_mean.sem, gn_mean.after(layer, 1))
                dve.scalar_tensor_tensor(orT, ps[:, 4:8, 0:T], -1.0 / D_R, orT, ALU.mult, ALU.add).then_inc(gn_cen.sem, 1)
                dve.wait_ge(gn_cen.sem, gn_cen.after(layer, 1))
                dve.wait_ge(gn_rstd.sem, gn_rstd.after(layer, 1))
                link(dve.tensor_tensor(orT, orT, squares_r, ALU.mult))
                for h in range(H_R):
                    last = dve.tensor_scalar(orT[:, h, :], orT[:, h, :], gain[:, G_GN + h:G_GN + h + 1], gain[:, G_GB + h:G_GB + h + 1],
                                             ALU.mult, ALU.add)
                link(last)
                dve.wait_ge(gr_silu.sem, gr_silu.after(layer, 1))
                dve.tensor_tensor(orT, orT, z[:, ZGR:ZGR + 4, :], ALU.mult).then_inc(or_done.sem, 1)
                dve.wait_ge(or_hi_done.sem, or_hi_done.after(layer, 1))
                dve.tensor_tensor(or_lo[:, :, :], orT, or_hi[:, :, :].bitcast(F32), ALU.subtract).then_inc(or_lo_done.sem, 1)

                for hb in range(2):
                    dve.wait_ge(pp_scores.sem, pp_scores.after(layer, hb + 1))
                    for i in range(4):
                        last = dve.scalar_tensor_tensor(prob_p[:, i, :], cst("causal"), 8.0 * slope(4 * hb + i), ps[:, i, 0:384],
                                                        ALU.mult, ALU.add)
                    link(last)
                    dve.tensor_reduce(mx[:, 0:4], prob_p[:, :, 0:P], AX, ALU.max)
                    link(dve.tensor_reduce(mx[:, 4:8], prob_p[:, :, P:384], AX, ALU.max))
                    dve.tensor_scalar(mx[:, 0:8], mx[:, 0:8], -SCALE_A, None, ALU.mult).then_inc(pp_max.sem, 1)
                    dve.wait_ge(pp_exp.sem, pp_exp.after(layer, hb + 1))
                    link(dve.reciprocal(mx[:, 8:16], small[:, 0, 0:8]))
                    dve.tensor_tensor(prob_p[:, :, 0:P], prob_p[:, :, 0:P], mx[:, 8:12].unsqueeze(2).to_broadcast([P, 4, P]), ALU.mult)
                    dve.tensor_tensor(prob_p[:, :, P:384], prob_p[:, :, P:384], mx[:, 12:16].unsqueeze(2).to_broadcast([P, 4, 2 * P]), ALU.mult)\
                       .then_inc(pp_norm.sem, 1)
                    dve.wait_ge(pp_tr.sem, pp_tr.after(layer, hb + 1))
                    dve.wait_ge(state_p_stored.sem, state_p_stored.after(layer, 1))
                    dve.tensor_copy(probT_p[:, 2:4, :], ps[:, 6:8, 0:384]).then_inc(pp_tr_dve.sem, 1)

                for s in range(2):
                    dve.wait_ge(state_stored[s].sem, state_stored[s].after(layer, 2))
                dve.wait_ge(new_scores.sem, new_scores.after(layer, 1))
                dve.tensor_tensor(S[:, :, PAST:PAST + TS], ps[:, 6, 0:2 * TS].rearrange("p (g t) -> p g t", g=2),
                                  cst("newb").rearrange("p (g t) -> p g t", g=2), ALU.add).then_inc(new_read.sem, 1)
                page_sum = small[:, :, 24:32]
                for g in range(2):
                    with dve.Fori(0, N_PAGES // 2) as i:
                        for s in range(2):
                            dve.wait_ge(kv_used.sem, kv_used.after(layer, 16 * g + 2 * s + 2) + i * 4)
                            dve.wait_ge(sc_done.sem, sc_done.after(layer, 8 * g + s - 1) + i * 2)
                            dve.tensor_copy(kT[:, s, 2:4, :], ps[:, 2:4, :]).then_inc(kt_dve.sem, 1)
                        for s in range(2):
                            dve.wait_ge(sc_done.sem, sc_done.after(layer, 8 * g + s + 1) + i * 2)
                            cols = ds(i * 256 + s * P, P)
                            at = C_AT["pastb"][0]
                            dve.tensor_tensor(S[:, g, cols], ps[:, 4 + s, 0:P], const[:, ds(i * 256 + (at + s * P), P)], ALU.add)
                            dve.tensor_reduce(page_sum[:, g, ds(i * 2 + s, 1)], ps[:, 4 + s, 0:P], AX, ALU.add).then_inc(sc_read.sem, 1)
                dve.wait_ge(new_read.sem, new_read.after(layer, 1))
                dve.wait_ge(sc_read.sem, sc_read.after(layer, 16))
                for g in range(2):
                    sg = small[:, g]
                    gate4, least, score, drop, bmax = sg[:, 32:36], sg[:, 36:37], sg[:, 40:44], sg[:, 48:53], sg[:, 56:61]
                    link(dve.tensor_reduce(gate4, page_sum[:, g, :].rearrange("p (b n) -> p b n", n=2), AX, ALU.add))
                    link(dve.tensor_reduce(least, gate4, AX, ALU.min))
                    link(dve.scalar_tensor_tensor(score, gate4, least, cst("rank"), ALU.is_equal, ALU.mult))
                    link(dve.tensor_reduce(sg[:, 37:38], score, AX, ALU.max))
                    dve.tensor_scalar(drop[:, 0:4], score, sg[:, 37:38], NEG, ALU.is_equal, ALU.mult)
                    dve.tensor_reduce(bmax[:, 0:4], S[:, g, 0:PAST].rearrange("p (b n) -> p b n", b=4), AX, ALU.max)
                    link(dve.tensor_reduce(bmax[:, 4:5], S[:, g, PAST:PAST + TS], AX, ALU.max))
                    link(dve.tensor_tensor(bmax[:, 0:4], bmax[:, 0:4], drop[:, 0:4], ALU.add))
                    link(dve.tensor_reduce(sg[:, 38:39], bmax, AX, ALU.max))
                    link(dve.tensor_scalar(sg[:, 39:40], sg[:, 38:39], -SCALE_A, None, ALU.mult))
                    dve.tensor_scalar(sg[:, 8:13], drop, sg[:, 39:40], None, ALU.add).then_inc(sm_bias.sem, 1)
                for g in range(2):
                    sg = small[:, g]
                    dve.wait_ge(sm_exp.sem, sm_exp.after(layer, g + 1))
                    link(dve.tensor_reduce(sg[:, 22:23], sg[:, 16:21], AX, ALU.add))
                    link(dve.reciprocal(sg[:, 23:24], sg[:, 22:23]))
                    dve.tensor_scalar(S[:, g, :], S[:, g, :], sg[:, 23:24], None, ALU.mult).then_inc(sm_norm.sem, 1)
                for g in range(2):
                    dve.wait_ge(sm_tr.sem, sm_tr.after(layer, g + 1))
                    dve.tensor_copy(probT_new[:, g, :], ps[0:TS, 6 - 2 * g, 0:P]).then_inc(sm_tr_dve.sem, 1)
                dve.wait_ge(oa_hi_done.sem, oa_hi_done.after(layer, 1))
                dve.tensor_tensor(oa_lo[:, :, :], oT, oa_hi[:, :, :].bitcast(F32), ALU.subtract).then_inc(oa_lo_done.sem, 1)

                def merge(i):
                    dve.wait_ge(slab_used.sem, slab_used.after(layer, GATE + 4) + i * 4)
                    dve.wait_ge(gate_done.sem, gate_done.after(layer, 2) + i * 2)
                    for n in range(2):
                        last = dve.tensor_tensor(hid_f[:, n], silu[:, n], ps[:, 4 + 2 * n:6 + 2 * n, 0:T], ALU.mult)
                    last.then_inc(merge_t.sem, 1)
                    dve.wait_ge(merge_t.sem, merge_t.after(layer, 1) + i)
                    dve.tensor_tensor(hid_f[:, 0], hid_f[:, 0], hid_f[:, 1], ALU.add).then_inc(merged.sem, 1)

                def merge_lo(i):
                    dve.wait_ge(mg_hi_done.sem, mg_hi_done.after(layer, 1) + i)
                    at = ds(i * 2, 2)
                    dve.tensor_tensor(mg_lo[:, at, :], hid_f[:, 0], mg_hi[:, at, :].bitcast(F32), ALU.subtract).then_inc(mg_done.sem, 1)

                def gate_step(i, first):
                    g2 = i * 2 + GATE // 2
                    lo(g2, 0)
                    lo(g2, 1)
                    if not first:
                        merge(i - 1)
                    lo(g2 + 1, 0, 4)
                    if not first:
                        merge_lo(i - 1)
                    lo(g2 + 1, 1, 4)

                gate_step(0, True)
                with dve.Fori(1, DP) as i:
                    gate_step(i, False)
                lo_slab(WO)
                lo_slab(WO + 1)
                merge(DP - 1)
                merge_lo(DP - 1)
                for i in range(DP):
                    if i < 2:
                        lo_slab(WO + 2 + i)
                    x_add(i, WO + i, 2 * (i % 2), 1.0)
                ffn(1, 2, G_FFN2, UP2, DOWN2)
                assert links[0] == LINKS, links

            dve.wait_ge(last_tr.sem, 1)
            for t in range(3):
                rows = P if t < 2 else TS
                dve.tensor_copy(stage[0:rows, t, 512:1024], ps[0:rows, 2 * t + 1, :]).then_inc(last_dve.sem, 1)


N_LOADS = 3 + 5 * DEPTH + 4 * DEPTH


_INS = ["x_prompt", "x_sample", "cache_k", "cache_v", "state_ret", "page_table", "g_ffn1", "w1_ffn1", "w3_ffn1", "w2_ffn1",
        "g_mix", "w_in", "g_q", "g_k", "gn_gain", "gn_bias", "w_pa", "w_pr", "w_o", "g_ffn2", "w1_ffn2", "w3_ffn2", "w2_ffn2"]
_OUTS = [(1, SEQ, D_MODEL), (DEC_BATCH, DEC_SEQ, D_MODEL), (DEPTH, 1, SEQ, H_A, D_A), (DEPTH, 1, SEQ, H_A, D_A),
         (DEPTH, 1, H_R, D_R, D_R), (DEPTH, DEC_BATCH, DEC_SEQ, H_A, D_A), (DEPTH, DEC_BATCH, DEC_SEQ, H_A, D_A),
         (DEPTH, DEC_BATCH, H_R, D_R, D_R)]


def kernel(**inputs):
    import concourse.bacc as bacc
    from concourse.bass_utils import run_bass_kernel_spmd

    nc = bacc.Bacc("TRN2", target_bir_lowering=False, num_devices=1)
    arrays = {f"in_{n}": np.ascontiguousarray(inputs[n]) for n in _INS}
    arrays["consts"] = constants()
    args = [nc.dram_tensor(n, a.shape, mybir.dt.from_np(a.dtype), kind="ExternalInput").ap() for n, a in arrays.items()]
    outs = [nc.dram_tensor(f"out_{i}", s, F32, kind="ExternalOutput").ap() for i, s in enumerate(_OUTS)]
    trunk(nc, *args, *outs)
    r = run_bass_kernel_spmd(nc, [arrays], core_ids=[0])
    return tuple(r.results[0][f"out_{i}"] for i in range(len(_OUTS)))
```

```python
from contextlib import ExitStack
import math

import numpy as np
import concourse.bass as bass
from concourse import mybir

F32 = mybir.dt.float32
F32R = mybir.dt.float32r
I32 = mybir.dt.int32
ALU = mybir.AluOpType
ACT = mybir.ActivationFunctionType
AX = mybir.AxisListType.X
ds = bass.ds

P = 128
D_MODEL, D_FF, DEPTH = 1024, 2816, 2
SEQ, DEC_BATCH, DEC_SEQ = 256, 8, 4
TS = DEC_BATCH * DEC_SEQ
T = SEQ + TS
PAST, PAGE, N_POOL = 1024, 128, 80
N_PAGES = PAST // PAGE
H_A, D_A = 8, 64
H_R, D_R = 4, 128
EPS = 1e-6
NEG = -1e30
SCALE_A = D_A ** -0.5

KC = D_MODEL // P
FC = D_FF // P
CW = 2 * P
SLAB = KC * CW
UP_PAIRS = D_FF // CW
DP = D_MODEL // CW
F_PARTS = ((0, 8), (8, 15), (15, 22))

UP1 = 0
DOWN1 = UP1 + 2 * UP_PAIRS
ZIN = DOWN1 + 3 * DP
Z_SLABS = 22
GR1 = Z_SLABS - 2
PROJ = ZIN + Z_SLABS
WO = PROJ + 2 * DP
UP2 = WO + DP
DOWN2 = UP2 + 2 * UP_PAIRS
SLABS = DOWN2 + 3 * DP
assert SLABS % 2 == 0

ZQ, ZK, ZV, ZQR, ZKR, ZVR, TOK, ZGR, ZGA, ZN = 0, 4, 8, 12, 16, 20, 24, 40, 44, 52


def z_place(m):
    return 2 * m if m < 12 else 2 * m + (ZGR - 24) if m < 18 else ZV + 2 * (m - 18) if m < 20 else ZVR + 2 * (m - 20)


C_SHAPES = (("ident", 128), ("ones", 128), ("heads", 128), ("causal", 384), ("pastb", P), ("pageb", N_PAGES), ("newb", 2 * TS),
            ("decay", H_R * SEQ), ("kdecay", 3 * H_R), ("qdecay", H_R * TS), ("batch", DEC_BATCH),
            ("rank", 4), ("sdecay", H_R * TS))
C_AT, _at = {}, 0
for _name, _n in C_SHAPES:
    C_AT[_name] = (_at, _n)
    _at += _n
C_N = _at
GL = 3 * KC + 2 * H_R + 2
G_FFN1, G_MIX, G_FFN2, G_GN, G_GB, G_Q, G_K = 0, 8, 16, 24, 28, 32, 33


def slope(h):
    return 2.0 ** (-8.0 * (h + 1.0) / H_A)


def log_decay(h):
    return math.log(1.0 - 2.0 ** (-5.0 - h))


def constants():
    c = {n: np.zeros((P, w), np.float64) for n, w in C_SHAPES}
    r = np.arange(P)
    c["ident"][:] = np.eye(P)
    c["ones"][:] = 1.0
    c["heads"][:] = (r[:, None] // D_A) == (r[None, :] // D_A)
    d = r[None, :] - r[:, None]
    c["causal"][:, 0:P] = np.where(d <= 0, d, -1e32)
    d = np.arange(SEQ)[None, :] - (r[:, None] + P)
    c["causal"][:, P:] = np.where(d <= 0, d, -1e32)
    q, h, jb = r % 4, (r // 4) % H_A, r // 32
    s8 = np.array([8.0 * slope(x) for x in h])
    c["pastb"][:] = s8[:, None] * (r[None, :] - q[:, None])
    c["pageb"][:] = s8[:, None] * (P * np.arange(N_PAGES)[None, :] - PAST)
    for g in range(2):
        for t in range(TS):
            ok = (t // 4 == 4 * g + jb) & (t % 4 <= q)
            c["newb"][:, g * TS + t] = np.where(ok, s8 * (t % 4 - q), NEG)
    ks = D_R ** -0.5
    for hh in range(H_R):
        lg = log_decay(hh)
        d = np.arange(SEQ)[None, :] - r[:, None]
        m = np.where(d >= 0, np.exp(lg * np.maximum(d, 0)), 0.0) * ks
        c["decay"][:, hh * SEQ:(hh + 1) * SEQ] = m
        for t in range(2):
            c["kdecay"][:, t * H_R + hh] = np.exp(lg * (SEQ - 1.0 - (t * P + r))) * ks
        c["kdecay"][:, 2 * H_R + hh] = np.exp(lg * (DEC_SEQ - 1.0 - r % 4)) * ks
        i = np.arange(TS)
        c["qdecay"][:, hh * TS:(hh + 1) * TS] = np.exp(lg * (i % 4 + 1.0))[None, :]
        ok = (r[:, None] // 4 == i[None, :] // 4) & (i[None, :] % 4 >= r[:, None] % 4)
        c["sdecay"][:, hh * TS:(hh + 1) * TS] = np.where(ok, np.exp(lg * np.maximum(i[None, :] % 4 - r[:, None] % 4, 0)), 0) * ks
    c["batch"][:] = (r[:, None] // 4) == np.arange(DEC_BATCH)[None, :]
    c["rank"][:] = np.arange(1, 5)[None, :]
    return np.concatenate([c[n] for n, _ in C_SHAPES], axis=1).astype(np.float32)


class Signal:

    def __init__(self, sem, per_layer, credit=0, step=1):
        self.sem, self.per_layer, self.credit, self.step = sem, per_layer, credit, step

    def after(self, layer, n):
        return (layer * self.per_layer + (n + self.credit)) * self.step


def trunk(nc, x_prompt, x_sample, cache_k, cache_v, state_ret, page_table, g_ffn1, w1_ffn1, w3_ffn1, w2_ffn1,
          g_mix, w_in, g_q, g_k, gn_gain, gn_bias, w_pa, w_pr, w_o, g_ffn2, w1_ffn2, w3_ffn2, w2_ffn2, consts,
          y_prompt, y_sample, k_prompt, v_prompt, state_prompt, k_sample, v_sample, state_sample):
    ctx = ExitStack()
    with ctx:
        def sb(name, shape, dt=F32):
            return ctx.enter_context(nc.sbuf_tensor(name, shape, dt))

        def signal(name, per_layer=1, credit=0, step=1):
            return Signal(ctx.enter_context(nc.semaphore(name)), per_layer, credit, step)

        xT = sb("xT", [P, KC, T])
        h_hi = sb("h_hi", [P, KC, T], F32R)
        h_lo = sb("h_lo", [P, KC, T], F32R)
        raw = sb("raw", [P, 2, SLAB])
        w_hi = sb("w_hi", [P, 2, SLAB], F32R)
        w_lo = sb("w_lo", [P, 2, SLAB], F32R)
        const = sb("const", [P, C_N])
        gains = sb("gains", [P, DEPTH * GL])
        gain = sb("gain", [P, GL])
        gain_rows = sb("gain_rows", [DEPTH * GL, P])
        pages = sb("pages", [1, DEC_BATCH * N_PAGES], I32)
        pair_buf = sb("pair_buf", [P, 2, 2, 2, T])
        silu, hid_f = pair_buf[:, 0], pair_buf[:, 1]
        rstd = sb("rstd", [P, T])
        kv = sb("kv", [P, 2, 4, H_A * D_A])
        q_blocks = sb("q_blocks", [P, DEC_BATCH, 4, 32])
        mx = sb("mx", [P, 16])
        small = sb("small", [P, 2, 64])
        attn_s = sb("attn_s", [P, 2 * (PAST + TS)])
        work = sb("work", [P, 2, 2048])
        o_all = sb("o_all", [P, 2, 4, T])
        arena = sb("arena", [P, ZN, T], F32R)
        hid_hi, hid_lo = arena[:, 0:FC], arena[:, FC:2 * FC]
        base = nc.sbuf_base - ZN * T * 4
        chunk = 4 * T

        def over(name, shape, dt, at):
            return nc.alloc_sbuf_tensor_at(name, shape, dt, offset=base + at)

        z = over("z", [P, ZN, T], F32, 0)
        v_tok = over("v_tok", [P, 3, 512], F32, TOK * chunk)
        kd_tok = over("kd_tok", [P, 3, 512], F32, TOK * chunk + 6144)
        vr_tok = over("vr_tok", [P, 3, 512], F32, TOK * chunk + 12288)
        oa_hi = over("oa_hi", [P, 4, T], F32R, ZQ * chunk)
        oa_lo = over("oa_lo", [P, 4, T], F32R, ZK * chunk)
        or_hi = over("or_hi", [P, 4, T], F32R, ZQR * chunk)
        or_lo = over("or_lo", [P, 4, T], F32R, ZKR * chunk)
        mg_hi = over("mg_hi", [P, KC, T], F32R, TOK * chunk)
        mg_lo = over("mg_lo", [P, KC, T], F32R, (TOK + KC) * chunk)
        stage = over("stage", [P, 3, D_MODEL], F32, 0)

        k_tok = o_all[:, :, :, :].rearrange("p a c t -> p (a c t)")[:, 0:1536].rearrange("p (t n) -> p t n", t=3)
        oT, orT = o_all[:, 0], o_all[:, 1]
        wk = work[:, :, :].rearrange("p a n -> p (a n)")
        squares = wk[:, 0:KC * T].rearrange("p (c t) -> p c t", c=KC)
        pair_flat = pair_buf[:, :, :, :, :].rearrange("p a b c t -> p (a b c t)")
        qk_squares = pair_flat.rearrange("p (c t) -> p c t", c=8)
        squares_r = pair_flat[:, 0:4 * T].rearrange("p (c t) -> p c t", c=4)
        state_p = pair_flat[:, 4 * T:4 * T + 512].rearrange("p (h e) -> p h e", h=H_R)
        S = attn_s[:, :].rearrange("p (g k) -> p g k", g=2)
        state = attn_s[:, 0:2048].rearrange("p (a b e) -> p a b e", a=2, b=8)
        kT = work[:, :, :].rearrange("p s (j n) -> p s j n", j=4)
        probT = wk[:, 0:2048].rearrange("p (g n r) -> p g n r", g=2, n=N_PAGES)
        probT_new = wk[0:TS, 2048:2304].rearrange("p (g r) -> p g r", g=2)
        v_masked = wk[0:TS, 2304:3328].rearrange("p (b e) -> p b e", b=8)
        inner = wk[:, 3328:3712]
        inner_s = wk[0:TS, 3712:3744]
        q_dec = wk[:, 3744:3776]
        prob_p = [v.rearrange("p (h k) -> p h k", h=4) for v in (wk[:, 0:1536], pair_flat[:, 0:1536])]
        probT_p = wk[:, 1536:3072].rearrange("p (h k) -> p h k", h=4)
        o_sample = oT[:, 0:2, 0:256]

        def cst(name, lo=0, hi=None):
            at, n = C_AT[name]
            return const[:, at + lo:at + (n if hi is None else hi)]

        ident, ones, heads = cst("ident"), cst("ones"), cst("heads")
        ps = ctx.enter_context(nc.psum_tensor("ps", [P, 8, 512], F32))

        raw_loaded = [signal(f"raw_loaded{s}", SLABS // 2, 0, 16) for s in range(2)]
        hi_done = signal("hi_done", SLABS)
        split_done = signal("split_done", SLABS, 2)
        slab_used = signal("slab_used", SLABS, 2)
        up_gate = signal("up_gate", 2 * UP_PAIRS)
        silu_done = signal("silu_done", 2 * UP_PAIRS)
        up_read = signal("up_read", 2 * UP_PAIRS, 2)
        up_prod = signal("up_prod", 2 * UP_PAIRS)
        hid_hi_done = signal("hid_hi_done", 2 * UP_PAIRS)
        hid_done = signal("hid_done", 2 * UP_PAIRS)
        x_done = signal("x_done", 3 * DP, 4)
        rms_sq = signal("rms_sq", 12)
        rms_acc = signal("rms_acc", 3)
        rms_sum = signal("rms_sum", 3)
        rms_ln = signal("rms_ln", 3)
        rms_rstd = signal("rms_rstd", 3)
        h_hi_done = signal("h_hi_done", 12)
        h_done = signal("h_done", 12)
        gain_done = signal("gain_done")
        z_done = signal("z_done", Z_SLABS)
        qk_sq, qk_sum, qk_ln, qk_rstd, qk_done = (signal(n, 2) for n in ("qk_sq", "qk_sum", "qk_ln", "qk_rstd", "qk_done"))
        q_blocks_done = signal("q_blocks_done")
        tr_done = signal("tr_done", 4)
        tok_act = signal("tok_act", 3)
        tok_dve = signal("tok_dve", 1)
        kv_stored = signal("kv_stored", 4, 0, 16)
        state_loaded = [signal(f"state_loaded{s}", 2, 0, 16) for s in range(2)]
        state_stored = [signal(f"state_stored{s}", 2, 0, 16) for s in range(2)]
        state_p_stored = signal("state_p_stored", 1, 0, 16)
        inner_done = signal("inner_done", H_R)
        ret_in = signal("ret_in", H_R)
        ret_out = signal("ret_out", H_R)
        ret_act = signal("ret_act", H_R)
        ret_dve = signal("ret_dve", H_R)
        gn_mean, gn_cen, gn_sq, gn_var, gn_ln, gn_rstd = (signal(n) for n in ("gn_mean", "gn_cen", "gn_sq", "gn_var", "gn_ln", "gn_rstd"))
        gr_silu, or_done, or_hi_done, or_lo_done = (signal(n) for n in ("gr_silu", "or_done", "or_hi_done", "or_lo_done"))
        pp_scores, pp_max, pp_exp, pp_norm, pp_tr, pp_tr_act, pp_tr_dve, pp_out, pp_read = (
            signal(n, 2) for n in ("pp_scores", "pp_max", "pp_exp", "pp_norm", "pp_tr", "pp_tr_act", "pp_tr_dve", "pp_out", "pp_read"))
        pp_biased = signal("pp_biased", 2)
        new_scores, new_read = signal("new_scores"), signal("new_read")
        kv_loaded = [signal(f"kv_loaded{s}", 16, 0, 64) for s in range(2)]
        kv_used = signal("kv_used", 64, 4)
        kt_act = signal("kt_act", 32, 1)
        kt_dve = signal("kt_dve", 32, 1)
        pv_evac, pv_tr, pv_out = signal("pv_evac", 2), signal("pv_tr", 2), signal("pv_out", 2)
        sc_done = signal("sc_done", 16, 2)
        sc_read = signal("sc_read", 16, 2)
        sm_bias, sm_exp, sm_norm, sm_tr, sm_tr_act, sm_tr_dve = (
            signal(n, 2) for n in ("sm_bias", "sm_exp", "sm_norm", "sm_tr", "sm_tr_act", "sm_tr_dve"))
        oa_hi_done, oa_lo_done = signal("oa_hi_done"), signal("oa_lo_done")
        gates_done = signal("gates_done", 2)
        proj_read = signal("proj_read", DP, 2)
        merged = signal("merged", DP)
        mg_hi_done = signal("mg_hi_done", DP)
        mg_done = signal("mg_done", DP)
        LINKS = 32
        dve_link = signal("dve_link", LINKS)
        pool_passed = signal("pool_passed")
        loaded = signal("loaded", 1, 0, 16)
        pages_loaded = signal("pages_loaded", 1, 0, 16)
        first_tr, gains_done, zeroed = signal("first_tr"), signal("gains_done"), signal("zeroed")
        last_tr, last_act, last_dve, y_stored = signal("last_tr"), signal("last_act"), signal("last_dve"), signal("y_stored", 1, 0, 16)

        def by_chunks(w):
            return w.rearrange("l (k p) f -> l p k f", p=P)

        up = ((by_chunks(w1_ffn1), by_chunks(w3_ffn1)), (by_chunks(w1_ffn2), by_chunks(w3_ffn2)))
        down = (by_chunks(w2_ffn1), by_chunks(w2_ffn2))
        w_in_v, w_pa_v, w_pr_v, w_o_v = (by_chunks(w) for w in (w_in, w_pa, w_pr, w_o))
        k_pages = cache_k.rearrange("l n p h d -> (l n) p (h d)")
        v_pages = cache_v.rearrange("l n p h d -> (l n) p (h d)")

        block = ctx.enter_context(nc.Block())

        @block.sync
        def _(sp):
            def load(layer, pair, slot, src, chunks, col):
                sp.wait_ge(split_done.sem, split_done.after(layer, 0) - 1 + (pair * 2 + slot))
                k0, k1 = chunks
                n = k1 - k0
                dst = raw[:, slot, 0:n * CW].rearrange("p (k f) -> p k f", k=n)
                sp.dma_start(dst, src[ds(layer, 1), :, k0:k1, ds(col, CW)].rearrange("l p k f -> p (l k) f"))\
                    .then_inc(raw_loaded[slot].sem, 16)

            with sp.Fori(0, DEPTH) as layer:
                def up_slabs(f, first):
                    with sp.Fori(0, UP_PAIRS) as i:
                        for s in range(2):
                            load(layer, i + first // 2, s, up[f][s], (0, KC), i * CW)

                def down_slabs(f, first):
                    with sp.Fori(0, DP // 2) as i:
                        for n in range(6):
                            load(layer, i * 3 + (first // 2 + n // 2), n % 2, down[f], F_PARTS[n % 3], i * (2 * CW) + n // 3 * CW)

                up_slabs(0, UP1)
                down_slabs(0, DOWN1)
                with sp.Fori(0, Z_SLABS // 2) as i:
                    for s in range(2):
                        load(layer, i + ZIN // 2, s, w_in_v, (0, KC), i * (2 * CW) + s * CW)

                def proj_slabs(i):
                    load(layer, i + PROJ // 2, 0, w_pr_v, (0, 4), i * CW)
                    load(layer, i + PROJ // 2, 1, w_pa_v, (0, 4), i * CW)

                def load_state(h):
                    src = state_ret[ds(layer, 1), :, h, :, :].rearrange("l b d e -> d (l b) e")
                    sp.dma_start(state[:, h % 2], src).then_inc(state_loaded[h % 2].sem, 16)

                proj_slabs(0)
                sp.wait_ge(sm_tr.sem, sm_tr.after(layer, 2))
                load_state(0)
                load_state(1)
                for h in range(H_R):
                    sp.wait_ge(ret_dve.sem, ret_dve.after(layer, h + 1))
                    sp.dma_start(state_sample[ds(layer, 1), :, h, :, :].rearrange("l b d e -> d (l b) e"),
                                 state[:, h % 2]).then_inc(state_stored[h % 2].sem, 16)
                    if h < 2:
                        sp.wait_ge(state_stored[h].sem, state_stored[h].after(layer, 1))
                        load_state(h + 2)
                sp.wait_ge(ret_act.sem, ret_act.after(layer, H_R))
                sp.dma_start(state_prompt[ds(layer, 1), 0].rearrange("l h d e -> d (l h) e"),
                             state_p).then_inc(state_p_stored.sem, 16)
                for i in range(1, DP):
                    proj_slabs(i)
                with sp.Fori(0, DP // 2) as i:
                    for s in range(2):
                        load(layer, i + WO // 2, s, w_o_v, (0, KC), i * (2 * CW) + s * CW)
                up_slabs(1, UP2)
                down_slabs(1, DOWN2)
            for s in range(2):
                sp.wait_ge(state_stored[s].sem, state_stored[s].after(DEPTH - 1, 2))
            sp.wait_ge(state_p_stored.sem, 16 * DEPTH)

        @block.gpsimd
        def _(pool):
            pool.dma_start(pages[:, :], page_table.rearrange("(o b) n -> o (b n)", o=1)).then_inc(pages_loaded.sem, 16)
            pool.wait_ge(pages_loaded.sem, 16)
            with pool.Fori(0, DEPTH) as layer:
                def load_unit(cache, g, n, slot, unit):
                    pool.wait_ge(kv_used.sem, kv_used.after(layer, 2 * unit - 2))
                    for j in range(4):
                        page = pool.value_load(pages[0:1, ds(n + (4 * g + j) * N_PAGES, 1)], min_val=0, max_val=N_POOL - 1)
                        pool.dma_start(kv[:, slot, j:j + 1, :], cache[ds(layer * N_POOL + page, 1), :, :].rearrange("a p n -> p a n"))\
                            .then_inc(kv_loaded[slot].sem, 16)

                def wait(signal, n):
                    pool.wait_ge(signal.sem, signal.after(layer, n))
                    pool.sem_inc(pool_passed.sem, 1)

                def load_units(cache, g, first):
                    with pool.Fori(0, N_PAGES // 2) as i:
                        for s in range(2):
                            load_unit(cache, g, i * 2 + s, s, i * 2 + (first + s))

                load_units(k_pages, 0, 0)
                load_units(k_pages, 1, 8)
                wait(tok_act, 1)
                pool.dma_start(v_prompt[ds(layer, 1), 0].rearrange("l (t p) h d -> p (l t) (h d)", p=P),
                               v_tok[:, 0:2, :]).then_inc(kv_stored.sem, 16)
                pool.dma_start(v_sample[ds(layer, 1)].rearrange("l b s h d -> (l b s) (h d)"),
                               v_tok[0:TS, 2, :]).then_inc(kv_stored.sem, 16)
                wait(tok_act, 3)
                pool.dma_start(k_prompt[ds(layer, 1), 0].rearrange("l (t p) h d -> p (l t) (h d)", p=P),
                               k_tok[:, 0:2, :]).then_inc(kv_stored.sem, 16)
                pool.dma_start(k_sample[ds(layer, 1)].rearrange("l b s h d -> (l b s) (h d)"),
                               k_tok[0:TS, 2, :]).then_inc(kv_stored.sem, 16)
                load_units(v_pages, 0, 16)
                load_units(v_pages, 1, 24)
            pool.wait_ge(kv_stored.sem, kv_stored.after(DEPTH - 1, 4))
            pool.wait_ge(last_act.sem, 3)
            pool.wait_ge(last_dve.sem, 3)
            pool.dma_start(y_prompt[0].rearrange("(t p) d -> p t d", p=P), stage[:, 0:2, :]).then_inc(y_stored.sem, 16)
            pool.dma_start(y_sample.rearrange("b s d -> (b s) d"), stage[0:TS, 2, :]).then_inc(y_stored.sem, 16)
            pool.wait_ge(y_stored.sem, 32)

        @block.scalar
        def _(act):
            n_loads = 0
            for dst, src in ((const[:, :], consts),
                             (stage[:, 0:2, :], x_prompt[0].rearrange("(t p) d -> p t d", p=P)),
                             (stage[0:TS, 2, :], x_sample.rearrange("b s d -> (b s) d"))):
                act.dma_start(dst, src).then_inc(loaded.sem, 16)
                n_loads += 1
            for row, arr, n in ((G_FFN1, g_ffn1, KC), (G_MIX, g_mix, KC), (G_FFN2, g_ffn2, KC), (G_GN, gn_gain, H_R), (G_GB, gn_bias, H_R)):
                for l in range(DEPTH):
                    act.dma_start(gain_rows[l * GL + row:l * GL + row + n, :], arr[l].rearrange("(c p) -> c p", p=P)).then_inc(loaded.sem, 16)
                    n_loads += 1
            for row, arr in ((G_Q, g_q), (G_K, g_k)):
                for l in range(DEPTH):
                    for half in range(2):
                        act.dma_start(gain_rows[l * GL + row:l * GL + row + 1, half * D_A:(half + 1) * D_A],
                                      arr[l:l + 1, :]).then_inc(loaded.sem, 16)
                        n_loads += 1
            assert n_loads == N_LOADS

            with act.Fori(0, DEPTH) as layer:
                def hi(pair, slot, chunks=KC):
                    act.wait_ge(raw_loaded[slot].sem, raw_loaded[slot].after(layer, pair + 1))
                    act.wait_ge(slab_used.sem, slab_used.after(layer, 2 * pair + slot - 1))
                    act.activation(w_hi[:, slot, 0:chunks * CW], raw[:, slot, 0:chunks * CW], ACT.Copy).then_inc(hi_done.sem, 1)

                def hi_slab(n, chunks=KC):
                    hi(n // 2, n % 2, chunks)

                def rms(r, i, g0):
                    act.wait_ge(x_done.sem, x_done.after(layer, DP * r - DP + i + 1))
                    for c in (2 * i, 2 * i + 1):
                        last = act.activation(h_hi[:, c, :], xT[:, c, :], ACT.Copy, scale=gain[:, g0 + c:g0 + c + 1])
                    last.then_inc(h_hi_done.sem, 1)
                    act.activation(squares[:, 2 * i:2 * i + 2, :], xT[:, 2 * i:2 * i + 2, :], ACT.Square).then_inc(rms_sq.sem, 1)

                def rms_end(r):
                    act.wait_ge(rms_sum.sem, rms_sum.after(layer, r + 1))
                    act.activation(rstd[:, :], ps[:, 4, 0:T], ACT.Ln, bias=eps_col, scale=1.0 / D_MODEL).then_inc(rms_ln.sem, 1)
                    act.wait_ge(rms_ln.sem, rms_ln.after(layer, r + 1))
                    act.activation(rstd[:, :], rstd[:, :], ACT.Exp, scale=-0.5).then_inc(rms_rstd.sem, 1)

                def up_silu(f, i, buf):
                    act.wait_ge(up_gate.sem, up_gate.after(layer, f * UP_PAIRS + 1) + i)
                    act.activation(silu[:, buf], silu[:, buf], ACT.Silu).then_inc(silu_done.sem, 1)

                def up_hi(f, i, buf):
                    act.wait_ge(up_prod.sem, up_prod.after(layer, f * UP_PAIRS + 1) + i)
                    act.activation(hid_hi[:, ds(i * 2, 2), :], hid_f[:, buf], ACT.Copy).then_inc(hid_hi_done.sem, 1)

                def ffn(f, r, first_up, first_down, rms_next):
                    hi_slab(first_up + 2)
                    rms_end(r)
                    with act.Fori(0, UP_PAIRS // 2) as t:
                        for b in range(2):
                            i = t * 2 + b
                            up_silu(f, i, b)
                            hi(i + (first_up // 2 + 1), 1)
                            up_hi(f, i, b)
                            hi(i + (first_up // 2 + 2), 0)
                    up_silu(f, UP_PAIRS - 1, 0)
                    hi_slab(first_down + 1, 7)
                    up_hi(f, UP_PAIRS - 1, 0)
                    hi_slab(first_down + 2, 7)
                    for i in range(1, DP):
                        hi_slab(first_down + 3 * i, 8)
                        hi_slab(first_down + 3 * i + 1, 7)
                        if rms_next:
                            rms_next(i - 1)
                        hi_slab(first_down + 3 * i + 2, 7)
                    if rms_next:
                        hi_slab(first_down + 3 * DP)
                        rms_next(DP - 1)
                        hi_slab(first_down + 3 * DP + 1)

                eps_col = EPS
                act.wait_ge(gain_done.sem, layer + 1)
                for i in range(DP - 1):
                    rms(0, i, G_FFN1)
                hi_slab(UP1)
                rms(0, DP - 1, G_FFN1)
                hi_slab(UP1 + 1)
                ffn(0, 0, UP1, DOWN1, lambda i: rms(1, i, G_MIX))

                hi_slab(ZIN + 2)
                rms_end(1)
                hi_slab(ZIN + 3)

                def qk_square(n):
                    act.wait_ge(z_done.sem, z_done.after(layer, 2 * n + 2))
                    act.activation(qk_squares[:, 4 * n:4 * n + 4], z[:, 4 * n:4 * n + 4, :], ACT.Square).then_inc(qk_sq.sem, 1)

                def qk_root(n):
                    act.wait_ge(qk_sum.sem, qk_sum.after(layer, n + 1))
                    act.activation(qk_squares[:, 4 * n:4 * n + 4], ps[:, 4:8, 0:T], ACT.Ln, bias=eps_col, scale=1.0 / D_A).then_inc(qk_ln.sem, 1)
                    act.wait_ge(qk_ln.sem, qk_ln.after(layer, n + 1))
                    act.activation(qk_squares[:, 4 * n:4 * n + 4], qk_squares[:, 4 * n:4 * n + 4], ACT.Exp, scale=-0.5).then_inc(qk_rstd.sem, 1)

                qk_square(0)
                hi_slab(ZIN + 4)
                qk_root(0)

                def unit_step(g, i, s):
                    hi(i + (ZIN // 2 + 2 + 4 * g + s), 1 - s)
                    act.wait_ge(sc_done.sem, sc_done.after(layer, 8 * g + s - 1) + i * 2)
                    for half in range(2):
                        act.wait_ge(kv_used.sem, kv_used.after(layer, 16 * g + 2 * s + half + 1) + i * 4)
                        act.activation(kT[:, s, 2 * half, :], ps[:, 4, :], ACT.Copy).then_inc(kt_act.sem, 1)

                with act.Fori(0, 4) as i:
                    for s in range(2):
                        unit_step(0, i, s)

                qk_square(1)
                qk_root(1)
                for tr, bank, tok in ((0, 0, v_tok), (1, 4, vr_tok), (3, 4, k_tok)):
                    act.wait_ge(tr_done.sem, tr_done.after(layer, tr + 1))
                    act.activation(tok[:, 0:2, :], ps[:, bank:bank + 2, :], ACT.Copy)
                    act.activation(tok[0:TS, 2, :], ps[0:TS, bank + 2, :], ACT.Copy).then_inc(tok_act.sem, 1)

                with act.Fori(0, 3) as i:
                    for s in range(2):
                        unit_step(1, i, s)

                def sample_exp(g):
                    act.wait_ge(sm_bias.sem, sm_bias.after(layer, g + 1))
                    for n in range(5):
                        cols = slice(256 * n, min(256 * n + 256, PAST + TS))
                        last = act.activation(S[:, g, cols], S[:, g, cols], ACT.Exp, bias=small[:, g, 8 + n:9 + n],
                                              scale=SCALE_A, accum_out=small[:, g, 16 + n:17 + n])
                    last.then_inc(sm_exp.sem, 1)

                def sample_transposed(g):
                    act.wait_ge(sm_tr.sem, sm_tr.after(layer, g + 1))
                    act.activation(probT[:, g].rearrange("p n r -> p (n r)").rearrange("p (a m) -> p a m", a=2),
                                   ps[:, 4:6, :], ACT.Copy).then_inc(sm_tr_act.sem, 1)

                unit_step(1, 3, 0)
                sample_exp(0)
                unit_step(1, 3, 1)
                hi_slab(ZIN + GR1 + 1)
                sample_transposed(0)
                sample_exp(1)
                hi_slab(PROJ, 4)
                act.wait_ge(z_done.sem, z_done.after(layer, 14))
                act.activation(z[:, ZGR:ZGR + 4, :], z[:, ZGR:ZGR + 4, :], ACT.Silu).then_inc(gr_silu.sem, 1)
                sample_transposed(1)
                hi_slab(PROJ + 1, 4)

                def heads_out(g):
                    act.wait_ge(pv_tr.sem, pv_tr.after(layer, g + 1))
                    for half in range(2):
                        rows = slice(64 * half, 64 * half + 64)
                        src = ps[rows, 5, :].rearrange("p (c j h q) -> p c j h q", c=4, j=4, q=4)[:, :, :, half, :]
                        last = act.activation(oT[rows, :, SEQ + 16 * g:SEQ + 16 * g + 16].rearrange("p c (j q) -> p c j q", j=4),
                                              src, ACT.Copy)
                    last.then_inc(pv_out.sem, 1)

                act.wait_ge(kv_stored.sem, kv_stored.after(layer, 4))
                for h in range(H_R):
                    act.wait_ge(ret_out.sem, ret_out.after(layer, h + 1))
                    act.activation(orT[:, h, :], ps[:, 1, 0:T], ACT.Copy)
                    act.activation(state_p[:, h, :], ps[:, 2, 0:P], ACT.Copy).then_inc(ret_act.sem, 1)
                    if h == 0:
                        act.wait_ge(z_done.sem, z_done.after(layer, 18))
                        act.activation(z[:, ZGA:ZGA + KC, :], z[:, ZGA:ZGA + KC, :], ACT.Sigmoid).then_inc(gates_done.sem, 1)
                    if h == 1:
                        heads_out(0)
                        act.wait_ge(z_done.sem, z_done.after(layer, Z_SLABS))
                        act.activation(z[:, ZV:ZV + 4, :], z[:, ZV:ZV + 4, :], ACT.Sigmoid)
                        act.activation(z[:, ZVR:ZVR + 4, :], z[:, ZVR:ZVR + 4, :], ACT.Sigmoid).then_inc(gates_done.sem, 1)
                heads_out(1)

                def prompt_exp(hb):
                    act.wait_ge(pp_max.sem, pp_max.after(layer, hb + 1))
                    for i in range(8):
                        hi_, tile = i % 4, i // 4
                        cols = slice(0, P) if tile == 0 else slice(P, 3 * P)
                        last = act.activation(prob_p[hb][:, hi_, cols], prob_p[hb][:, hi_, cols], ACT.Exp,
                                              bias=mx[:, 8 * hb + i:8 * hb + i + 1],
                                              scale=SCALE_A, accum_out=small[:, hb, i:i + 1])
                    last.then_inc(pp_exp.sem, 1)

                def prompt_out(hb):
                    act.wait_ge(pp_tr.sem, pp_tr.after(layer, hb + 1))
                    if hb:
                        act.wait_ge(pp_out.sem, pp_out.after(layer, hb))
                    act.activation(probT_p[:, :, :].rearrange("p h k -> p (h k)")[:, 0:512], ps[:, 4, :], ACT.Copy).then_inc(pp_tr_act.sem, 1)
                    act.wait_ge(pp_out.sem, pp_out.after(layer, hb + 1))
                    act.activation(oT[:, 2 * hb:2 * hb + 2, 0:SEQ], ps[:, 7, :].rearrange("p (c t) -> p c t", c=2), ACT.Copy)\
                       .then_inc(pp_read.sem, 1)

                act.wait_ge(gn_cen.sem, gn_cen.after(layer, 1))
                act.activation(squares_r, orT, ACT.Square).then_inc(gn_sq.sem, 1)
                prompt_exp(0)
                act.wait_ge(gn_var.sem, gn_var.after(layer, 1))
                act.activation(squares_r, ps[:, 4:8, 0:T], ACT.Ln, bias=eps_col, scale=1.0 / D_R).then_inc(gn_ln.sem, 1)
                act.wait_ge(gn_ln.sem, gn_ln.after(layer, 1))
                act.activation(squares_r, squares_r, ACT.Exp, scale=-0.5).then_inc(gn_rstd.sem, 1)
                prompt_exp(1)
                prompt_out(0)
                act.wait_ge(or_done.sem, or_done.after(layer, 1))
                act.activation(or_hi[:, :, :], orT, ACT.Copy).then_inc(or_hi_done.sem, 1)
                prompt_out(1)
                act.wait_ge(pp_read.sem, pp_read.after(layer, 2))
                act.wait_ge(pv_out.sem, pv_out.after(layer, 2))
                act.activation(oa_hi[:, :, :], oT, ACT.Copy).then_inc(oa_hi_done.sem, 1)

                def merge_hi(i):
                    act.wait_ge(merged.sem, merged.after(layer, i + 1))
                    act.activation(mg_hi[:, 2 * i:2 * i + 2, :], hid_f[:, i % 2], ACT.Copy).then_inc(mg_hi_done.sem, 1)

                for i in range(1, DP):
                    hi_slab(PROJ + 2 * i, 4)
                    hi_slab(PROJ + 2 * i + 1, 4)
                    if i > 1:
                        merge_hi(i - 2)
                merge_hi(DP - 2)
                hi_slab(WO)
                hi_slab(WO + 1)
                merge_hi(DP - 1)
                hi_slab(WO + 2)
                rms(2, 0, G_FFN2)
                hi_slab(WO + 3)
                rms(2, 1, G_FFN2)
                rms(2, 2, G_FFN2)
                hi_slab(UP2)
                rms(2, 3, G_FFN2)
                hi_slab(UP2 + 1)
                ffn(1, 2, UP2, DOWN2, None)

            act.wait_ge(last_tr.sem, 1)
            for t in range(3):
                rows = P if t < 2 else TS
                act.activation(stage[0:rows, t, 0:512], ps[0:rows, 2 * t, :], ACT.Copy).then_inc(last_act.sem, 1)

        @block.tensor
        def _(pe):
            def triple(out, w, wl, x, xl, start, stop):
                pe.matmul(out, w, x, start=start, stop=False)
                pe.matmul(out, wl, x, start=False, stop=False)
                return pe.matmul(out, w, xl, start=False, stop=stop)

            pe.wait_ge(loaded.sem, 16 * N_LOADS)
            for c in range(KC):
                for t in range(3):
                    rows = P if t < 2 else TS
                    pe.transpose(ps[:, c, t * P:t * P + rows], stage[0:rows, t, c * P:(c + 1) * P], ident[0:rows, 0:rows])
            pe.transpose(ps[:, 0, 300:300 + DEPTH * GL], gain_rows[:, :], ident[0:DEPTH * GL, 0:DEPTH * GL]).then_inc(first_tr.sem, 1)

            with pe.Fori(0, DEPTH) as layer:
                def half_slab(pair, slot, t, bank, hi, lo, k0, n, start=True, stop=True, first_of=None):
                    if t == 0:
                        pe.wait_ge(split_done.sem, split_done.after(layer, 2 * pair + slot + 1))
                    for k in range(n):
                        if first_of is not None and t == 0 and k % 2 == 0:
                            pe.wait_ge(h_done.sem, h_done.after(layer, 4 * first_of + k // 2 + 1))
                        cols = slice(k * CW + t * P, k * CW + t * P + P)
                        last = triple(ps[:, bank + t, 0:T], w_hi[:, slot, cols], w_lo[:, slot, cols],
                                      hi[:, k0 + k, :], lo[:, k0 + k, :], start and k == 0, stop and k == n - 1)
                    if t == 1:
                        last.then_inc(slab_used.sem, 1)

                def slab(pair, slot, bank, hi, lo, k0, n, start=True, stop=True, first_of=None):
                    for t in range(2):
                        half_slab(pair, slot, t, bank, hi, lo, k0, n, start, stop, first_of)

                def first_slab(r, pair):
                    slab(pair, 0, 0, h_hi, h_lo, 0, KC, first_of=r)
                    pe.wait_ge(rms_acc.sem, rms_acc.after(layer, r + 1))
                    for c in range(2):
                        last = pe.matmul(ps[:, 4, 0:T], ones, squares[:, c, :], start=c == 0, stop=c == 1)
                    last.then_inc(rms_sum.sem, 1)

                def ffn(f, r, first_up, first_down):
                    def up_pair(i, buf):
                        pe.wait_ge(up_read.sem, up_read.after(layer, f * UP_PAIRS - 1) + i)
                        if buf:
                            pe.wait_ge(rms_ln.sem, rms_ln.after(layer, r + 1))
                        for s in range(2):
                            slab(i + first_up // 2, s, 4 * buf + 2 * s, h_hi, h_lo, 0, KC)

                    pe.wait_ge(up_read.sem, up_read.after(layer, f * UP_PAIRS - 1))
                    first_slab(r, first_up // 2)
                    slab(first_up // 2, 1, 2, h_hi, h_lo, 0, KC)
                    with pe.Fori(0, UP_PAIRS // 2) as t:
                        up_pair(t * 2 + 1, 1)
                        up_pair(t * 2 + 2, 0)
                    with pe.Fori(0, DP // 2) as t:
                        for n in range(6):
                            k0, k1 = F_PARTS[n % 3]
                            bank = 4 + 2 * (n // 3)
                            if n % 3 == 0:
                                pe.wait_ge(x_done.sem, x_done.after(layer, (0, 2 * DP)[f] + n // 3 - 1) + t * 2)
                                if n == 0:
                                    pe.wait_ge(up_read.sem, up_read.after(layer, f * UP_PAIRS + UP_PAIRS - 1))
                            pe.wait_ge(hid_done.sem, hid_done.after(layer, f * UP_PAIRS + (k1 + 1) // 2))
                            slab(t * 3 + (first_down // 2 + n // 2), n % 2, bank, hid_hi, hid_lo, k0, k1 - k0, n % 3 == 0, n % 3 == 2)

                ffn(0, 0, UP1, DOWN1)

                first_slab(1, ZIN // 2)
                slab(ZIN // 2, 1, 2, h_hi, h_lo, 0, KC)

                def z_free(m):
                    pe.wait_ge(z_done.sem, z_done.after(layer, m - 1))

                z_free(2)
                slab(ZIN // 2 + 1, 0, 0, h_hi, h_lo, 0, KC)

                def qk_sums(n):
                    pe.wait_ge(qk_sq.sem, qk_sq.after(layer, n + 1))
                    for c in range(4):
                        last = pe.matmul(ps[:, 4 + c, 0:T], heads, qk_squares[:, 4 * n + c, :], start=True, stop=True)
                    last.then_inc(qk_sum.sem, 1)

                pe.wait_ge(rms_ln.sem, rms_ln.after(layer, 2))
                qk_sums(0)
                z_free(3)
                slab(ZIN // 2 + 1, 1, 2, h_hi, h_lo, 0, KC)

                def unit_step(g, i, s):
                    def transposes(half):
                        pe.wait_ge(kt_act.sem, kt_act.after(layer, 16 * g + 2 * s + half) + i * 4)
                        pe.wait_ge(kt_dve.sem, kt_dve.after(layer, 16 * g + 2 * s + half) + i * 4)
                        for j in range(2):
                            for c in range(4):
                                last = pe.transpose(ps[:, 4 + j, c * P:(c + 1) * P], kv[:, s, 2 * half + j, c * P:(c + 1) * P], ident)
                        last.then_inc(kv_used.sem, 1)

                    pe.wait_ge(kv_loaded[s].sem, (layer * 16 + i + (4 * g + 1)) * 64)
                    if g == 0:
                        pe.wait_ge(qk_ln.sem, qk_ln.after(layer, 1))
                    else:
                        pe.wait_ge(tok_act.sem, tok_act.after(layer, 3))
                        pe.wait_ge(tok_dve.sem, tok_dve.after(layer, 1))
                        pe.wait_ge(new_read.sem, new_read.after(layer, 1))
                    pe.wait_ge(z_done.sem, z_done.after(layer, 3 + 8 * g + s) + i * 2)
                    for half in range(2):
                        transposes(half)
                        half_slab(i + (ZIN // 2 + 2 + 4 * g), s, half, 2 * s, h_hi, h_lo, 0, KC)
                    pe.wait_ge(kt_act.sem, kt_act.after(layer, 16 * g + 2 * s + 2) + i * 4)
                    pe.wait_ge(kt_dve.sem, kt_dve.after(layer, 16 * g + 2 * s + 2) + i * 4)
                    pe.wait_ge(q_blocks_done.sem, q_blocks_done.after(layer, 1))
                    pe.wait_ge(sc_read.sem, sc_read.after(layer, 8 * g + s - 1) + i * 2)
                    for c in range(4):
                        for j in range(4):
                            last = pe.matmul(ps[32 * j:32 * j + 32, 6 + s, 0:P], q_blocks[:, 4 * g + j, c, :],
                                             kT[:, s, j, c * P:(c + 1) * P], start=c == 0, stop=c == 3)
                    last.then_inc(sc_done.sem, 1)

                with pe.Fori(0, 4) as i:
                    for s in range(2):
                        unit_step(0, i, s)

                pe.wait_ge(kt_act.sem, kt_act.after(layer, 16))
                pe.wait_ge(kt_dve.sem, kt_dve.after(layer, 16))
                pe.wait_ge(sc_read.sem, sc_read.after(layer, 8))
                qk_sums(1)

                def token_major(zc, bank):
                    for c in range(4):
                        for t in range(3):
                            rows = P if t < 2 else TS
                            last = pe.transpose(ps[0:rows, bank + t, c * P:(c + 1) * P], z[:, zc + c, t * P:t * P + rows], ident)
                    last.then_inc(tr_done.sem, 1)

                pe.wait_ge(z_done.sem, z_done.after(layer, 12))
                token_major(ZV, 0)
                pe.wait_ge(qk_ln.sem, qk_ln.after(layer, 2))
                token_major(ZVR, 4)
                pe.wait_ge(tok_act.sem, tok_act.after(layer, 1))
                token_major(ZKR, 0)
                pe.wait_ge(qk_done.sem, qk_done.after(layer, 2))
                for g in range(2):
                    for c in range(4):
                        for j in range(4):
                            last = pe.matmul(ps[32 * j:32 * j + 32, 7, g * TS:(g + 1) * TS], q_blocks[:, 4 * g + j, c, :],
                                             z[:, ZK + c, SEQ:T], start=c == 0, stop=c == 3)
                last.then_inc(new_scores.sem, 1)
                pe.wait_ge(tok_act.sem, tok_act.after(layer, 2))
                token_major(ZK, 4)

                with pe.Fori(0, 3) as i:
                    for s in range(2):
                        unit_step(1, i, s)
                for s in range(2):
                    unit_step(1, 3, s)

                def transpose_probs(g):
                    pe.wait_ge(sm_norm.sem, sm_norm.after(layer, g + 1))
                    for n in range(N_PAGES):
                        pe.transpose(ps[:, 4 + n // 4, (n % 4) * P:(n % 4 + 1) * P], S[:, g, n * P:(n + 1) * P], ident)
                    pe.transpose(ps[0:TS, 6, 0:P], S[:, g, PAST:PAST + TS], ident).then_inc(sm_tr.sem, 1)

                pe.wait_ge(kt_act.sem, kt_act.after(layer, 32))
                pe.wait_ge(kt_dve.sem, kt_dve.after(layer, 32))
                pe.wait_ge(sc_read.sem, sc_read.after(layer, 16))
                transpose_probs(0)
                for s in range(2):
                    z_free(GR1 + s)
                    slab((ZIN + GR1) // 2, s, 2 * s, h_hi, h_lo, 0, KC)
                pe.wait_ge(sm_tr_act.sem, sm_tr_act.after(layer, 1))
                pe.wait_ge(sm_tr_dve.sem, sm_tr_dve.after(layer, 1))
                transpose_probs(1)

                def value_units(g, first, last_):
                    if first == 0:
                        pe.wait_ge(sm_tr_act.sem, sm_tr_act.after(layer, g + 1))
                        pe.wait_ge(sm_tr_dve.sem, sm_tr_dve.after(layer, g + 1))
                        if g:
                            pe.wait_ge(pv_evac.sem, pv_evac.after(layer, g))
                        pe.matmul(ps[:, 7, :], probT_new[:, g, :], v_tok[0:TS, 2, :], start=True, stop=False, skip_group_check=True)
                    for n in range(first, last_):
                        pe.wait_ge(kv_loaded[n % 2].sem, kv_loaded[n % 2].after(layer, 0) + (8 + 4 * g + n // 2 + 1) * 64)
                        for j in range(4):
                            rows = slice(32 * j, 32 * j + 32)
                            last = pe.matmul(ps[rows, 7, :], probT[:, g, n, rows], kv[:, n % 2, j, :],
                                             start=False, stop=n == N_PAGES - 1, skip_group_check=True)
                            if j % 2:
                                last.then_inc(kv_used.sem, 1)

                def values_transposed(g):
                    pe.wait_ge(pv_evac.sem, pv_evac.after(layer, g + 1))
                    if g:
                        pe.wait_ge(pv_out.sem, pv_out.after(layer, g))
                    for c in range(4):
                        last = pe.transpose(ps[:, 5, c * (P - 8):c * (P - 8) + P], o_sample[:, c // 2, c % 2 * P:(c % 2 + 1) * P], ident)
                    last.then_inc(pv_tr.sem, 1)

                def ret_inner(h):
                    if h:
                        pe.wait_ge(ret_in.sem, ret_in.after(layer, h))
                    else:
                        pe.wait_ge(z_done.sem, z_done.after(layer, Z_SLABS))
                    kr, qr = z[:, ZKR + h, :], z[:, ZQR + h, :]
                    pe.matmul(ps[:, 0, 0:256], kr[:, 0:P], qr[:, 0:SEQ], start=True, stop=True)
                    pe.matmul(ps[:, 0, 256:384], kr[:, P:SEQ], qr[:, P:SEQ], start=True, stop=True)
                    pe.matmul(ps[0:TS, 0, 384:384 + TS], kr[:, SEQ:T], qr[:, SEQ:T], start=True, stop=True).then_inc(inner_done.sem, 1)

                def ret_main(h):
                    pe.wait_ge(ret_in.sem, ret_in.after(layer, h + 1))
                    if h:
                        pe.wait_ge(ret_act.sem, ret_act.after(layer, h))
                        pe.wait_ge(ret_dve.sem, ret_dve.after(layer, h))
                    cols = slice(h * D_R, (h + 1) * D_R)
                    for t in range(2):
                        pe.matmul(ps[:, 2, 0:P], kd_tok[:, t, cols], vr_tok[:, t, cols], start=t == 0, stop=t == 1)
                    for n in range(2):
                        pe.matmul(ps[:, 3 + n, :], kd_tok[0:TS, 2, cols], v_masked[:, 4 * n:4 * n + 4, :], start=True, stop=True)
                    pe.matmul(ps[:, 1, 0:P], vr_tok[:, 0, cols], inner[:, 0:P], start=True, stop=True)
                    pe.matmul(ps[:, 1, P:SEQ], vr_tok[:, 0, cols], inner[:, P:SEQ], start=True, stop=False)
                    pe.matmul(ps[:, 1, P:SEQ], vr_tok[:, 1, cols], inner[:, SEQ:384], start=False, stop=True)
                    pe.matmul(ps[:, 1, SEQ:T], vr_tok[0:TS, 2, cols], inner_s, start=True, stop=True, skip_group_check=True)
                    pe.wait_ge(state_loaded[h % 2].sem, state_loaded[h % 2].after(layer, h // 2 + 1))
                    for b in range(DEC_BATCH):
                        last = pe.matmul(ps[:, 1, SEQ + 4 * b:SEQ + 4 * b + 4], state[:, h % 2, b, :], q_dec[:, 4 * b:4 * b + 4],
                                         start=False, stop=True, skip_group_check=True)
                    last.then_inc(ret_out.sem, 1)

                ret_inner(0)
                value_units(0, 0, 4)
                ret_main(0)
                ret_inner(1)
                value_units(0, 4, 8)
                ret_main(1)
                ret_inner(2)
                values_transposed(0)
                value_units(1, 0, 4)
                ret_main(2)
                ret_inner(3)
                value_units(1, 4, 8)
                ret_main(3)
                values_transposed(1)

                def prompt_scores(hb):
                    if hb == 0:
                        pe.wait_ge(ret_act.sem, ret_act.after(layer, H_R))
                        pe.wait_ge(ret_dve.sem, ret_dve.after(layer, H_R))
                    else:
                        pe.wait_ge(pp_biased.sem, pp_biased.after(layer, hb))
                    for i in range(4):
                        h = 4 * hb + i
                        rows = slice(64 * (h % 2), 64 * (h % 2) + 64)
                        q, k = z[rows, ZQ + h // 2, :], z[rows, ZK + h // 2, :]
                        pe.matmul(ps[:, i, 0:P], q[:, 0:P], k[:, 0:P], start=True, stop=True)
                        last = pe.matmul(ps[:, i, P:384], q[:, P:SEQ], k[:, 0:SEQ], start=True, stop=True)
                    last.then_inc(pp_scores.sem, 1)

                def prompt_out(hb):
                    pe.wait_ge(pp_norm.sem, pp_norm.after(layer, hb + 1))
                    if hb == 0:
                        pe.wait_ge(gn_ln.sem, gn_ln.after(layer, 1))
                    else:
                        pe.wait_ge(pp_tr_act.sem, pp_tr_act.after(layer, hb))
                        pe.wait_ge(pp_tr_dve.sem, pp_tr_dve.after(layer, hb))
                    for i in range(4):
                        for t in range(3):
                            n = 3 * i + t
                            last = pe.transpose(ps[:, 4 + n // 4, n % 4 * P:(n % 4 + 1) * P], prob_p[hb][:, i, t * P:(t + 1) * P], ident)
                    last.then_inc(pp_tr.sem, 1)
                    pe.wait_ge(pp_tr_act.sem, pp_tr_act.after(layer, hb + 1))
                    pe.wait_ge(pp_tr_dve.sem, pp_tr_dve.after(layer, hb + 1))
                    if hb:
                        pe.wait_ge(pp_read.sem, pp_read.after(layer, hb))
                    for i in range(4):
                        h = 4 * hb + i
                        out = ps[64 * (i % 2):64 * (i % 2) + 64, 7, (i // 2) * SEQ:(i // 2 + 1) * SEQ]
                        cols = slice(h * D_A, (h + 1) * D_A)
                        pe.matmul(out[:, 0:P], v_tok[:, 0, cols], probT_p[:, i, 0:P], start=True, stop=True)
                        pe.matmul(out[:, P:SEQ], v_tok[:, 0, cols], probT_p[:, i, P:SEQ], start=True, stop=False)
                        last = pe.matmul(out[:, P:SEQ], v_tok[:, 1, cols], probT_p[:, i, SEQ:384], start=False, stop=True)
                    last.then_inc(pp_out.sem, 1)

                prompt_scores(0)
                pe.wait_ge(pv_out.sem, pv_out.after(layer, 2))
                for h in range(H_R):
                    last = pe.matmul(ps[:, 4 + h, 0:T], ones, orT[:, h, :], start=True, stop=True)
                last.then_inc(gn_mean.sem, 1)
                pe.wait_ge(gn_sq.sem, gn_sq.after(layer, 1))
                for h in range(H_R):
                    last = pe.matmul(ps[:, 4 + h, 0:T], ones, squares_r[:, h, :], start=True, stop=True)
                last.then_inc(gn_var.sem, 1)
                prompt_scores(1)
                prompt_out(0)
                prompt_out(1)

                pe.wait_ge(pp_biased.sem, pp_biased.after(layer, 2))
                for i in range(DP):
                    bank = 4 * (i % 2)
                    pe.wait_ge(proj_read.sem, proj_read.after(layer, i - 1))
                    pe.wait_ge(or_lo_done.sem, or_lo_done.after(layer, 1))
                    slab(PROJ // 2 + i, 0, bank, or_hi, or_lo, 0, 4)
                    pe.wait_ge(oa_lo_done.sem, oa_lo_done.after(layer, 1))
                    slab(PROJ // 2 + i, 1, bank + 2, oa_hi, oa_lo, 0, 4)
                with pe.Fori(0, DP // 2) as i:
                    for s in range(2):
                        pe.wait_ge(mg_done.sem, mg_done.after(layer, DP))
                        pe.wait_ge(x_done.sem, x_done.after(layer, DP + s - 1) + i * 2)
                        slab(i + WO // 2, s, 2 * s, mg_hi, mg_lo, 0, KC)
                ffn(1, 2, UP2, DOWN2)

            pe.wait_ge(x_done.sem, x_done.after(DEPTH - 1, 3 * DP))
            for t in range(3):
                rows = P if t < 2 else TS
                for c in range(KC):
                    last = pe.transpose(ps[0:rows, 2 * t + c // 4, (c % 4) * P:(c % 4 + 1) * P], xT[:, c, t * P:t * P + rows], ident)
            last.then_inc(last_tr.sem, 1)

        @block.vector
        def _(dve):
            dve.sem_inc(split_done.sem, 2)
            dve.sem_inc(slab_used.sem, 2)
            dve.sem_inc(up_read.sem, 2)
            dve.sem_inc(kv_used.sem, 4)
            dve.sem_inc(kt_act.sem, 1)
            dve.sem_inc(kt_dve.sem, 1)
            dve.sem_inc(sc_done.sem, 2)
            dve.sem_inc(sc_read.sem, 2)
            dve.sem_inc(proj_read.sem, 2)
            dve.memset(q_blocks[:, :, :, :], 0.0).then_inc(zeroed.sem, 1)
            dve.memset(small[:, :, :], 0.0).then_inc(zeroed.sem, 1)
            dve.wait_ge(zeroed.sem, 2)
            dve.wait_ge(first_tr.sem, 1)
            dve.tensor_copy(gains[:, :], ps[:, 0, 300:300 + DEPTH * GL]).then_inc(gains_done.sem, 1)
            for c in range(0, KC, 2):
                dve.tensor_copy(xT[:, c:c + 2, :], ps[:, c:c + 2, 0:T]).then_inc(x_done.sem, 1)
            dve.wait_ge(gains_done.sem, 1)

            with dve.Fori(0, DEPTH) as layer:
                links = [0]

                def link(ins):
                    links[0] += 1
                    ins.then_inc(dve_link.sem, 1)
                    dve.wait_ge(dve_link.sem, dve_link.after(layer, links[0]))

                def lo(pair, slot, chunks=KC):
                    dve.wait_ge(hi_done.sem, hi_done.after(layer, 2 * pair + slot + 1))
                    n = chunks * CW
                    dve.tensor_tensor(w_lo[:, slot, 0:n], raw[:, slot, 0:n], w_hi[:, slot, 0:n].bitcast(F32), ALU.subtract)\
                       .then_inc(split_done.sem, 1)

                def lo_slab(n, chunks=KC):
                    lo(n // 2, n % 2, chunks)

                def x_add(i, slab_n, bank, factor):
                    dve.wait_ge(slab_used.sem, slab_used.after(layer, slab_n + 1))
                    dve.scalar_tensor_tensor(xT[:, 2 * i:2 * i + 2, :], ps[:, bank:bank + 2, 0:T], factor,
                                             xT[:, 2 * i:2 * i + 2, :], ALU.mult, ALU.add).then_inc(x_done.sem, 1)

                def rms(r, i, g0):
                    dve.wait_ge(h_hi_done.sem, h_hi_done.after(layer, 4 * r + i + 1))
                    for c in (2 * i, 2 * i + 1):
                        last = dve.scalar_tensor_tensor(h_lo[:, c, :], xT[:, c, :], gain[:, g0 + c:g0 + c + 1],
                                                        h_hi[:, c, :].bitcast(F32), ALU.mult, ALU.subtract)
                    last.then_inc(h_done.sem, 1)
                    if i:
                        dve.wait_ge(rms_sq.sem, rms_sq.after(layer, 4 * r + i + 1))
                        last = dve.tensor_tensor(squares[:, 0:2, :], squares[:, 0:2, :], squares[:, 2 * i:2 * i + 2, :], ALU.add)
                        if i < DP - 1:
                            link(last)
                        else:
                            last.then_inc(rms_acc.sem, 1)

                rstd2 = rstd[:, :].unsqueeze(1).to_broadcast([P, 2, T])

                def up_gated(f, i, slabs, buf):
                    dve.wait_ge(rms_rstd.sem, rms_rstd.after(layer, 2 * f + 1))
                    dve.wait_ge(slab_used.sem, slab_used.after(layer, slabs + 1) + i * 2)
                    dve.tensor_tensor(silu[:, buf], ps[:, 4 * buf:4 * buf + 2, 0:T], rstd2, ALU.mult).then_inc(up_gate.sem, 1)

                def up_linear(f, i, slabs, buf):
                    dve.wait_ge(slab_used.sem, slab_used.after(layer, slabs + 2) + i * 2)
                    dve.tensor_tensor(hid_f[:, buf], ps[:, 4 * buf + 2:4 * buf + 4, 0:T], rstd2, ALU.mult).then_inc(up_read.sem, 1)

                def up_product(f, i, buf):
                    dve.wait_ge(silu_done.sem, silu_done.after(layer, f * UP_PAIRS + 1) + i)
                    dve.wait_ge(up_read.sem, up_read.after(layer, f * UP_PAIRS + 1) + i)
                    dve.tensor_tensor(hid_f[:, buf], silu[:, buf], hid_f[:, buf], ALU.mult).then_inc(up_prod.sem, 1)
                    dve.wait_ge(hid_hi_done.sem, hid_hi_done.after(layer, f * UP_PAIRS + 1) + i)
                    at = ds(i * 2, 2)
                    dve.tensor_tensor(hid_lo[:, at, :], hid_f[:, buf], hid_hi[:, at, :].bitcast(F32), ALU.subtract).then_inc(hid_done.sem, 1)

                def ffn(f, r, first_up, first_down, rms_next):
                    lo_slab(first_up + 2)
                    up_gated(f, 0, first_up, 0)
                    with dve.Fori(0, UP_PAIRS // 2) as t:
                        for b in range(2):
                            i = t * 2 + b
                            up_linear(f, i, first_up, b)
                            lo(i + (first_up // 2 + 1), 1)
                            up_product(f, i, b)
                            up_gated(f, i + 1, first_up, 1 - b)
                            lo(i + (first_up // 2 + 2), 0)
                    up_linear(f, UP_PAIRS - 1, first_up, 0)
                    lo_slab(first_down + 1, 7)
                    up_product(f, UP_PAIRS - 1, 0)
                    lo_slab(first_down + 2, 7)
                    for i in range(1, DP):
                        lo_slab(first_down + 3 * i, 8)
                        lo_slab(first_down + 3 * i + 1, 7)
                        x_add(i - 1, first_down + 3 * i - 1, 4 + 2 * ((i - 1) % 2), 0.5)
                        if rms_next:
                            rms_next(i - 1)
                        lo_slab(first_down + 3 * i + 2, 7)
                    if rms_next:
                        lo_slab(first_down + 3 * DP)
                    x_add(DP - 1, first_down + 3 * DP - 1, 4 + 2 * ((DP - 1) % 2), 0.5)
                    if rms_next:
                        rms_next(DP - 1)
                        lo_slab(first_down + 3 * DP + 1)

                dve.tensor_copy(gain[:, :], gains[:, ds(layer * GL, GL)]).then_inc(gain_done.sem, 1)
                dve.wait_ge(gain_done.sem, layer + 1)
                for i in range(DP - 1):
                    rms(0, i, G_FFN1)
                lo_slab(UP1)
                rms(0, DP - 1, G_FFN1)
                lo_slab(UP1 + 1)
                ffn(0, 0, UP1, DOWN1, lambda i: rms(1, i, G_MIX))

                def z_copy(m, place, slot):
                    dve.wait_ge(slab_used.sem, slab_used.after(layer, ZIN + 1) + m)
                    dve.tensor_tensor(z[:, ds(place, 2), :], ps[:, 2 * slot:2 * slot + 2, 0:T], rstd2, ALU.mult).then_inc(z_done.sem, 1)

                def qk_norm(n, g):
                    dve.wait_ge(qk_rstd.sem, qk_rstd.after(layer, n + 1))
                    dve.scalar_tensor_tensor(z[:, 4 * n:4 * n + 4, :], z[:, 4 * n:4 * n + 4, :], gain[:, g:g + 1], qk_squares[:, 4 * n:4 * n + 4, :],
                                             ALU.mult, ALU.mult).then_inc(qk_done.sem, 1)

                lo_slab(ZIN + 2)
                dve.wait_ge(rms_rstd.sem, rms_rstd.after(layer, 2))
                z_copy(0, z_place(0), 0)
                z_copy(1, z_place(1), 1)
                lo_slab(ZIN + 3)
                z_copy(2, z_place(2), 0)
                lo_slab(ZIN + 4)
                qk_norm(0, G_Q)
                dve.wait_ge(qk_done.sem, qk_done.after(layer, 1))
                for c in range(4):
                    for half in range(2):
                        rows, col = slice(64 * half, 64 * half + 64), 8 * c + 4 * half
                        last = dve.tensor_copy(q_blocks[rows, :, c, col:col + 4],
                                               z[rows, ZQ + c, SEQ:T].rearrange("p (b q) -> p b q", b=8))
                last.then_inc(q_blocks_done.sem, 1)
                z_copy(3, z_place(3), 1)

                page_sum = small[:, :, 24:32]

                def unit_step(g, i, s):
                    def k_transposed(half):
                        dve.wait_ge(kv_used.sem, kv_used.after(layer, 16 * g + 2 * s + half + 1) + i * 4)
                        dve.tensor_copy(kT[:, s, 2 * half + 1, :], ps[:, 5, :]).then_inc(kt_dve.sem, 1)

                    dve.wait_ge(sc_done.sem, sc_done.after(layer, 8 * g + s - 1) + i * 2)
                    k_transposed(0)
                    lo(i + (ZIN // 2 + 2 + 4 * g + s), 1 - s)
                    k_transposed(1)
                    m = i * 2 + (4 + 8 * g + s)
                    z_copy(m, m + m if g == 0 else z_place(m) if isinstance(i, int) else m + m + (ZGR - 24), s)
                    dve.wait_ge(sc_done.sem, sc_done.after(layer, 8 * g + s + 1) + i * 2)
                    at = C_AT["pageb"][0]
                    dve.scalar_tensor_tensor(S[:, g, ds(i * 256 + s * P, P)], ps[:, 6 + s, 0:P], const[:, ds(i * 2 + (at + s), 1)],
                                             cst("pastb"), ALU.add, ALU.add)
                    dve.tensor_reduce(page_sum[:, g, ds(i * 2 + s, 1)], ps[:, 6 + s, 0:P], AX, ALU.add).then_inc(sc_read.sem, 1)

                with dve.Fori(0, 4) as i:
                    for s in range(2):
                        unit_step(0, i, s)

                qk_norm(1, G_K)
                dve.wait_ge(tr_done.sem, tr_done.after(layer, 3))
                kdecay = cst("kdecay").rearrange("p (t h) -> p t h", t=3)
                for t in range(3):
                    rows = P if t < 2 else TS
                    last = dve.tensor_tensor(kd_tok[0:rows, t, :].rearrange("p (h d) -> p h d", h=H_R),
                                             ps[0:rows, t, :].rearrange("p (h d) -> p h d", h=H_R),
                                             kdecay[0:rows, t, :].unsqueeze(2).to_broadcast([rows, H_R, D_R]), ALU.mult)
                last.then_inc(tok_dve.sem, 1)
                dve.wait_ge(new_scores.sem, new_scores.after(layer, 1))
                dve.tensor_tensor(S[:, :, PAST:PAST + TS], ps[:, 7, 0:2 * TS].rearrange("p (g t) -> p g t", g=2),
                                  cst("newb").rearrange("p (g t) -> p g t", g=2), ALU.add).then_inc(new_read.sem, 1)

                with dve.Fori(0, 3) as i:
                    for s in range(2):
                        unit_step(1, i, s)

                def sample_bias(g):
                    dve.wait_ge(new_read.sem, new_read.after(layer, 1))
                    dve.wait_ge(sc_read.sem, sc_read.after(layer, 8 * (g + 1)))
                    sg = small[:, g]
                    gate4, least, score, drop, bmax = sg[:, 32:36], sg[:, 36:37], sg[:, 40:44], sg[:, 48:53], sg[:, 56:61]
                    link(dve.tensor_reduce(gate4, page_sum[:, g, :].rearrange("p (b n) -> p b n", n=2), AX, ALU.add))
                    link(dve.tensor_reduce(least, gate4, AX, ALU.min))
                    link(dve.scalar_tensor_tensor(score, gate4, least, cst("rank"), ALU.is_equal, ALU.mult))
                    link(dve.tensor_reduce(sg[:, 37:38], score, AX, ALU.max))
                    dve.tensor_scalar(drop[:, 0:4], score, sg[:, 37:38], NEG, ALU.is_equal, ALU.mult)
                    dve.tensor_reduce(bmax[:, 0:4], S[:, g, 0:PAST].rearrange("p (b n) -> p b n", b=4), AX, ALU.max)
                    link(dve.tensor_reduce(bmax[:, 4:5], S[:, g, PAST:PAST + TS], AX, ALU.max))
                    link(dve.tensor_tensor(bmax[:, 0:4], bmax[:, 0:4], drop[:, 0:4], ALU.add))
                    link(dve.tensor_reduce(sg[:, 38:39], bmax, AX, ALU.max))
                    link(dve.tensor_scalar(sg[:, 39:40], sg[:, 38:39], -SCALE_A, None, ALU.mult))
                    dve.tensor_scalar(sg[:, 8:13], drop, sg[:, 39:40], None, ALU.add).then_inc(sm_bias.sem, 1)

                def sample_norm(g):
                    sg = small[:, g]
                    dve.wait_ge(sm_exp.sem, sm_exp.after(layer, g + 1))
                    link(dve.tensor_reduce(sg[:, 22:23], sg[:, 16:21], AX, ALU.add))
                    link(dve.reciprocal(sg[:, 23:24], sg[:, 22:23]))
                    dve.tensor_scalar(S[:, g, :], S[:, g, :], sg[:, 23:24], None, ALU.mult).then_inc(sm_norm.sem, 1)

                def sample_transposed(g):
                    dve.wait_ge(sm_tr.sem, sm_tr.after(layer, g + 1))
                    dve.tensor_copy(probT_new[:, g, :], ps[0:TS, 6, 0:P]).then_inc(sm_tr_dve.sem, 1)

                sample_bias(0)
                unit_step(1, 3, 0)
                sample_norm(0)
                unit_step(1, 3, 1)
                sample_bias(1)
                lo_slab(ZIN + GR1 + 1)
                sample_transposed(0)
                z_copy(GR1, z_place(GR1), 0)
                sample_norm(1)
                lo_slab(PROJ, 4)
                z_copy(GR1 + 1, z_place(GR1 + 1), 1)
                sample_transposed(1)
                lo_slab(PROJ + 1, 4)

                def ret_operands(h):
                    dve.wait_ge(inner_done.sem, inner_done.after(layer, h + 1))
                    if h:
                        dve.wait_ge(ret_out.sem, ret_out.after(layer, h))
                    decay = cst("decay", h * SEQ, (h + 1) * SEQ)
                    dve.tensor_tensor(inner[:, 0:SEQ], ps[:, 0, 0:SEQ], decay, ALU.mult)
                    dve.tensor_tensor(inner[:, SEQ:384], ps[:, 0, SEQ:384], decay[:, 0:P], ALU.mult)
                    dve.tensor_tensor(inner_s, ps[0:TS, 0, 384:384 + TS], cst("sdecay", h * TS, (h + 1) * TS)[0:TS, :], ALU.mult)
                    dve.tensor_tensor(q_dec, z[:, ZQR + h, SEQ:T], cst("qdecay", h * TS, (h + 1) * TS), ALU.mult)
                    dve.tensor_tensor(v_masked, vr_tok[0:TS, 2:3, h * D_R:(h + 1) * D_R].to_broadcast([TS, DEC_BATCH, D_R]),
                                      cst("batch")[0:TS, :].unsqueeze(2).to_broadcast([TS, DEC_BATCH, D_R]), ALU.mult).then_inc(ret_in.sem, 1)

                def ret_state(h):
                    dve.wait_ge(ret_out.sem, ret_out.after(layer, h + 1))
                    st = state[:, h % 2].rearrange("p b e -> p (b e)").rearrange("p (n m) -> p n m", n=2)
                    dve.scalar_tensor_tensor(st, st, math.exp(log_decay(h) * DEC_SEQ), ps[:, 3:5, :], ALU.mult, ALU.add)\
                       .then_inc(ret_dve.sem, 1)

                def values_out(g):
                    dve.wait_ge(kv_used.sem, kv_used.after(layer, 48 + 16 * g))
                    if g:
                        dve.wait_ge(pv_tr.sem, pv_tr.after(layer, g))
                    else:
                        dve.wait_ge(kv_stored.sem, kv_stored.after(layer, 4))
                    dve.tensor_copy(o_sample, ps[:, 7, :].rearrange("p (c t) -> p c t", c=2)).then_inc(pv_evac.sem, 1)

                ret_operands(0)
                for h in range(H_R):
                    if h + 1 < H_R:
                        ret_operands(h + 1)
                    ret_state(h)
                    if h == 0:
                        values_out(0)
                    if h == 2:
                        values_out(1)

                def prompt_bias(hb):
                    dve.wait_ge(pp_scores.sem, pp_scores.after(layer, hb + 1))
                    m = mx[:, 8 * hb:8 * hb + 8]
                    for i in range(4):
                        last = dve.scalar_tensor_tensor(prob_p[hb][:, i, :], cst("causal"), 8.0 * slope(4 * hb + i), ps[:, i, 0:384],
                                                        ALU.mult, ALU.add)
                    last.then_inc(pp_biased.sem, 1)
                    dve.wait_ge(pp_biased.sem, pp_biased.after(layer, hb + 1))
                    dve.tensor_reduce(m[:, 0:4], prob_p[hb][:, :, 0:P], AX, ALU.max)
                    link(dve.tensor_reduce(m[:, 4:8], prob_p[hb][:, :, P:384], AX, ALU.max))
                    dve.tensor_scalar(m, m, -SCALE_A, None, ALU.mult).then_inc(pp_max.sem, 1)

                def prompt_norm(hb):
                    dve.wait_ge(pp_exp.sem, pp_exp.after(layer, hb + 1))
                    m = mx[:, 8 * hb:8 * hb + 8]
                    link(dve.reciprocal(m, small[:, hb, 0:8]))
                    dve.tensor_tensor(prob_p[hb][:, :, 0:P], prob_p[hb][:, :, 0:P], m[:, 0:4].unsqueeze(2).to_broadcast([P, 4, P]), ALU.mult)
                    dve.tensor_tensor(prob_p[hb][:, :, P:384], prob_p[hb][:, :, P:384], m[:, 4:8].unsqueeze(2).to_broadcast([P, 4, 2 * P]), ALU.mult)\
                       .then_inc(pp_norm.sem, 1)

                def prompt_transposed(hb):
                    dve.wait_ge(pp_tr.sem, pp_tr.after(layer, hb + 1))
                    if hb:
                        dve.wait_ge(pp_out.sem, pp_out.after(layer, hb))
                    dve.tensor_copy(probT_p[:, :, :].rearrange("p h k -> p (h k)")[:, 512:1536].rearrange("p (a n) -> p a n", a=2),
                                    ps[:, 5:7, :]).then_inc(pp_tr_dve.sem, 1)

                prompt_bias(0)
                dve.wait_ge(gn_mean.sem, gn_mean.after(layer, 1))
                dve.scalar_tensor_tensor(orT, ps[:, 4:8, 0:T], -1.0 / D_R, orT, ALU.mult, ALU.add).then_inc(gn_cen.sem, 1)
                prompt_norm(0)
                dve.wait_ge(gn_cen.sem, gn_cen.after(layer, 1))
                dve.wait_ge(gn_rstd.sem, gn_rstd.after(layer, 1))
                link(dve.tensor_tensor(orT, orT, squares_r, ALU.mult))
                dve.wait_ge(state_p_stored.sem, state_p_stored.after(layer, 1))
                prompt_bias(1)
                for h in range(H_R):
                    last = dve.tensor_scalar(orT[:, h, :], orT[:, h, :], gain[:, G_GN + h:G_GN + h + 1], gain[:, G_GB + h:G_GB + h + 1],
                                             ALU.mult, ALU.add)
                link(last)
                prompt_transposed(0)
                dve.wait_ge(gr_silu.sem, gr_silu.after(layer, 1))
                dve.tensor_tensor(orT, orT, z[:, ZGR:ZGR + 4, :], ALU.mult).then_inc(or_done.sem, 1)
                prompt_norm(1)
                dve.wait_ge(or_hi_done.sem, or_hi_done.after(layer, 1))
                dve.wait_ge(or_done.sem, or_done.after(layer, 1))
                dve.tensor_tensor(or_lo[:, :, :], orT, or_hi[:, :, :].bitcast(F32), ALU.subtract).then_inc(or_lo_done.sem, 1)
                prompt_transposed(1)
                dve.wait_ge(oa_hi_done.sem, oa_hi_done.after(layer, 1))
                dve.tensor_tensor(oa_lo[:, :, :], oT, oa_hi[:, :, :].bitcast(F32), ALU.subtract).then_inc(oa_lo_done.sem, 1)

                def merge(i):
                    bank = 4 * (i % 2)
                    dve.wait_ge(slab_used.sem, slab_used.after(layer, PROJ + 2 * i + 2))
                    dve.wait_ge(gates_done.sem, gates_done.after(layer, 2))
                    if i > 1:
                        dve.wait_ge(mg_done.sem, mg_done.after(layer, i - 1))
                    r = z_place(Z_SLABS - DP + i)
                    dve.tensor_tensor(silu[:, i % 2], z[:, r:r + 2, :], ps[:, bank:bank + 2, 0:T], ALU.mult)
                    a = ZGA + 2 * i
                    dve.tensor_tensor(hid_f[:, i % 2], z[:, a:a + 2, :], ps[:, bank + 2:bank + 4, 0:T], ALU.mult).then_inc(proj_read.sem, 1)
                    dve.wait_ge(proj_read.sem, proj_read.after(layer, i + 1))
                    dve.tensor_tensor(hid_f[:, i % 2], hid_f[:, i % 2], silu[:, i % 2], ALU.add).then_inc(merged.sem, 1)

                def merge_lo(i):
                    dve.wait_ge(mg_hi_done.sem, mg_hi_done.after(layer, i + 1))
                    dve.tensor_tensor(mg_lo[:, 2 * i:2 * i + 2, :], hid_f[:, i % 2], mg_hi[:, 2 * i:2 * i + 2, :].bitcast(F32), ALU.subtract)\
                       .then_inc(mg_done.sem, 1)

                for i in range(1, DP):
                    lo_slab(PROJ + 2 * i, 4)
                    merge(i - 1)
                    lo_slab(PROJ + 2 * i + 1, 4)
                    if i > 1:
                        merge_lo(i - 2)
                merge_lo(DP - 2)
                lo_slab(WO)
                lo_slab(WO + 1)
                merge(DP - 1)
                merge_lo(DP - 1)
                lo_slab(WO + 2)
                x_add(0, WO, 0, 1.0)
                rms(2, 0, G_FFN2)
                lo_slab(WO + 3)
                x_add(1, WO + 1, 2, 1.0)
                rms(2, 1, G_FFN2)
                x_add(2, WO + 2, 0, 1.0)
                rms(2, 2, G_FFN2)
                lo_slab(UP2)
                x_add(3, WO + 3, 2, 1.0)
                rms(2, 3, G_FFN2)
                lo_slab(UP2 + 1)
                ffn(1, 2, UP2, DOWN2, None)
                assert links[0] == LINKS, links

            dve.wait_ge(last_tr.sem, 1)
            for t in range(3):
                rows = P if t < 2 else TS
                dve.tensor_copy(stage[0:rows, t, 512:1024], ps[0:rows, 2 * t + 1, :]).then_inc(last_dve.sem, 1)


N_LOADS = 3 + 5 * DEPTH + 4 * DEPTH


_INS = ["x_prompt", "x_sample", "cache_k", "cache_v", "state_ret", "page_table", "g_ffn1", "w1_ffn1", "w3_ffn1", "w2_ffn1",
        "g_mix", "w_in", "g_q", "g_k", "gn_gain", "gn_bias", "w_pa", "w_pr", "w_o", "g_ffn2", "w1_ffn2", "w3_ffn2", "w2_ffn2"]
_OUTS = [(1, SEQ, D_MODEL), (DEC_BATCH, DEC_SEQ, D_MODEL), (DEPTH, 1, SEQ, H_A, D_A), (DEPTH, 1, SEQ, H_A, D_A),
         (DEPTH, 1, H_R, D_R, D_R), (DEPTH, DEC_BATCH, DEC_SEQ, H_A, D_A), (DEPTH, DEC_BATCH, DEC_SEQ, H_A, D_A),
         (DEPTH, DEC_BATCH, H_R, D_R, D_R)]


def kernel(**inputs):
    import concourse.bacc as bacc
    from concourse.bass_utils import run_bass_kernel_spmd

    nc = bacc.Bacc("TRN2", target_bir_lowering=False, num_devices=1)
    arrays = {f"in_{n}": np.ascontiguousarray(inputs[n]) for n in _INS}
    arrays["consts"] = constants()
    args = [nc.dram_tensor(n, a.shape, mybir.dt.from_np(a.dtype), kind="ExternalInput").ap() for n, a in arrays.items()]
    outs = [nc.dram_tensor(f"out_{i}", s, F32, kind="ExternalOutput").ap() for i, s in enumerate(_OUTS)]
    trunk(nc, *args, *outs)
    r = run_bass_kernel_spmd(nc, [arrays], core_ids=[0])
    return tuple(r.results[0][f"out_{i}"] for i in range(len(_OUTS)))
```

```python
from contextlib import ExitStack
import math

import numpy as np
import concourse.bass as bass
from concourse import mybir

F32 = mybir.dt.float32
F32R = mybir.dt.float32r
I32 = mybir.dt.int32
ALU = mybir.AluOpType
ACT = mybir.ActivationFunctionType
AX = mybir.AxisListType.X
ds = bass.ds

P = 128
D_MODEL, D_FF, DEPTH = 1024, 2816, 2
SEQ, DEC_BATCH, DEC_SEQ = 256, 8, 4
TS = DEC_BATCH * DEC_SEQ
T = SEQ + TS
PAST, PAGE, N_POOL = 1024, 128, 80
N_PAGES = PAST // PAGE
H_A, D_A = 8, 64
H_R, D_R = 4, 128
EPS = 1e-6
NEG = -1e30
SCALE_A = D_A ** -0.5

KC = D_MODEL // P
FC = D_FF // P
CW = 2 * P
SLAB = KC * CW
UP_PAIRS = D_FF // CW
DP = D_MODEL // CW
F_PARTS = ((0, 8), (8, 15), (15, 22))

UP1 = 0
DOWN1 = UP1 + 2 * UP_PAIRS
ZIN = DOWN1 + 3 * DP
Z_SLABS = 22
GR1 = Z_SLABS - 2
PROJ = ZIN + Z_SLABS
WO = PROJ + 2 * DP
UP2 = WO + DP
DOWN2 = UP2 + 2 * UP_PAIRS
SLABS = DOWN2 + 3 * DP
assert SLABS % 4 == 2


def slot(n):
    v = n + 2
    return (n % 4, n // 4) if n < PROJ else (v % 4, v // 4 - (v % 4 < 2))



ZQ, ZK, ZV, ZQR, ZKR, ZVR, TOK, ZGR, ZGA, ZN = 0, 4, 8, 12, 16, 20, 24, 40, 44, 52


def z_place(m):
    return 2 * m if m < 12 else 2 * m + (ZGR - 24) if m < 18 else ZV + 2 * (m - 18) if m < 20 else ZVR + 2 * (m - 20)


C_SHAPES = (("ident", 128), ("ones", 128), ("heads", 128), ("causal", 384), ("pastb", P), ("pageb", N_PAGES), ("newb", 2 * TS),
            ("decay", H_R * SEQ), ("kdecay", 3 * H_R), ("qdecay", H_R * TS), ("batch", DEC_BATCH),
            ("rank", 4), ("sdecay", H_R * TS))
C_AT, _at = {}, 0
for _name, _n in C_SHAPES:
    C_AT[_name] = (_at, _n)
    _at += _n
C_N = _at
GL = 3 * KC + 2 * H_R + 2
G_FFN1, G_MIX, G_FFN2, G_GN, G_GB, G_Q, G_K = 0, 8, 16, 24, 28, 32, 33
G_PARTS = ((G_FFN1, KC), (G_MIX, KC), (G_FFN2, KC), (G_GN, H_R), (G_GB, H_R), (G_Q, 1), (G_K, 1))


def slope(h):
    return 2.0 ** (-8.0 * (h + 1.0) / H_A)


def log_decay(h):
    return math.log(1.0 - 2.0 ** (-5.0 - h))


def constants():
    c = {n: np.zeros((P, w), np.float64) for n, w in C_SHAPES}
    r = np.arange(P)
    c["ident"][:] = np.eye(P)
    c["ones"][:] = 1.0
    c["heads"][:] = (r[:, None] // D_A) == (r[None, :] // D_A)
    d = r[None, :] - r[:, None]
    c["causal"][:, 0:P] = np.where(d <= 0, d, -1e32)
    d = np.arange(SEQ)[None, :] - (r[:, None] + P)
    c["causal"][:, P:] = np.where(d <= 0, d, -1e32)
    q, h, jb = r % 4, (r // 4) % H_A, r // 32
    s8 = np.array([8.0 * slope(x) for x in h])
    c["pastb"][:] = s8[:, None] * (r[None, :] - q[:, None])
    c["pageb"][:] = s8[:, None] * (P * np.arange(N_PAGES)[None, :] - PAST)
    for g in range(2):
        for t in range(TS):
            ok = (t // 4 == 4 * g + jb) & (t % 4 <= q)
            c["newb"][:, g * TS + t] = np.where(ok, s8 * (t % 4 - q), NEG)
    ks = D_R ** -0.5
    for hh in range(H_R):
        lg = log_decay(hh)
        d = np.arange(SEQ)[None, :] - r[:, None]
        m = np.where(d >= 0, np.exp(lg * np.maximum(d, 0)), 0.0) * ks
        c["decay"][:, hh * SEQ:(hh + 1) * SEQ] = m
        for t in range(2):
            c["kdecay"][:, t * H_R + hh] = np.exp(lg * (SEQ - 1.0 - (t * P + r))) * ks
        c["kdecay"][:, 2 * H_R + hh] = np.exp(lg * (DEC_SEQ - 1.0 - r % 4)) * ks
        i = np.arange(TS)
        c["qdecay"][:, hh * TS:(hh + 1) * TS] = np.exp(lg * (i % 4 + 1.0))[None, :]
        ok = (r[:, None] // 4 == i[None, :] // 4) & (i[None, :] % 4 >= r[:, None] % 4)
        c["sdecay"][:, hh * TS:(hh + 1) * TS] = np.where(ok, np.exp(lg * np.maximum(i[None, :] % 4 - r[:, None] % 4, 0)), 0) * ks
    c["batch"][:] = (r[:, None] // 4) == np.arange(DEC_BATCH)[None, :]
    c["rank"][:] = np.arange(1, 5)[None, :]
    return np.concatenate([c[n] for n, _ in C_SHAPES], axis=1).astype(np.float32)


class Signal:

    def __init__(self, sem, per_layer, credit=0, step=1):
        self.sem, self.per_layer, self.credit, self.step = sem, per_layer, credit, step

    def after(self, layer, n):
        return (layer * self.per_layer + (n + self.credit)) * self.step


def trunk(nc, x_prompt, x_sample, cache_k, cache_v, state_ret, page_table, g_ffn1, w1_ffn1, w3_ffn1, w2_ffn1,
          g_mix, w_in, g_q, g_k, gn_gain, gn_bias, w_pa, w_pr, w_o, g_ffn2, w1_ffn2, w3_ffn2, w2_ffn2, consts,
          y_prompt, y_sample, k_prompt, v_prompt, state_prompt, k_sample, v_sample, state_sample):
    ctx = ExitStack()
    with ctx:
        def sb(name, shape, dt=F32):
            return ctx.enter_context(nc.sbuf_tensor(name, shape, dt))

        def signal(name, per_layer=1, credit=0, step=1):
            return Signal(ctx.enter_context(nc.semaphore(name)), per_layer, credit, step)

        xT = sb("xT", [P, KC, T])
        h_at = nc.sbuf_base
        h_hi = sb("h_hi", [P, KC, T], F32R)
        h_lo = sb("h_lo", [P, KC, T], F32R)
        w_at = nc.sbuf_base
        w_lo = sb("w_lo", [P, 4, SLAB], F32R)
        raw = nc.alloc_sbuf_tensor_at("raw", [P, 4, SLAB], F32, offset=w_at)
        w_hi = sb("w_hi", [P, 2, SLAB], F32R)
        const = sb("const", [P, C_N])
        gains = sb("gains", [P, DEPTH * GL])
        gain = sb("gain", [P, GL])
        gain_rows = sb("gain_rows", [DEPTH * GL, P])
        pages = sb("pages", [1, DEC_BATCH * N_PAGES], I32)
        pair_buf = sb("pair_buf", [P, 2, 2, 2, T])
        silu, hid_f = pair_buf[:, 0], pair_buf[:, 1]
        rstd = sb("rstd", [P, T])
        kv = sb("kv", [P, 2, 4, H_A * D_A])
        q_blocks = sb("q_blocks", [P, DEC_BATCH, 4, 32])
        mx = sb("mx", [P, 16])
        small = sb("small", [P, 2, 64])
        attn_s = sb("attn_s", [P, 2 * (PAST + TS)])
        work = sb("work", [P, 2, 2048])
        o_all = sb("o_all", [P, 2, 4, T])
        arena = sb("arena", [P, ZN, T], F32R)
        hid_hi, hid_lo = arena[:, 0:FC], arena[:, FC:2 * FC]
        base = nc.sbuf_base - ZN * T * 4
        chunk = 4 * T

        def over(name, shape, dt, at):
            return nc.alloc_sbuf_tensor_at(name, shape, dt, offset=base + at)

        z = over("z", [P, ZN, T], F32, 0)
        v_tok = over("v_tok", [P, 3, 512], F32, TOK * chunk)
        kd_tok = over("kd_tok", [P, 3, 512], F32, TOK * chunk + 6144)
        vr_tok = over("vr_tok", [P, 3, 512], F32, TOK * chunk + 12288)
        oa_hi = over("oa_hi", [P, 4, T], F32R, ZQ * chunk)
        oa_lo = over("oa_lo", [P, 4, T], F32R, ZK * chunk)
        or_hi = over("or_hi", [P, 4, T], F32R, ZQR * chunk)
        or_lo = over("or_lo", [P, 4, T], F32R, ZKR * chunk)
        mg_hi = over("mg_hi", [P, KC, T], F32R, TOK * chunk)
        mg_lo = over("mg_lo", [P, KC, T], F32R, (TOK + KC) * chunk)
        stage = over("stage", [P, 3, D_MODEL], F32, 0)

        k_tok = o_all[:, :, :, :].rearrange("p a c t -> p (a c t)")[:, 0:1536].rearrange("p (t n) -> p t n", t=3)
        oT, orT = o_all[:, 0], o_all[:, 1]
        wk = work[:, :, :].rearrange("p a n -> p (a n)")
        squares = wk[:, 0:KC * T].rearrange("p (c t) -> p c t", c=KC)
        pair_flat = pair_buf[:, :, :, :, :].rearrange("p a b c t -> p (a b c t)")
        qk_squares = pair_flat.rearrange("p (c t) -> p c t", c=8)
        squares_r = pair_flat[:, 0:4 * T].rearrange("p (c t) -> p c t", c=4)
        state_p = pair_flat[:, 4 * T:4 * T + 512].rearrange("p (h e) -> p h e", h=H_R)
        S = attn_s[:, :].rearrange("p (g k) -> p g k", g=2)
        state = attn_s[:, 0:2048].rearrange("p (a b e) -> p a b e", a=2, b=8)
        kT = work[:, :, :].rearrange("p s (j n) -> p s j n", j=4)
        probT = wk[:, 0:2048].rearrange("p (g n r) -> p g n r", g=2, n=N_PAGES)
        probT_new = wk[0:TS, 2048:2304].rearrange("p (g r) -> p g r", g=2)
        v_masked = wk[0:TS, 2304:3328].rearrange("p (b e) -> p b e", b=8)
        probT_p = wk[:, 2304:3840].rearrange("p (h k) -> p h k", h=4)
        h_free = nc.alloc_sbuf_tensor_at("h_free", [P, 2, KC * T], F32, offset=h_at)
        prob_p = [h_free[:, n, 0:1536].rearrange("p (h k) -> p h k", h=4) for n in range(2)]
        inner = [h_free[:, n, 1536:1920] for n in range(2)]
        inner_s = [h_free[0:TS, n, 1920:1952] for n in range(2)]
        q_dec = [h_free[:, n, 1952:1984] for n in range(2)]
        o_sample = (h_free[:, 1, 0:512], kd_tok[:, 0, :])

        def cst(name, lo=0, hi=None):
            at, n = C_AT[name]
            return const[:, at + lo:at + (n if hi is None else hi)]

        ident, ones, heads = cst("ident"), cst("ones"), cst("heads")
        ps = ctx.enter_context(nc.psum_tensor("ps", [P, 8, 512], F32))

        raw_loaded = [signal(f"raw_loaded{s}", sum(slot(n)[0] == s for n in range(SLABS)), 0, 16) for s in range(4)]
        hi_done = signal("hi_done", SLABS)
        split_done = signal("split_done", SLABS)
        slab_used = signal("slab_used", SLABS, 4)
        up_gate = signal("up_gate", 2 * UP_PAIRS)
        silu_done = signal("silu_done", 2 * UP_PAIRS)
        up_read = signal("up_read", 2 * UP_PAIRS, 2)
        up_prod = signal("up_prod", 2 * UP_PAIRS)
        hid_hi_done = signal("hid_hi_done", 2 * UP_PAIRS)
        hid_done = signal("hid_done", 2 * UP_PAIRS)
        x_done = signal("x_done", 3 * DP, DP)
        rms_sq = signal("rms_sq", 12)
        rms_acc = signal("rms_acc", 3)
        rms_sum = signal("rms_sum", 3)
        rms_ln = signal("rms_ln", 3)
        rms_rstd = signal("rms_rstd", 3)
        h_hi_done = signal("h_hi_done", 12)
        h_done = signal("h_done", 12)
        gain_done = signal("gain_done")
        z_done = signal("z_done", Z_SLABS)
        qk_sq, qk_sum, qk_ln, qk_rstd, qk_done = (signal(n, 2) for n in ("qk_sq", "qk_sum", "qk_ln", "qk_rstd", "qk_done"))
        q_blocks_done = signal("q_blocks_done")
        tr_done = signal("tr_done", 4)
        tok_act = signal("tok_act", 3)
        tok_dve = signal("tok_dve", 1)
        kv_stored = signal("kv_stored", 4, 0, 16)
        state_loaded = [signal(f"state_loaded{s}", 2, 0, 16) for s in range(2)]
        state_stored = [signal(f"state_stored{s}", 2, 0, 16) for s in range(2)]
        state_p_stored = signal("state_p_stored", 1, 0, 16)
        inner_done = signal("inner_done", H_R)
        ret_in = signal("ret_in", H_R)
        ret_o = signal("ret_o", H_R)
        ret_masked = signal("ret_masked", H_R)
        ret_o_read = signal("ret_o_read", H_R)
        ret_out = signal("ret_out", H_R)
        ret_act = signal("ret_act", H_R)
        ret_dve = signal("ret_dve", H_R)
        gn_mean, gn_cen, gn_sq, gn_var, gn_ln, gn_rstd = (signal(n) for n in ("gn_mean", "gn_cen", "gn_sq", "gn_var", "gn_ln", "gn_rstd"))
        gr_silu, or_done, or_hi_done, or_lo_done = (signal(n) for n in ("gr_silu", "or_done", "or_hi_done", "or_lo_done"))
        pp_scores, pp_max, pp_exp, pp_norm, pp_tr, pp_tr_act, pp_tr_dve, pp_out, pp_read = (
            signal(n, 2) for n in ("pp_scores", "pp_max", "pp_exp", "pp_norm", "pp_tr", "pp_tr_act", "pp_tr_dve", "pp_out", "pp_read"))
        pp_even = signal("pp_even", 2)
        pp_biased = signal("pp_biased", 2)
        new_scores, new_read = signal("new_scores"), signal("new_read")
        kv_loaded = [signal(f"kv_loaded{s}", 16, 0, 64) for s in range(2)]
        kv_used = signal("kv_used", 64, 4)
        kt_act = signal("kt_act", 32, 1)
        kt_dve = signal("kt_dve", 32, 1)
        pv_evac, pv_tr, pv_out = signal("pv_evac", 2), signal("pv_tr", 2), signal("pv_out", 2)
        sc_done = signal("sc_done", 16, 2)
        sc_read = signal("sc_read", 16, 2)
        sm_bias, sm_exp, sm_norm, sm_tr, sm_tr_act, sm_tr_dve = (
            signal(n, 2) for n in ("sm_bias", "sm_exp", "sm_norm", "sm_tr", "sm_tr_act", "sm_tr_dve"))
        oa_hi_done, oa_lo_done = signal("oa_hi_done"), signal("oa_lo_done")
        gates_done = signal("gates_done", 2)
        proj_read = signal("proj_read", DP, 2)
        merged = signal("merged", DP)
        mg_hi_done = signal("mg_hi_done", DP)
        mg_done = signal("mg_done", DP)
        LINKS = 32
        dve_link = signal("dve_link", LINKS)
        pool_passed = signal("pool_passed")
        x_loaded, gains_loaded, consts_loaded = (signal(n, 1, 0, 16) for n in ("x_loaded", "gains_loaded", "consts_loaded"))
        pages_loaded = signal("pages_loaded", 1, 0, 16)
        first_read = signal("first_read")
        first_tr, gains_done, zeroed = signal("first_tr"), signal("gains_done"), signal("zeroed")
        last_tr, last_act, last_dve, y_stored = signal("last_tr"), signal("last_act"), signal("last_dve"), signal("y_stored", 1, 0, 16)

        def by_chunks(w):
            return w.rearrange("l (k p) f -> l p k f", p=P)

        up = ((by_chunks(w1_ffn1), by_chunks(w3_ffn1)), (by_chunks(w1_ffn2), by_chunks(w3_ffn2)))
        down = (by_chunks(w2_ffn1), by_chunks(w2_ffn2))
        w_in_v, w_pa_v, w_pr_v, w_o_v = (by_chunks(w) for w in (w_in, w_pa, w_pr, w_o))
        k_pages = cache_k.rearrange("l n p h d -> (l n) p (h d)")
        v_pages = cache_v.rearrange("l n p h d -> (l n) p (h d)")

        block = ctx.enter_context(nc.Block())

        @block.sync
        def _(sp):
            def load(layer, q, k, src, chunks, col):
                sp.wait_ge(slab_used.sem, slab_used.after(layer, k - (1 if PROJ <= k < PROJ + 2 else 3)) + q * 4)
                at = slot(k)[0]
                k0, k1 = chunks
                n = k1 - k0
                dst = raw[:, at, 0:n * CW].rearrange("p (k f) -> p k f", k=n)
                sp.dma_start(dst, src[ds(layer, 1), :, k0:k1, ds(col, CW)].rearrange("l p k f -> p (l k) f"))\
                    .then_inc(raw_loaded[at].sem, 16)

            sp.dma_start(stage[:, 0:2, :], x_prompt[0].rearrange("(t p) d -> p t d", p=P)).then_inc(x_loaded.sem, 16)

            with sp.Fori(0, DEPTH) as layer:
                def up_slabs(f, first):
                    for s in range(2):
                        load(layer, 0, first + s, up[f][s], (0, KC), 0)
                    sp.wait_ge(gains_loaded.sem, 16 * 9)
                    with sp.Fori(0, UP_PAIRS // 2) as t:
                        for j in range(4):
                            load(layer, t, first + 2 + j, up[f][j % 2], (0, KC), t * (2 * CW) + (1 + j // 2) * CW)

                def down_slabs(f, first):
                    for n in range(3 * DP):
                        load(layer, 0, first + n, down[f], F_PARTS[n % 3], n // 3 * CW)

                up_slabs(0, UP1)
                down_slabs(0, DOWN1)
                with sp.Fori(0, Z_SLABS // 4) as t:
                    for j in range(4):
                        load(layer, t, ZIN + j, w_in_v, (0, KC), t * (4 * CW) + j * CW)
                for m in range(Z_SLABS - Z_SLABS % 4, Z_SLABS):
                    load(layer, 0, ZIN + m, w_in_v, (0, KC), m * CW)

                def proj_slabs(i):
                    load(layer, 0, PROJ + 2 * i, w_pr_v, (0, 4), i * CW)
                    load(layer, 0, PROJ + 2 * i + 1, w_pa_v, (0, 4), i * CW)

                def load_state(h):
                    src = state_ret[ds(layer, 1), :, h, :, :].rearrange("l b d e -> d (l b) e")
                    sp.dma_start(state[:, h % 2], src).then_inc(state_loaded[h % 2].sem, 16)

                proj_slabs(0)
                sp.wait_ge(sm_tr.sem, sm_tr.after(layer, 2))
                load_state(0)
                load_state(1)
                for h in range(H_R):
                    sp.wait_ge(ret_dve.sem, ret_dve.after(layer, h + 1))
                    sp.dma_start(state_sample[ds(layer, 1), :, h, :, :].rearrange("l b d e -> d (l b) e"),
                                 state[:, h % 2]).then_inc(state_stored[h % 2].sem, 16)
                    if h < 2:
                        sp.wait_ge(state_stored[h].sem, state_stored[h].after(layer, 1))
                        load_state(h + 2)
                sp.wait_ge(ret_act.sem, ret_act.after(layer, H_R))
                sp.dma_start(state_prompt[ds(layer, 1), 0].rearrange("l h d e -> d (l h) e"),
                             state_p).then_inc(state_p_stored.sem, 16)
                for i in range(1, DP):
                    proj_slabs(i)
                for i in range(DP):
                    load(layer, 0, WO + i, w_o_v, (0, KC), i * CW)
                up_slabs(1, UP2)
                down_slabs(1, DOWN2)
            for s in range(2):
                sp.wait_ge(state_stored[s].sem, state_stored[s].after(DEPTH - 1, 2))
            sp.wait_ge(state_p_stored.sem, 16 * DEPTH)

        @block.gpsimd
        def _(pool):
            pool.dma_start(pages[:, :], page_table.rearrange("(o b) n -> o (b n)", o=1)).then_inc(pages_loaded.sem, 16)
            pool.wait_ge(pages_loaded.sem, 16)
            pool.wait_ge(gains_loaded.sem, 16 * 9)
            with pool.Fori(0, DEPTH) as layer:
                def load_unit(cache, g, n, slot, unit):
                    pool.wait_ge(kv_used.sem, kv_used.after(layer, 2 * unit - 2))
                    for j in range(4):
                        page = pool.value_load(pages[0:1, ds(n + (4 * g + j) * N_PAGES, 1)], min_val=0, max_val=N_POOL - 1)
                        pool.dma_start(kv[:, slot, j:j + 1, :], cache[ds(layer * N_POOL + page, 1), :, :].rearrange("a p n -> p a n"))\
                            .then_inc(kv_loaded[slot].sem, 16)

                def wait(signal, n):
                    pool.wait_ge(signal.sem, signal.after(layer, n))
                    pool.sem_inc(pool_passed.sem, 1)

                def load_units(cache, g, first):
                    with pool.Fori(0, N_PAGES // 2) as i:
                        for s in range(2):
                            load_unit(cache, g, i * 2 + s, s, i * 2 + (first + s))

                load_units(k_pages, 0, 0)
                load_units(k_pages, 1, 8)
                wait(tok_act, 1)
                pool.dma_start(v_prompt[ds(layer, 1), 0].rearrange("l (t p) h d -> p (l t) (h d)", p=P),
                               v_tok[:, 0:2, :]).then_inc(kv_stored.sem, 16)
                pool.dma_start(v_sample[ds(layer, 1)].rearrange("l b s h d -> (l b s) (h d)"),
                               v_tok[0:TS, 2, :]).then_inc(kv_stored.sem, 16)
                wait(tok_act, 3)
                pool.dma_start(k_prompt[ds(layer, 1), 0].rearrange("l (t p) h d -> p (l t) (h d)", p=P),
                               k_tok[:, 0:2, :]).then_inc(kv_stored.sem, 16)
                pool.dma_start(k_sample[ds(layer, 1)].rearrange("l b s h d -> (l b s) (h d)"),
                               k_tok[0:TS, 2, :]).then_inc(kv_stored.sem, 16)
                load_units(v_pages, 0, 16)
                load_units(v_pages, 1, 24)
            pool.wait_ge(kv_stored.sem, kv_stored.after(DEPTH - 1, 4))
            pool.wait_ge(last_act.sem, 3)
            pool.wait_ge(last_dve.sem, 3)
            pool.dma_start(y_prompt[0].rearrange("(t p) d -> p t d", p=P), stage[:, 0:2, :]).then_inc(y_stored.sem, 16)
            pool.dma_start(y_sample.rearrange("b s d -> (b s) d"), stage[0:TS, 2, :]).then_inc(y_stored.sem, 16)
            pool.wait_ge(y_stored.sem, 32)

        @block.scalar
        def _(act):
            n_first = C_AT["ones"][0] + C_AT["ones"][1]
            for dst, src in ((const[:, 0:n_first], consts[:, 0:n_first]),
                             (stage[0:TS, 2, :], x_sample.rearrange("b s d -> (b s) d"))):
                act.dma_start(dst, src).then_inc(x_loaded.sem, 16)
            for (row, n), arr in zip(G_PARTS, (g_ffn1, g_mix, g_ffn2, gn_gain, gn_bias)):
                act.dma_start(gain_rows[DEPTH * row:DEPTH * (row + n), :], arr.rearrange("l (c p) -> (l c) p", p=P)).then_inc(gains_loaded.sem, 16)
            for (row, n), arr in zip(G_PARTS[5:], (g_q, g_k)):
                for half in range(2):
                    act.dma_start(gain_rows[DEPTH * row:DEPTH * (row + 1), half * D_A:(half + 1) * D_A], arr).then_inc(gains_loaded.sem, 16)
            act.dma_start(const[:, n_first:], consts[:, n_first:]).then_inc(consts_loaded.sem, 16)

            with act.Fori(0, DEPTH) as layer:
                def hi(q, k, chunks=KC):
                    at, before = slot(k)
                    act.wait_ge(raw_loaded[at].sem, raw_loaded[at].after(layer, q + (before + 1)))
                    act.wait_ge(slab_used.sem, slab_used.after(layer, k - 1) + q * 4)
                    act.activation(w_hi[:, k % 2, 0:chunks * CW], raw[:, at, 0:chunks * CW], ACT.Copy).then_inc(hi_done.sem, 1)

                def hi_slab(n, chunks=KC):
                    hi(0, n, chunks)

                def rms(r, i, g0):
                    act.wait_ge(x_done.sem, x_done.after(layer, DP * r - DP + i + 1))
                    for c in (2 * i, 2 * i + 1):
                        last = act.activation(h_hi[:, c, :], xT[:, c, :], ACT.Copy, scale=gain[:, g0 + c:g0 + c + 1])
                    last.then_inc(h_hi_done.sem, 1)

                def rms_square(r, i):
                    act.activation(squares[:, 2 * i:2 * i + 2, :], xT[:, 2 * i:2 * i + 2, :], ACT.Square).then_inc(rms_sq.sem, 1)

                def rms_end(r):
                    act.wait_ge(rms_sum.sem, rms_sum.after(layer, r + 1))
                    act.activation(rstd[:, :], ps[:, 7, 0:T], ACT.Ln, bias=eps_col, scale=1.0 / D_MODEL).then_inc(rms_ln.sem, 1)
                    act.wait_ge(rms_ln.sem, rms_ln.after(layer, r + 1))
                    act.activation(rstd[:, :], rstd[:, :], ACT.Exp, scale=-0.5).then_inc(rms_rstd.sem, 1)

                def up_silu(f, i, buf):
                    act.wait_ge(up_gate.sem, up_gate.after(layer, f * UP_PAIRS + 1) + i)
                    act.activation(silu[:, buf], silu[:, buf], ACT.Silu).then_inc(silu_done.sem, 1)

                def up_hi(f, i, buf):
                    act.wait_ge(up_prod.sem, up_prod.after(layer, f * UP_PAIRS + 1) + i)
                    act.activation(hid_hi[:, ds(i * 2, 2), :], hid_f[:, buf], ACT.Copy).then_inc(hid_hi_done.sem, 1)

                def ffn(f, r, first_up, first_down, rms_next):
                    hi_slab(first_up + 2)
                    rms_end(r)
                    with act.Fori(0, UP_PAIRS // 2) as t:
                        for b in range(2):
                            i = t * 2 + b
                            up_silu(f, i, b)
                            hi(t, first_up + 2 * b + 3)
                            up_hi(f, i, b)
                            hi(t, first_up + 2 * b + 4)
                    up_silu(f, UP_PAIRS - 1, 0)
                    hi_slab(first_down + 1, 7)
                    up_hi(f, UP_PAIRS - 1, 0)
                    hi_slab(first_down + 2, 7)
                    for i in range(1, DP):
                        hi_slab(first_down + 3 * i, 8)
                        hi_slab(first_down + 3 * i + 1, 7)
                        if rms_next:
                            rms_next(i - 1)
                            rms_square(r + 1, i - 1)
                        hi_slab(first_down + 3 * i + 2, 7)
                    if rms_next:
                        hi_slab(first_down + 3 * DP)
                        rms_next(DP - 1)
                        hi_slab(first_down + 3 * DP + 1)
                        rms_square(r + 1, DP - 1)

                eps_col = EPS
                hi_slab(UP1)
                act.wait_ge(gain_done.sem, layer + 1)
                for i in range(DP - 1):
                    rms(0, i, G_FFN1)
                    rms_square(0, i)
                rms(0, DP - 1, G_FFN1)
                hi_slab(UP1 + 1)
                rms_square(0, DP - 1)
                ffn(0, 0, UP1, DOWN1, lambda i: rms(1, i, G_MIX))

                hi_slab(ZIN + 2)
                rms_end(1)
                hi_slab(ZIN + 3)

                def qk_square(n):
                    act.wait_ge(z_done.sem, z_done.after(layer, 2 * n + 2))
                    act.activation(qk_squares[:, 4 * n:4 * n + 4], z[:, 4 * n:4 * n + 4, :], ACT.Square).then_inc(qk_sq.sem, 1)

                def qk_root(n):
                    act.wait_ge(qk_sum.sem, qk_sum.after(layer, n + 1))
                    act.activation(qk_squares[:, 4 * n:4 * n + 4], ps[:, 4:8, 0:T], ACT.Ln, bias=eps_col, scale=1.0 / D_A).then_inc(qk_ln.sem, 1)
                    act.wait_ge(qk_ln.sem, qk_ln.after(layer, n + 1))
                    act.activation(qk_squares[:, 4 * n:4 * n + 4], qk_squares[:, 4 * n:4 * n + 4], ACT.Exp, scale=-0.5).then_inc(qk_rstd.sem, 1)

                qk_square(0)
                hi_slab(ZIN + 4)
                qk_root(0)

                def unit_step(g, t, b, s):
                    i = t * 2 + b
                    hi(t, ZIN + 5 + 8 * g + 2 * b + s)
                    act.wait_ge(sc_done.sem, sc_done.after(layer, 8 * g + s - 1) + i * 2)
                    for half in range(2):
                        act.wait_ge(kv_used.sem, kv_used.after(layer, 16 * g + 2 * s + half + 1) + i * 4)
                        act.activation(kT[:, s, 2 * half, :], ps[:, 4, :], ACT.Copy).then_inc(kt_act.sem, 1)

                with act.Fori(0, N_PAGES // 4) as t:
                    for n in range(4):
                        unit_step(0, t, n // 2, n % 2)

                qk_square(1)
                qk_root(1)
                for tr, bank, tok in ((0, 0, v_tok), (1, 4, vr_tok), (3, 4, k_tok)):
                    act.wait_ge(tr_done.sem, tr_done.after(layer, tr + 1))
                    act.activation(tok[:, 0:2, :], ps[:, bank:bank + 2, :], ACT.Copy)
                    act.activation(tok[0:TS, 2, :], ps[0:TS, bank + 2, :], ACT.Copy).then_inc(tok_act.sem, 1)

                for n in range(6):
                    unit_step(1, n // 4, n // 2 % 2, n % 2)

                def sample_exp(g):
                    act.wait_ge(sm_bias.sem, sm_bias.after(layer, g + 1))
                    for n in range(5):
                        cols = slice(256 * n, min(256 * n + 256, PAST + TS))
                        last = act.activation(S[:, g, cols], S[:, g, cols], ACT.Exp, bias=small[:, g, 8 + n:9 + n],
                                              scale=SCALE_A, accum_out=small[:, g, 16 + n:17 + n])
                    last.then_inc(sm_exp.sem, 1)

                def sample_transposed(g):
                    act.wait_ge(sm_tr.sem, sm_tr.after(layer, g + 1))
                    act.activation(probT[:, g].rearrange("p n r -> p (n r)").rearrange("p (a m) -> p a m", a=2),
                                   ps[:, 4:6, :], ACT.Copy).then_inc(sm_tr_act.sem, 1)

                unit_step(1, 1, 1, 0)
                sample_exp(0)
                unit_step(1, 1, 1, 1)
                sample_transposed(0)
                hi_slab(ZIN + GR1 + 1)
                sample_exp(1)
                hi_slab(PROJ, 4)
                act.wait_ge(z_done.sem, z_done.after(layer, 14))
                act.activation(z[:, ZGR:ZGR + 4, :], z[:, ZGR:ZGR + 4, :], ACT.Silu).then_inc(gr_silu.sem, 1)
                sample_transposed(1)
                hi_slab(PROJ + 1, 4)

                def heads_out(g):
                    act.wait_ge(pv_tr.sem, pv_tr.after(layer, g + 1))
                    for half in range(2):
                        rows = slice(64 * half, 64 * half + 64)
                        src = ps[rows, (5, 7)[g], :].rearrange("p (c j h q) -> p c j h q", c=4, j=4, q=4)[:, :, :, half, :]
                        last = act.activation(oT[rows, :, SEQ + 16 * g:SEQ + 16 * g + 16].rearrange("p c (j q) -> p c j q", j=4),
                                              src, ACT.Copy)
                    last.then_inc(pv_out.sem, 1)

                act.wait_ge(kv_stored.sem, kv_stored.after(layer, 4))
                for h in range(H_R):
                    act.wait_ge(ret_o.sem, ret_o.after(layer, h + 1))
                    act.activation(orT[:, h, :], ps[:, 1, 0:T], ACT.Copy).then_inc(ret_o_read.sem, 1)
                    act.wait_ge(ret_out.sem, ret_out.after(layer, h + 1))
                    act.activation(state_p[:, h, :], ps[:, 2, 0:P], ACT.Copy).then_inc(ret_act.sem, 1)
                    if h == 2:
                        heads_out(0)
                    if h == 0:
                        act.wait_ge(z_done.sem, z_done.after(layer, 18))
                        act.activation(z[:, ZGA:ZGA + KC, :], z[:, ZGA:ZGA + KC, :], ACT.Sigmoid).then_inc(gates_done.sem, 1)
                    if h == 1:
                        act.wait_ge(z_done.sem, z_done.after(layer, Z_SLABS))
                        act.activation(z[:, ZV:ZV + 4, :], z[:, ZV:ZV + 4, :], ACT.Sigmoid)
                        act.activation(z[:, ZVR:ZVR + 4, :], z[:, ZVR:ZVR + 4, :], ACT.Sigmoid).then_inc(gates_done.sem, 1)

                def prompt_exp(hb):
                    act.wait_ge(pp_max.sem, pp_max.after(layer, hb + 1))
                    for i in range(8):
                        hi_, tile = i % 4, i // 4
                        cols = slice(0, P) if tile == 0 else slice(P, 3 * P)
                        last = act.activation(prob_p[hb][:, hi_, cols], prob_p[hb][:, hi_, cols], ACT.Exp,
                                              bias=mx[:, 8 * hb + i:8 * hb + i + 1],
                                              scale=SCALE_A, accum_out=small[:, hb, i:i + 1])
                    last.then_inc(pp_exp.sem, 1)

                def prompt_transposed(hb):
                    act.wait_ge(pp_tr.sem, pp_tr.after(layer, hb + 1))
                    if hb:
                        act.wait_ge(pp_out.sem, pp_out.after(layer, hb))
                    act.activation(probT_p[:, :, :].rearrange("p h k -> p (h k)")[:, 0:512], ps[:, 0, :], ACT.Copy).then_inc(pp_tr_act.sem, 1)

                def prompt_out(hb):
                    act.wait_ge(pp_out.sem, pp_out.after(layer, hb + 1))
                    act.activation(oT[:, 2 * hb:2 * hb + 2, 0:SEQ], ps[:, 3, :].rearrange("p (c t) -> p c t", c=2), ACT.Copy)\
                       .then_inc(pp_read.sem, 1)

                prompt_exp(0)
                act.wait_ge(gn_cen.sem, gn_cen.after(layer, 1))
                act.activation(squares_r, orT, ACT.Square).then_inc(gn_sq.sem, 1)
                act.wait_ge(gn_var.sem, gn_var.after(layer, 1))
                act.activation(squares_r, ps[:, 0:4, 0:T], ACT.Ln, bias=eps_col, scale=1.0 / D_R).then_inc(gn_ln.sem, 1)
                act.wait_ge(gn_ln.sem, gn_ln.after(layer, 1))
                act.activation(squares_r, squares_r, ACT.Exp, scale=-0.5).then_inc(gn_rstd.sem, 1)
                prompt_transposed(0)
                prompt_exp(1)
                prompt_out(0)
                prompt_transposed(1)
                heads_out(1)
                act.wait_ge(or_done.sem, or_done.after(layer, 1))
                act.activation(or_hi[:, :, :], orT, ACT.Copy).then_inc(or_hi_done.sem, 1)
                prompt_out(1)
                act.wait_ge(pp_read.sem, pp_read.after(layer, 2))
                act.wait_ge(pv_out.sem, pv_out.after(layer, 2))
                act.activation(oa_hi[:, :, :], oT, ACT.Copy).then_inc(oa_hi_done.sem, 1)

                def merge_hi(i):
                    act.wait_ge(merged.sem, merged.after(layer, i + 1))
                    act.activation(mg_hi[:, 2 * i:2 * i + 2, :], hid_f[:, i % 2], ACT.Copy).then_inc(mg_hi_done.sem, 1)

                for i in range(1, DP):
                    hi_slab(PROJ + 2 * i, 4)
                    hi_slab(PROJ + 2 * i + 1, 4)
                    if i > 1:
                        merge_hi(i - 2)
                hi_slab(WO)
                merge_hi(DP - 2)
                merge_hi(DP - 1)
                hi_slab(WO + 1)
                hi_slab(WO + 2)
                rms(2, 0, G_FFN2)
                rms_square(2, 0)
                hi_slab(WO + 3)
                rms(2, 1, G_FFN2)
                rms_square(2, 1)
                hi_slab(UP2)
                rms(2, 2, G_FFN2)
                rms_square(2, 2)
                rms(2, 3, G_FFN2)
                hi_slab(UP2 + 1)
                rms_square(2, 3)
                ffn(1, 2, UP2, DOWN2, None)

            act.wait_ge(last_tr.sem, 1)
            for t in range(3):
                rows = P if t < 2 else TS
                act.activation(stage[0:rows, t, 0:512], ps[0:rows, 2 * t, :], ACT.Copy).then_inc(last_act.sem, 1)

        @block.tensor
        def _(pe):
            def triple(out, w, wl, x, xl, start, stop):
                pe.matmul(out, w, x, start=start, stop=False)
                pe.matmul(out, wl, x, start=False, stop=False)
                return pe.matmul(out, w, xl, start=False, stop=stop)

            pe.wait_ge(x_loaded.sem, 16 * 3)
            for c in range(KC):
                for t in range(3):
                    rows = P if t < 2 else TS
                    last = pe.transpose(ps[:, c, t * P:t * P + rows], stage[0:rows, t, c * P:(c + 1) * P], ident[0:rows, 0:rows])
                if c % 2:
                    last.then_inc(first_tr.sem, 1)
            pe.wait_ge(gains_loaded.sem, 16 * 9)
            pe.wait_ge(first_read.sem, 1)
            pe.transpose(ps[:, 0, 0:DEPTH * GL], gain_rows[:, :], ident[0:DEPTH * GL, 0:DEPTH * GL]).then_inc(first_tr.sem, 1)
            pe.wait_ge(gains_done.sem, 1)

            with pe.Fori(0, DEPTH) as layer:
                def half_slab(q, n, t, bank, hi, lo, k0, chunks, start=True, stop=True):
                    if t == 0:
                        pe.wait_ge(split_done.sem, split_done.after(layer, n + 1) + q * 4)
                    for k in range(chunks):
                        cols = slice(k * CW + t * P, k * CW + t * P + P)
                        last = triple(ps[:, bank + t, 0:T], w_hi[:, n % 2, cols], w_lo[:, slot(n)[0], cols],
                                      hi[:, k0 + k, :], lo[:, k0 + k, :], start and k == 0, stop and k == chunks - 1)
                    if t == 1:
                        last.then_inc(slab_used.sem, 1)

                def slab(q, n, bank, hi, lo, k0, chunks, start=True, stop=True):
                    for t in range(2):
                        half_slab(q, n, t, bank, hi, lo, k0, chunks, start, stop)

                def slab_by_chunks(n, bank, hi, lo, ready, before):
                    pe.wait_ge(split_done.sem, split_done.after(layer, n + 1))
                    for k in range(KC):
                        if k % 2 == 0:
                            pe.wait_ge(ready.sem, ready.after(layer, before + k // 2 + 1))
                        for t in range(2):
                            cols = slice(k * CW + t * P, k * CW + t * P + P)
                            last = triple(ps[:, bank + t, 0:T], w_hi[:, n % 2, cols], w_lo[:, slot(n)[0], cols],
                                          hi[:, k, :], lo[:, k, :], k == 0, k == KC - 1)
                    last.then_inc(slab_used.sem, 1)

                def first_slabs(r, first):
                    slab_by_chunks(first, 0, h_hi, h_lo, h_done, 4 * r)
                    half_slab(0, first + 1, 0, 2, h_hi, h_lo, 0, KC)
                    pe.wait_ge(rms_acc.sem, rms_acc.after(layer, r + 1))
                    for c in range(2):
                        last = pe.matmul(ps[:, 7, 0:T], ones, squares[:, c, :], start=c == 0, stop=c == 1)
                    last.then_inc(rms_sum.sem, 1)
                    half_slab(0, first + 1, 1, 2, h_hi, h_lo, 0, KC)

                def ffn(f, r, first_up, first_down):
                    def up_pair(t, j):
                        i, buf = t * 2 + j, j % 2
                        pe.wait_ge(up_read.sem, up_read.after(layer, f * UP_PAIRS - 1) + i)
                        for s in range(2):
                            if buf and s:
                                pe.wait_ge(rms_ln.sem, rms_ln.after(layer, r + 1))
                            slab(t, first_up + 2 * j + s, 4 * buf + 2 * s, h_hi, h_lo, 0, KC)

                    pe.wait_ge(up_read.sem, up_read.after(layer, f * UP_PAIRS - 1))
                    first_slabs(r, first_up)
                    with pe.Fori(0, UP_PAIRS // 2) as t:
                        up_pair(t, 1)
                        up_pair(t, 2)
                    for n in range(3 * DP):
                        k0, k1 = F_PARTS[n % 3]
                        if n % 3 == 0:
                            pe.wait_ge(x_done.sem, x_done.after(layer, (0, 2 * DP)[f] + n // 3 - 1))
                        if n == 0:
                            pe.wait_ge(up_read.sem, up_read.after(layer, f * UP_PAIRS + UP_PAIRS - 1))
                        pe.wait_ge(hid_done.sem, hid_done.after(layer, f * UP_PAIRS + (k1 + 1) // 2))
                        slab(0, first_down + n, 4 + 2 * (n // 3 % 2), hid_hi, hid_lo, k0, k1 - k0, n % 3 == 0, n % 3 == 2)

                ffn(0, 0, UP1, DOWN1)

                first_slabs(1, ZIN)

                def z_free(m):
                    pe.wait_ge(z_done.sem, z_done.after(layer, m - 1))

                z_free(2)
                slab(0, ZIN + 2, 0, h_hi, h_lo, 0, KC)

                def qk_sums(n):
                    pe.wait_ge(qk_sq.sem, qk_sq.after(layer, n + 1))
                    for c in range(4):
                        last = pe.matmul(ps[:, 4 + c, 0:T], heads, qk_squares[:, 4 * n + c, :], start=True, stop=True)
                    last.then_inc(qk_sum.sem, 1)

                pe.wait_ge(rms_ln.sem, rms_ln.after(layer, 2))
                pe.wait_ge(consts_loaded.sem, 16)
                qk_sums(0)
                z_free(3)
                slab(0, ZIN + 3, 2, h_hi, h_lo, 0, KC)

                def unit_step(g, t, b, s):
                    i = t * 2 + b

                    def transposes(half):
                        pe.wait_ge(kt_act.sem, kt_act.after(layer, 16 * g + 2 * s + half) + i * 4)
                        pe.wait_ge(kt_dve.sem, kt_dve.after(layer, 16 * g + 2 * s + half) + i * 4)
                        for j in range(2):
                            for c in range(4):
                                last = pe.transpose(ps[:, 4 + j, c * P:(c + 1) * P], kv[:, s, 2 * half + j, c * P:(c + 1) * P], ident)
                        last.then_inc(kv_used.sem, 1)

                    pe.wait_ge(kv_loaded[s].sem, (layer * 16 + i + (4 * g + 1)) * 64)
                    if g == 0:
                        pe.wait_ge(qk_ln.sem, qk_ln.after(layer, 1))
                    else:
                        pe.wait_ge(tok_act.sem, tok_act.after(layer, 3))
                        pe.wait_ge(tok_dve.sem, tok_dve.after(layer, 1))
                        pe.wait_ge(new_read.sem, new_read.after(layer, 1))
                    pe.wait_ge(z_done.sem, z_done.after(layer, 3 + 8 * g + s) + i * 2)
                    for half in range(2):
                        transposes(half)
                        half_slab(t, ZIN + 4 + 8 * g + 2 * b + s, half, 2 * s, h_hi, h_lo, 0, KC)
                    pe.wait_ge(kt_act.sem, kt_act.after(layer, 16 * g + 2 * s + 2) + i * 4)
                    pe.wait_ge(kt_dve.sem, kt_dve.after(layer, 16 * g + 2 * s + 2) + i * 4)
                    pe.wait_ge(q_blocks_done.sem, q_blocks_done.after(layer, 1))
                    pe.wait_ge(sc_read.sem, sc_read.after(layer, 8 * g + s - 1) + i * 2)
                    for c in range(4):
                        for j in range(4):
                            last = pe.matmul(ps[32 * j:32 * j + 32, 6 + s, 0:P], q_blocks[:, 4 * g + j, c, :],
                                             kT[:, s, j, c * P:(c + 1) * P], start=c == 0, stop=c == 3)
                    last.then_inc(sc_done.sem, 1)

                with pe.Fori(0, N_PAGES // 4) as t:
                    for n in range(4):
                        unit_step(0, t, n // 2, n % 2)

                pe.wait_ge(kt_act.sem, kt_act.after(layer, 16))
                pe.wait_ge(kt_dve.sem, kt_dve.after(layer, 16))
                pe.wait_ge(sc_read.sem, sc_read.after(layer, 8))
                qk_sums(1)

                def token_major(zc, bank):
                    for c in range(4):
                        for t in range(3):
                            rows = P if t < 2 else TS
                            last = pe.transpose(ps[0:rows, bank + t, c * P:(c + 1) * P], z[:, zc + c, t * P:t * P + rows], ident)
                    last.then_inc(tr_done.sem, 1)

                pe.wait_ge(z_done.sem, z_done.after(layer, 12))
                token_major(ZV, 0)
                pe.wait_ge(qk_ln.sem, qk_ln.after(layer, 2))
                token_major(ZVR, 4)
                pe.wait_ge(tok_act.sem, tok_act.after(layer, 1))
                token_major(ZKR, 0)
                pe.wait_ge(qk_done.sem, qk_done.after(layer, 2))
                for g in range(2):
                    for c in range(4):
                        for j in range(4):
                            last = pe.matmul(ps[32 * j:32 * j + 32, 7, g * TS:(g + 1) * TS], q_blocks[:, 4 * g + j, c, :],
                                             z[:, ZK + c, SEQ:T], start=c == 0, stop=c == 3)
                last.then_inc(new_scores.sem, 1)
                pe.wait_ge(tok_act.sem, tok_act.after(layer, 2))
                token_major(ZK, 4)

                for n in range(N_PAGES):
                    unit_step(1, n // 4, n // 2 % 2, n % 2)

                def transpose_probs(g):
                    pe.wait_ge(sm_norm.sem, sm_norm.after(layer, g + 1))
                    for n in range(N_PAGES):
                        pe.transpose(ps[:, 4 + n // 4, (n % 4) * P:(n % 4 + 1) * P], S[:, g, n * P:(n + 1) * P], ident)
                    pe.transpose(ps[0:TS, 6, 0:P], S[:, g, PAST:PAST + TS], ident).then_inc(sm_tr.sem, 1)

                def value_units(g, first, last_):
                    if first == 0:
                        pe.wait_ge(sm_tr_act.sem, sm_tr_act.after(layer, g + 1))
                        pe.wait_ge(sm_tr_dve.sem, sm_tr_dve.after(layer, g + 1))
                        if g:
                            pe.wait_ge(pv_evac.sem, pv_evac.after(layer, g))
                        pe.matmul(ps[:, 7, :], probT_new[:, g, :], v_tok[0:TS, 2, :], start=True, stop=False, skip_group_check=True)
                    for n in range(first, last_):
                        pe.wait_ge(kv_loaded[n % 2].sem, kv_loaded[n % 2].after(layer, 0) + (8 + 4 * g + n // 2 + 1) * 64)
                        for j in range(4):
                            rows = slice(32 * j, 32 * j + 32)
                            last = pe.matmul(ps[rows, 7, :], probT[:, g, n, rows], kv[:, n % 2, j, :],
                                             start=False, stop=n == N_PAGES - 1, skip_group_check=True)
                            if j % 2:
                                last.then_inc(kv_used.sem, 1)

                pe.wait_ge(kt_act.sem, kt_act.after(layer, 32))
                pe.wait_ge(kt_dve.sem, kt_dve.after(layer, 32))
                pe.wait_ge(sc_read.sem, sc_read.after(layer, 16))
                transpose_probs(0)
                z_free(GR1)
                for half in range(2):
                    half_slab(0, ZIN + GR1, half, 0, h_hi, h_lo, 0, KC)
                    value_units(0, half, half + 1)
                z_free(GR1 + 1)
                half_slab(0, ZIN + GR1 + 1, 0, 2, h_hi, h_lo, 0, KC)
                value_units(0, 2, 3)
                half_slab(0, ZIN + GR1 + 1, 1, 2, h_hi, h_lo, 0, KC)
                pe.wait_ge(sm_tr_act.sem, sm_tr_act.after(layer, 1))
                pe.wait_ge(sm_tr_dve.sem, sm_tr_dve.after(layer, 1))
                transpose_probs(1)

                def values_transposed(g):
                    pe.wait_ge(pv_evac.sem, pv_evac.after(layer, g + 1))
                    for c in range(4):
                        last = pe.transpose(ps[:, (5, 7)[g], c * (P - 8):c * (P - 8) + P], o_sample[g][:, c * P:(c + 1) * P], ident)
                    last.then_inc(pv_tr.sem, 1)

                def ret_inner(h):
                    if h:
                        pe.wait_ge(ret_in.sem, ret_in.after(layer, h))
                    else:
                        pe.wait_ge(z_done.sem, z_done.after(layer, Z_SLABS - 1))
                    kr, qr = z[:, ZKR + h, :], z[:, ZQR + h, :]
                    pe.matmul(ps[:, 0, 0:256], kr[:, 0:P], qr[:, 0:SEQ], start=True, stop=True)
                    pe.matmul(ps[:, 0, 256:384], kr[:, P:SEQ], qr[:, P:SEQ], start=True, stop=True)
                    pe.matmul(ps[0:TS, 0, 384:384 + TS], kr[:, SEQ:T], qr[:, SEQ:T], start=True, stop=True).then_inc(inner_done.sem, 1)

                def ret_outputs(h):
                    pe.wait_ge(ret_in.sem, ret_in.after(layer, h + 1))
                    if h:
                        pe.wait_ge(ret_o_read.sem, ret_o_read.after(layer, h))
                    cols = slice(h * D_R, (h + 1) * D_R)
                    inn, inn_s, qd = inner[h % 2], inner_s[h % 2], q_dec[h % 2]
                    pe.matmul(ps[:, 1, 0:P], vr_tok[:, 0, cols], inn[:, 0:P], start=True, stop=True)
                    pe.matmul(ps[:, 1, P:SEQ], vr_tok[:, 0, cols], inn[:, P:SEQ], start=True, stop=False)
                    pe.matmul(ps[:, 1, P:SEQ], vr_tok[:, 1, cols], inn[:, SEQ:384], start=False, stop=True)
                    pe.matmul(ps[:, 1, SEQ:T], vr_tok[0:TS, 2, cols], inn_s, start=True, stop=True, skip_group_check=True)
                    pe.wait_ge(state_loaded[h % 2].sem, state_loaded[h % 2].after(layer, h // 2 + 1))
                    for b in range(DEC_BATCH):
                        last = pe.matmul(ps[:, 1, SEQ + 4 * b:SEQ + 4 * b + 4], state[:, h % 2, b, :], qd[:, 4 * b:4 * b + 4],
                                         start=False, stop=True, skip_group_check=True)
                    last.then_inc(ret_o.sem, 1)

                def ret_states(h):
                    pe.wait_ge(ret_masked.sem, ret_masked.after(layer, h + 1))
                    if h:
                        pe.wait_ge(ret_act.sem, ret_act.after(layer, h))
                        pe.wait_ge(ret_dve.sem, ret_dve.after(layer, h))
                    else:
                        pe.wait_ge(z_done.sem, z_done.after(layer, Z_SLABS))
                        pe.wait_ge(sm_tr_act.sem, sm_tr_act.after(layer, 2))
                    cols = slice(h * D_R, (h + 1) * D_R)
                    for t in range(2):
                        pe.matmul(ps[:, 2, 0:P], kd_tok[:, t, cols], vr_tok[:, t, cols], start=t == 0, stop=t == 1)
                    for n in range(2):
                        last = pe.matmul(ps[:, 3 + n, :], kd_tok[0:TS, 2, cols], v_masked[:, 4 * n:4 * n + 4, :], start=True, stop=True)
                    last.then_inc(ret_out.sem, 1)

                ret_inner(0)
                value_units(0, 3, 4)
                for h in range(H_R):
                    n = 2 * (h % 2) + 4 * (1 - h // 2)
                    if h + 1 < H_R:
                        ret_inner(h + 1)
                    ret_outputs(h)
                    value_units(h // 2, n, n + 1)
                    if h == 2:
                        values_transposed(0)
                    ret_states(h)
                    value_units(h // 2, n + 1, n + 2)

                def score_pieces(i):
                    return ps[:, 6, i * P:(i + 1) * P], ps[:, 4 + i % 2, i // 2 * SEQ:(i // 2 + 1) * SEQ]

                def prompt_scores(hb):
                    if hb == 0:
                        pe.wait_ge(ret_dve.sem, ret_dve.after(layer, H_R))
                        pe.wait_ge(pv_out.sem, pv_out.after(layer, 1))
                    else:
                        pe.wait_ge(pp_biased.sem, pp_biased.after(layer, hb))
                    for i in (0, 2, 1, 3):
                        h = 4 * hb + i
                        rows = slice(64 * (h % 2), 64 * (h % 2) + 64)
                        q, k = z[rows, ZQ + h // 2, :], z[rows, ZK + h // 2, :]
                        near, far = score_pieces(i)
                        if i == 1:
                            pe.wait_ge(pp_even.sem, pp_even.after(layer, hb + 1))
                        last = pe.matmul(near, q[:, 0:P], k[:, 0:P], start=True, stop=True)
                        if i == 2:
                            last.then_inc(pp_even.sem, 1)
                        last = pe.matmul(far, q[:, P:SEQ], k[:, 0:SEQ], start=True, stop=True)
                    last.then_inc(pp_scores.sem, 1)

                def prompt_probs(hb):
                    pe.wait_ge(pp_norm.sem, pp_norm.after(layer, hb + 1))
                    if hb == 0:
                        pe.wait_ge(gn_ln.sem, gn_ln.after(layer, 1))
                    else:
                        pe.wait_ge(pp_tr_act.sem, pp_tr_act.after(layer, hb))
                        pe.wait_ge(pp_tr_dve.sem, pp_tr_dve.after(layer, hb))
                    for i in range(4):
                        for t in range(3):
                            n = 3 * i + t
                            last = pe.transpose(ps[:, n // 4, n % 4 * P:(n % 4 + 1) * P], prob_p[hb][:, i, t * P:(t + 1) * P], ident)
                    last.then_inc(pp_tr.sem, 1)

                def prompt_out(hb):
                    pe.wait_ge(pp_tr_act.sem, pp_tr_act.after(layer, hb + 1))
                    pe.wait_ge(pp_tr_dve.sem, pp_tr_dve.after(layer, hb + 1))
                    if hb:
                        pe.wait_ge(pp_read.sem, pp_read.after(layer, hb))
                    for i in range(4):
                        h = 4 * hb + i
                        out = ps[64 * (i % 2):64 * (i % 2) + 64, 3, (i // 2) * SEQ:(i // 2 + 1) * SEQ]
                        cols = slice(h * D_A, (h + 1) * D_A)
                        pe.matmul(out[:, 0:P], v_tok[:, 0, cols], probT_p[:, i, 0:P], start=True, stop=True)
                        pe.matmul(out[:, P:SEQ], v_tok[:, 0, cols], probT_p[:, i, P:SEQ], start=True, stop=False)
                        last = pe.matmul(out[:, P:SEQ], v_tok[:, 1, cols], probT_p[:, i, SEQ:384], start=False, stop=True)
                    last.then_inc(pp_out.sem, 1)

                prompt_scores(0)
                pe.wait_ge(ret_act.sem, ret_act.after(layer, H_R))
                for h in range(H_R):
                    last = pe.matmul(ps[:, h, 0:T], ones, orT[:, h, :], start=True, stop=True)
                last.then_inc(gn_mean.sem, 1)
                value_units(1, 4, 5)
                prompt_scores(1)
                value_units(1, 5, 6)
                pe.wait_ge(gn_sq.sem, gn_sq.after(layer, 1))
                for h in range(H_R):
                    last = pe.matmul(ps[:, h, 0:T], ones, squares_r[:, h, :], start=True, stop=True)
                last.then_inc(gn_var.sem, 1)
                prompt_probs(0)
                value_units(1, 6, 7)
                prompt_out(0)
                value_units(1, 7, 8)
                prompt_probs(1)
                values_transposed(1)
                prompt_out(1)

                for i in range(DP):
                    bank = 4 * (1 - i % 2)
                    pe.wait_ge(proj_read.sem, proj_read.after(layer, i - 1))
                    if i == 0:
                        pe.wait_ge(pp_biased.sem, pp_biased.after(layer, 2))
                    pe.wait_ge(or_lo_done.sem, or_lo_done.after(layer, 1))
                    slab(0, PROJ + 2 * i, bank, or_hi, or_lo, 0, 4)
                    pe.wait_ge(oa_lo_done.sem, oa_lo_done.after(layer, 1))
                    slab(0, PROJ + 2 * i + 1, bank + 2, oa_hi, oa_lo, 0, 4)
                for i in range(DP):
                    if i < 2:
                        pe.wait_ge(proj_read.sem, proj_read.after(layer, DP - 1))
                    else:
                        pe.wait_ge(x_done.sem, x_done.after(layer, DP + i - 1))
                    if i == 0:
                        slab_by_chunks(WO, 4, mg_hi, mg_lo, mg_done, 0)
                    else:
                        slab(0, WO + i, 4 + 2 * (i % 2), mg_hi, mg_lo, 0, KC)
                ffn(1, 2, UP2, DOWN2)

            pe.wait_ge(x_done.sem, x_done.after(DEPTH, 0))
            for t in range(3):
                rows = P if t < 2 else TS
                for c in range(KC):
                    last = pe.transpose(ps[0:rows, 2 * t + c // 4, (c % 4) * P:(c % 4 + 1) * P], xT[:, c, t * P:t * P + rows], ident)
            last.then_inc(last_tr.sem, 1)

        @block.vector
        def _(dve):
            dve.sem_inc(slab_used.sem, 4)
            dve.sem_inc(up_read.sem, 2)
            dve.sem_inc(kv_used.sem, 4)
            dve.sem_inc(kt_act.sem, 1)
            dve.sem_inc(kt_dve.sem, 1)
            dve.sem_inc(sc_done.sem, 2)
            dve.sem_inc(sc_read.sem, 2)
            dve.sem_inc(proj_read.sem, 2)
            dve.memset(q_blocks[:, :, :, :], 0.0).then_inc(zeroed.sem, 1)
            dve.memset(small[:, :, :], 0.0).then_inc(zeroed.sem, 1)
            dve.wait_ge(zeroed.sem, 2)
            for i in range(DP):
                dve.wait_ge(first_tr.sem, i + 1)
                last = dve.tensor_copy(xT[:, 2 * i:2 * i + 2, :], ps[:, 2 * i:2 * i + 2, 0:T])
                if i == 0:
                    last.then_inc(first_read.sem, 1)
                elif i == DP - 1:
                    last.then_inc(first_read.sem, 1)
            dve.wait_ge(first_read.sem, 2)
            dve.memset(ps[:, 6:8, 0:T], 0.0).then_inc(first_read.sem, 1)
            dve.wait_ge(first_read.sem, 3)
            dve.sem_inc(x_done.sem, DP - 1)
            dve.wait_ge(first_tr.sem, DP + 1)
            dve.tensor_copy(gains[:, :], ps[:, 0, 0:DEPTH * GL]).then_inc(gains_done.sem, 1)
            dve.wait_ge(gains_done.sem, 1)

            with dve.Fori(0, DEPTH) as layer:
                links = [0]

                def link(ins):
                    links[0] += 1
                    ins.then_inc(dve_link.sem, 1)
                    dve.wait_ge(dve_link.sem, dve_link.after(layer, links[0]))

                def lo(q, k, chunks=KC):
                    dve.wait_ge(hi_done.sem, hi_done.after(layer, k + 1) + q * 4)
                    at, n = slot(k)[0], chunks * CW
                    dve.tensor_tensor(w_lo[:, at, 0:n], raw[:, at, 0:n], w_hi[:, k % 2, 0:n].bitcast(F32), ALU.subtract)\
                       .then_inc(split_done.sem, 1)

                def lo_slab(n, chunks=KC):
                    lo(0, n, chunks)

                def x_add(i, slab_n, bank, factor, last_of=None):
                    dve.wait_ge(slab_used.sem, slab_used.after(layer, slab_n + 1 if last_of is None else 0))
                    dve.scalar_tensor_tensor(xT[:, 2 * i:2 * i + 2, :], ps[:, bank:bank + 2, 0:T], factor,
                                             xT[:, 2 * i:2 * i + 2, :], ALU.mult, ALU.add).then_inc(x_done.sem, 1)

                def rms(r, i, g0):
                    dve.wait_ge(h_hi_done.sem, h_hi_done.after(layer, 4 * r + i + 1))
                    for c in (2 * i, 2 * i + 1):
                        last = dve.scalar_tensor_tensor(h_lo[:, c, :], xT[:, c, :], gain[:, g0 + c:g0 + c + 1],
                                                        h_hi[:, c, :].bitcast(F32), ALU.mult, ALU.subtract)
                    last.then_inc(h_done.sem, 1)

                def rms_add(r, i):
                    if i:
                        dve.wait_ge(rms_sq.sem, rms_sq.after(layer, 4 * r + i + 1))
                        last = dve.tensor_tensor(squares[:, 0:2, :], squares[:, 0:2, :], squares[:, 2 * i:2 * i + 2, :], ALU.add)
                        if i < DP - 1:
                            link(last)
                        else:
                            last.then_inc(rms_acc.sem, 1)

                rstd2 = rstd[:, :].unsqueeze(1).to_broadcast([P, 2, T])

                def up_gated(f, i, slabs, buf):
                    dve.wait_ge(rms_rstd.sem, rms_rstd.after(layer, 2 * f + 1))
                    dve.wait_ge(slab_used.sem, slab_used.after(layer, slabs + 1) + i * 2)
                    dve.tensor_tensor(silu[:, buf], ps[:, 4 * buf:4 * buf + 2, 0:T], rstd2, ALU.mult).then_inc(up_gate.sem, 1)

                def up_linear(f, i, slabs, buf):
                    dve.wait_ge(slab_used.sem, slab_used.after(layer, slabs + 2) + i * 2)
                    dve.tensor_tensor(hid_f[:, buf], ps[:, 4 * buf + 2:4 * buf + 4, 0:T], rstd2, ALU.mult).then_inc(up_read.sem, 1)

                def up_product(f, i, buf):
                    dve.wait_ge(silu_done.sem, silu_done.after(layer, f * UP_PAIRS + 1) + i)
                    dve.wait_ge(up_read.sem, up_read.after(layer, f * UP_PAIRS + 1) + i)
                    dve.tensor_tensor(hid_f[:, buf], silu[:, buf], hid_f[:, buf], ALU.mult).then_inc(up_prod.sem, 1)
                    dve.wait_ge(hid_hi_done.sem, hid_hi_done.after(layer, f * UP_PAIRS + 1) + i)
                    at = ds(i * 2, 2)
                    dve.tensor_tensor(hid_lo[:, at, :], hid_f[:, buf], hid_hi[:, at, :].bitcast(F32), ALU.subtract).then_inc(hid_done.sem, 1)

                def ffn(f, r, first_up, first_down, rms_next):
                    lo_slab(first_up + 2)
                    up_gated(f, 0, first_up, 0)
                    with dve.Fori(0, UP_PAIRS // 2) as t:
                        for b in range(2):
                            i = t * 2 + b
                            up_linear(f, i, first_up, b)
                            lo(t, first_up + 2 * b + 3)
                            up_product(f, i, b)
                            up_gated(f, i + 1, first_up, 1 - b)
                            lo(t, first_up + 2 * b + 4)
                    up_linear(f, UP_PAIRS - 1, first_up, 0)
                    lo_slab(first_down + 1, 7)
                    up_product(f, UP_PAIRS - 1, 0)
                    lo_slab(first_down + 2, 7)
                    for i in range(1, DP):
                        lo_slab(first_down + 3 * i, 8)
                        lo_slab(first_down + 3 * i + 1, 7)
                        x_add(i - 1, first_down + 3 * i - 1, 4 + 2 * ((i - 1) % 2), 0.5)
                        if rms_next:
                            rms_next(i - 1)
                            rms_add(r + 1, i - 1)
                        lo_slab(first_down + 3 * i + 2, 7)
                    if rms_next:
                        lo_slab(first_down + 3 * DP)
                    if rms_next:
                        x_add(DP - 1, first_down + 3 * DP - 1, 4 + 2 * ((DP - 1) % 2), 0.5)
                        rms_next(DP - 1)
                        lo_slab(first_down + 3 * DP + 1)
                        rms_add(r + 1, DP - 1)

                for row, n in G_PARTS:
                    last = dve.tensor_copy(gain[:, row:row + n], gains[:, ds(layer * n + DEPTH * row, n)])
                last.then_inc(gain_done.sem, 1)
                lo_slab(UP1)
                dve.wait_ge(gain_done.sem, layer + 1)
                for i in range(DP - 1):
                    rms(0, i, G_FFN1)
                    rms_add(0, i)
                x_add(DP - 1, 0, 6, 0.5, layer)
                rms(0, DP - 1, G_FFN1)
                lo_slab(UP1 + 1)
                rms_add(0, DP - 1)
                ffn(0, 0, UP1, DOWN1, lambda i: rms(1, i, G_MIX))

                def z_copy(m, place, slot):
                    dve.wait_ge(slab_used.sem, slab_used.after(layer, ZIN + 1) + m)
                    dve.tensor_tensor(z[:, ds(place, 2), :], ps[:, 2 * slot:2 * slot + 2, 0:T], rstd2, ALU.mult).then_inc(z_done.sem, 1)

                def qk_norm(n, g):
                    dve.wait_ge(qk_rstd.sem, qk_rstd.after(layer, n + 1))
                    dve.scalar_tensor_tensor(z[:, 4 * n:4 * n + 4, :], z[:, 4 * n:4 * n + 4, :], gain[:, g:g + 1], qk_squares[:, 4 * n:4 * n + 4, :],
                                             ALU.mult, ALU.mult).then_inc(qk_done.sem, 1)

                dve.wait_ge(consts_loaded.sem, 16)
                lo_slab(ZIN + 2)
                dve.wait_ge(rms_rstd.sem, rms_rstd.after(layer, 2))
                z_copy(0, z_place(0), 0)
                z_copy(1, z_place(1), 1)
                lo_slab(ZIN + 3)
                z_copy(2, z_place(2), 0)
                lo_slab(ZIN + 4)
                qk_norm(0, G_Q)
                dve.wait_ge(qk_done.sem, qk_done.after(layer, 1))
                for c in range(4):
                    for half in range(2):
                        rows, col = slice(64 * half, 64 * half + 64), 8 * c + 4 * half
                        last = dve.tensor_copy(q_blocks[rows, :, c, col:col + 4],
                                               z[rows, ZQ + c, SEQ:T].rearrange("p (b q) -> p b q", b=8))
                last.then_inc(q_blocks_done.sem, 1)
                z_copy(3, z_place(3), 1)

                page_sum = small[:, :, 24:32]

                def unit_step(g, t, b, s):
                    i = t * 2 + b

                    def k_transposed(half):
                        dve.wait_ge(kv_used.sem, kv_used.after(layer, 16 * g + 2 * s + half + 1) + i * 4)
                        dve.tensor_copy(kT[:, s, 2 * half + 1, :], ps[:, 5, :]).then_inc(kt_dve.sem, 1)

                    dve.wait_ge(sc_done.sem, sc_done.after(layer, 8 * g + s - 1) + i * 2)
                    k_transposed(0)
                    lo(t, ZIN + 5 + 8 * g + 2 * b + s)
                    k_transposed(1)
                    m = i * 2 + (4 + 8 * g + s)
                    z_copy(m, z_place(m) if g else m * 2, s)
                    dve.wait_ge(sc_done.sem, sc_done.after(layer, 8 * g + s + 1) + i * 2)
                    at = C_AT["pageb"][0]
                    dve.scalar_tensor_tensor(S[:, g, ds(i * 256 + s * P, P)], ps[:, 6 + s, 0:P], const[:, ds(i * 2 + (at + s), 1)],
                                             cst("pastb"), ALU.add, ALU.add)
                    dve.tensor_reduce(page_sum[:, g, ds(i * 2 + s, 1)], ps[:, 6 + s, 0:P], AX, ALU.add).then_inc(sc_read.sem, 1)

                with dve.Fori(0, N_PAGES // 4) as t:
                    for n in range(4):
                        unit_step(0, t, n // 2, n % 2)

                qk_norm(1, G_K)
                dve.wait_ge(tr_done.sem, tr_done.after(layer, 3))
                kdecay = cst("kdecay").rearrange("p (t h) -> p t h", t=3)
                for t in range(3):
                    rows = P if t < 2 else TS
                    last = dve.tensor_tensor(kd_tok[0:rows, t, :].rearrange("p (h d) -> p h d", h=H_R),
                                             ps[0:rows, t, :].rearrange("p (h d) -> p h d", h=H_R),
                                             kdecay[0:rows, t, :].unsqueeze(2).to_broadcast([rows, H_R, D_R]), ALU.mult)
                last.then_inc(tok_dve.sem, 1)
                dve.wait_ge(new_scores.sem, new_scores.after(layer, 1))
                dve.tensor_tensor(S[:, :, PAST:PAST + TS], ps[:, 7, 0:2 * TS].rearrange("p (g t) -> p g t", g=2),
                                  cst("newb").rearrange("p (g t) -> p g t", g=2), ALU.add).then_inc(new_read.sem, 1)

                for n in range(6):
                    unit_step(1, n // 4, n // 2 % 2, n % 2)

                def sample_bias(g):
                    dve.wait_ge(new_read.sem, new_read.after(layer, 1))
                    dve.wait_ge(sc_read.sem, sc_read.after(layer, 8 * (g + 1)))
                    sg = small[:, g]
                    gate4, least, score, drop, bmax = sg[:, 32:36], sg[:, 36:37], sg[:, 40:44], sg[:, 48:53], sg[:, 56:61]
                    link(dve.tensor_reduce(gate4, page_sum[:, g, :].rearrange("p (b n) -> p b n", n=2), AX, ALU.add))
                    link(dve.tensor_reduce(least, gate4, AX, ALU.min))
                    link(dve.scalar_tensor_tensor(score, gate4, least, cst("rank"), ALU.is_equal, ALU.mult))
                    link(dve.tensor_reduce(sg[:, 37:38], score, AX, ALU.max))
                    dve.tensor_scalar(drop[:, 0:4], score, sg[:, 37:38], NEG, ALU.is_equal, ALU.mult)
                    dve.tensor_reduce(bmax[:, 0:4], S[:, g, 0:PAST].rearrange("p (b n) -> p b n", b=4), AX, ALU.max)
                    link(dve.tensor_reduce(bmax[:, 4:5], S[:, g, PAST:PAST + TS], AX, ALU.max))
                    link(dve.tensor_tensor(bmax[:, 0:4], bmax[:, 0:4], drop[:, 0:4], ALU.add))
                    link(dve.tensor_reduce(sg[:, 38:39], bmax, AX, ALU.max))
                    link(dve.tensor_scalar(sg[:, 39:40], sg[:, 38:39], -SCALE_A, None, ALU.mult))
                    dve.tensor_scalar(sg[:, 8:13], drop, sg[:, 39:40], None, ALU.add).then_inc(sm_bias.sem, 1)

                def sample_norm(g):
                    sg = small[:, g]
                    dve.wait_ge(sm_exp.sem, sm_exp.after(layer, g + 1))
                    link(dve.tensor_reduce(sg[:, 22:23], sg[:, 16:21], AX, ALU.add))
                    link(dve.reciprocal(sg[:, 23:24], sg[:, 22:23]))
                    dve.tensor_scalar(S[:, g, :], S[:, g, :], sg[:, 23:24], None, ALU.mult).then_inc(sm_norm.sem, 1)

                def sample_transposed(g):
                    dve.wait_ge(sm_tr.sem, sm_tr.after(layer, g + 1))
                    dve.tensor_copy(probT_new[:, g, :], ps[0:TS, 6, 0:P]).then_inc(sm_tr_dve.sem, 1)

                sample_bias(0)
                unit_step(1, 1, 1, 0)
                sample_norm(0)
                unit_step(1, 1, 1, 1)
                sample_transposed(0)
                sample_bias(1)
                lo_slab(ZIN + GR1 + 1)
                z_copy(GR1, z_place(GR1), 0)
                sample_norm(1)
                lo_slab(PROJ, 4)
                z_copy(GR1 + 1, z_place(GR1 + 1), 1)
                sample_transposed(1)

                def ret_operands(h):
                    dve.wait_ge(inner_done.sem, inner_done.after(layer, h + 1))
                    if h > 1:
                        dve.wait_ge(ret_o.sem, ret_o.after(layer, h - 1))
                    inn, inn_s = inner[h % 2], inner_s[h % 2]
                    decay = cst("decay", h * SEQ, (h + 1) * SEQ)
                    dve.tensor_tensor(inn[:, 0:SEQ], ps[:, 0, 0:SEQ], decay, ALU.mult)
                    dve.tensor_tensor(inn[:, SEQ:384], ps[:, 0, SEQ:384], decay[:, 0:P], ALU.mult)
                    dve.tensor_tensor(inn_s, ps[0:TS, 0, 384:384 + TS], cst("sdecay", h * TS, (h + 1) * TS)[0:TS, :], ALU.mult)
                    dve.tensor_tensor(q_dec[h % 2], z[:, ZQR + h, SEQ:T], cst("qdecay", h * TS, (h + 1) * TS), ALU.mult).then_inc(ret_in.sem, 1)

                def ret_mask(h):
                    if h:
                        dve.wait_ge(ret_out.sem, ret_out.after(layer, h))
                    dve.tensor_tensor(v_masked, vr_tok[0:TS, 2:3, h * D_R:(h + 1) * D_R].to_broadcast([TS, DEC_BATCH, D_R]),
                                      cst("batch")[0:TS, :].unsqueeze(2).to_broadcast([TS, DEC_BATCH, D_R]), ALU.mult).then_inc(ret_masked.sem, 1)

                def ret_state(h):
                    dve.wait_ge(ret_out.sem, ret_out.after(layer, h + 1))
                    st = state[:, h % 2].rearrange("p b e -> p (b e)").rearrange("p (n m) -> p n m", n=2)
                    dve.scalar_tensor_tensor(st, st, math.exp(log_decay(h) * DEC_SEQ), ps[:, 3:5, :], ALU.mult, ALU.add)\
                       .then_inc(ret_dve.sem, 1)

                def values_out(g):
                    dve.wait_ge(kv_used.sem, kv_used.after(layer, 48 + 16 * g))
                    if g:
                        dve.wait_ge(ret_out.sem, ret_out.after(layer, H_R))
                    else:
                        dve.wait_ge(z_done.sem, z_done.after(layer, Z_SLABS))
                    dve.tensor_copy(o_sample[g], ps[:, 7, :]).then_inc(pv_evac.sem, 1)

                ret_operands(0)
                ret_mask(0)
                lo_slab(PROJ + 1, 4)
                for h in range(1, H_R):
                    ret_operands(h)
                    if h == 2:
                        values_out(0)
                    ret_state(h - 1)
                    ret_mask(h)
                ret_state(H_R - 1)

                def prompt_bias(hb):
                    dve.wait_ge(pp_scores.sem, pp_scores.after(layer, hb + 1))
                    m = mx[:, 8 * hb:8 * hb + 8]
                    for i in range(4):
                        s8 = 8.0 * slope(4 * hb + i)
                        near, far = ps[:, 6, i * P:(i + 1) * P], ps[:, 4 + i % 2, i // 2 * SEQ:(i // 2 + 1) * SEQ]
                        dve.scalar_tensor_tensor(prob_p[hb][:, i, 0:P], cst("causal", 0, P), s8, near, ALU.mult, ALU.add)
                        last = dve.scalar_tensor_tensor(prob_p[hb][:, i, P:384], cst("causal", P), s8, far, ALU.mult, ALU.add)
                    last.then_inc(pp_biased.sem, 1)
                    dve.wait_ge(pp_biased.sem, pp_biased.after(layer, hb + 1))
                    dve.tensor_reduce(m[:, 0:4], prob_p[hb][:, :, 0:P], AX, ALU.max)
                    link(dve.tensor_reduce(m[:, 4:8], prob_p[hb][:, :, P:384], AX, ALU.max))
                    dve.tensor_scalar(m, m, -SCALE_A, None, ALU.mult).then_inc(pp_max.sem, 1)

                def prompt_norm(hb):
                    dve.wait_ge(pp_exp.sem, pp_exp.after(layer, hb + 1))
                    m = mx[:, 8 * hb:8 * hb + 8]
                    link(dve.reciprocal(m, small[:, hb, 0:8]))
                    dve.tensor_tensor(prob_p[hb][:, :, 0:P], prob_p[hb][:, :, 0:P], m[:, 0:4].unsqueeze(2).to_broadcast([P, 4, P]), ALU.mult)
                    dve.tensor_tensor(prob_p[hb][:, :, P:384], prob_p[hb][:, :, P:384], m[:, 4:8].unsqueeze(2).to_broadcast([P, 4, 2 * P]), ALU.mult)\
                       .then_inc(pp_norm.sem, 1)

                def prompt_transposed(hb):
                    dve.wait_ge(pp_tr.sem, pp_tr.after(layer, hb + 1))
                    if hb:
                        dve.wait_ge(pp_out.sem, pp_out.after(layer, hb))
                    dve.tensor_copy(probT_p[:, :, :].rearrange("p h k -> p (h k)")[:, 512:1536].rearrange("p (a n) -> p a n", a=2),
                                    ps[:, 1:3, :]).then_inc(pp_tr_dve.sem, 1)

                prompt_bias(0)
                dve.wait_ge(gn_mean.sem, gn_mean.after(layer, 1))
                dve.scalar_tensor_tensor(orT, ps[:, 0:4, 0:T], -1.0 / D_R, orT, ALU.mult, ALU.add).then_inc(gn_cen.sem, 1)
                prompt_norm(0)
                dve.wait_ge(pv_tr.sem, pv_tr.after(layer, 1))
                prompt_bias(1)
                prompt_transposed(0)
                dve.wait_ge(gn_cen.sem, gn_cen.after(layer, 1))
                dve.wait_ge(gn_rstd.sem, gn_rstd.after(layer, 1))
                link(dve.tensor_tensor(orT, orT, squares_r, ALU.mult))
                prompt_norm(1)
                values_out(1)
                for h in range(H_R):
                    last = dve.tensor_scalar(orT[:, h, :], orT[:, h, :], gain[:, G_GN + h:G_GN + h + 1], gain[:, G_GB + h:G_GB + h + 1],
                                             ALU.mult, ALU.add)
                prompt_transposed(1)
                link(last)
                dve.wait_ge(gr_silu.sem, gr_silu.after(layer, 1))
                dve.tensor_tensor(orT, orT, z[:, ZGR:ZGR + 4, :], ALU.mult).then_inc(or_done.sem, 1)
                dve.wait_ge(or_hi_done.sem, or_hi_done.after(layer, 1))
                dve.wait_ge(or_done.sem, or_done.after(layer, 1))
                dve.tensor_tensor(or_lo[:, :, :], orT, or_hi[:, :, :].bitcast(F32), ALU.subtract).then_inc(or_lo_done.sem, 1)
                dve.wait_ge(oa_hi_done.sem, oa_hi_done.after(layer, 1))
                dve.tensor_tensor(oa_lo[:, :, :], oT, oa_hi[:, :, :].bitcast(F32), ALU.subtract).then_inc(oa_lo_done.sem, 1)

                def merge(i):
                    bank = 4 * (1 - i % 2)
                    dve.wait_ge(slab_used.sem, slab_used.after(layer, PROJ + 2 * i + 2))
                    dve.wait_ge(gates_done.sem, gates_done.after(layer, 2))
                    if i > 1:
                        dve.wait_ge(mg_done.sem, mg_done.after(layer, i - 1))
                    r = z_place(Z_SLABS - DP + i)
                    dve.tensor_tensor(silu[:, i % 2], z[:, r:r + 2, :], ps[:, bank:bank + 2, 0:T], ALU.mult)
                    a = ZGA + 2 * i
                    dve.tensor_tensor(hid_f[:, i % 2], z[:, a:a + 2, :], ps[:, bank + 2:bank + 4, 0:T], ALU.mult).then_inc(proj_read.sem, 1)

                def merge_sum(i):
                    dve.wait_ge(proj_read.sem, proj_read.after(layer, i + 1))
                    dve.tensor_tensor(hid_f[:, i % 2], hid_f[:, i % 2], silu[:, i % 2], ALU.add).then_inc(merged.sem, 1)

                def merge_lo(i):
                    dve.wait_ge(mg_hi_done.sem, mg_hi_done.after(layer, i + 1))
                    dve.tensor_tensor(mg_lo[:, 2 * i:2 * i + 2, :], hid_f[:, i % 2], mg_hi[:, 2 * i:2 * i + 2, :].bitcast(F32), ALU.subtract)\
                       .then_inc(mg_done.sem, 1)

                for i in range(1, DP):
                    lo_slab(PROJ + 2 * i, 4)
                    merge(i - 1)
                    lo_slab(PROJ + 2 * i + 1, 4)
                    merge_sum(i - 1)
                    if i > 1:
                        merge_lo(i - 2)
                lo_slab(WO)
                merge_lo(DP - 2)
                merge(DP - 1)
                merge_sum(DP - 1)
                merge_lo(DP - 1)
                lo_slab(WO + 1)
                lo_slab(WO + 2)
                x_add(0, WO, 4, 1.0)
                rms(2, 0, G_FFN2)
                rms_add(2, 0)
                lo_slab(WO + 3)
                x_add(1, WO + 1, 6, 1.0)
                rms(2, 1, G_FFN2)
                rms_add(2, 1)
                x_add(2, WO + 2, 4, 1.0)
                lo_slab(UP2)
                rms(2, 2, G_FFN2)
                rms_add(2, 2)
                x_add(3, WO + 3, 6, 1.0)
                rms(2, 3, G_FFN2)
                lo_slab(UP2 + 1)
                rms_add(2, 3)
                ffn(1, 2, UP2, DOWN2, None)
                assert links[0] == LINKS, links

            dve.wait_ge(slab_used.sem, slab_used.after(DEPTH, 0))
            dve.scalar_tensor_tensor(xT[:, KC - 2:KC, :], ps[:, 6:8, 0:T], 0.5, xT[:, KC - 2:KC, :], ALU.mult, ALU.add).then_inc(x_done.sem, 1)
            dve.wait_ge(last_tr.sem, 1)
            for t in range(3):
                rows = P if t < 2 else TS
                dve.tensor_copy(stage[0:rows, t, 512:1024], ps[0:rows, 2 * t + 1, :]).then_inc(last_dve.sem, 1)


_INS = ["x_prompt", "x_sample", "cache_k", "cache_v", "state_ret", "page_table", "g_ffn1", "w1_ffn1", "w3_ffn1", "w2_ffn1",
        "g_mix", "w_in", "g_q", "g_k", "gn_gain", "gn_bias", "w_pa", "w_pr", "w_o", "g_ffn2", "w1_ffn2", "w3_ffn2", "w2_ffn2"]
_OUTS = [(1, SEQ, D_MODEL), (DEC_BATCH, DEC_SEQ, D_MODEL), (DEPTH, 1, SEQ, H_A, D_A), (DEPTH, 1, SEQ, H_A, D_A),
         (DEPTH, 1, H_R, D_R, D_R), (DEPTH, DEC_BATCH, DEC_SEQ, H_A, D_A), (DEPTH, DEC_BATCH, DEC_SEQ, H_A, D_A),
         (DEPTH, DEC_BATCH, H_R, D_R, D_R)]


def kernel(**inputs):
    import concourse.bacc as bacc
    from concourse.bass_utils import run_bass_kernel_spmd

    nc = bacc.Bacc("TRN2", target_bir_lowering=False, num_devices=1)
    arrays = {f"in_{n}": np.ascontiguousarray(inputs[n]) for n in _INS}
    arrays["consts"] = constants()
    args = [nc.dram_tensor(n, a.shape, mybir.dt.from_np(a.dtype), kind="ExternalInput").ap() for n, a in arrays.items()]
    outs = [nc.dram_tensor(f"out_{i}", s, F32, kind="ExternalOutput").ap() for i, s in enumerate(_OUTS)]
    trunk(nc, *args, *outs)
    r = run_bass_kernel_spmd(nc, [arrays], core_ids=[0])
    return tuple(r.results[0][f"out_{i}"] for i in range(len(_OUTS)))
```
